# Optimizing a Trainium2 kernel written in Bass

```python
import jax, jax.numpy as jnp
from jax import lax
import numpy as np

D_MODEL = 1024
BATCH = 1
SEQ = 1024
DEPTH = 2

D_MIX = D_MODEL
GLA_HEADS = 4
GLA_WIDTH = D_MIX // 2
GLA_DV = GLA_WIDTH // GLA_HEADS
GLA_DK = GLA_DV // 2
GLA_LOWRANK = 16
GLA_TAU = 16.0
GLA_CHUNK = 64
DIL_HEADS = 4
DIL_WIDTH = D_MIX - GLA_WIDTH
DIL_HD = DIL_WIDTH // DIL_HEADS
DIL_PATTERNS = ((128, 1), (512, 4), (2048, 16))
ROPE_THETA = 10000.0
EPS = 1e-6
IN_SIZES = (GLA_HEADS * GLA_DK, GLA_HEADS * GLA_DK, GLA_WIDTH, GLA_WIDTH, GLA_LOWRANK,
            DIL_WIDTH, DIL_WIDTH, DIL_WIDTH, DIL_WIDTH)
IN_COLS = sum(IN_SIZES)

kernel_name = "hybrid_gla_dilated_parallel_heads"

def rmsnorm(x, g):
    x32 = x.astype(jnp.float32)
    r = x32 * lax.rsqrt(jnp.mean(x32 * x32, axis=-1, keepdims=True) + EPS)
    return (r * g.astype(jnp.float32)).astype(x.dtype)

def head_rmsnorm(o, g):
    r = o * lax.rsqrt(jnp.mean(o * o, axis=-1, keepdims=True) + EPS)
    B, S, H, dh = o.shape
    return r.reshape(B, S, H * dh) * g.astype(jnp.float32)

def rope(x):
    S, hd = x.shape[1], x.shape[3]
    inv_freq = ROPE_THETA ** (-jnp.arange(0, hd, 2, dtype=jnp.float32) / hd)
    ang = jnp.arange(S, dtype=jnp.float32)[:, None] * inv_freq[None, :]
    cos = jnp.cos(ang)[None, :, None, :]
    sin = jnp.sin(ang)[None, :, None, :]
    x32 = x.astype(jnp.float32)
    x1, x2 = x32[..., : hd // 2], x32[..., hd // 2:]
    return jnp.concatenate([x1 * cos - x2 * sin, x2 * cos + x1 * sin], axis=-1)

def gla_mixer(q, k, v, lr, w_gate_up, b_gate_up):
    B, S, H, DK = q.shape
    DV = v.shape[-1]
    C = GLA_CHUNK
    n = S // C
    z = jnp.einsum('bsr,rk->bsk', lr.astype(jnp.float32), w_gate_up.astype(jnp.float32)) + b_gate_up.astype(jnp.float32)
    log_a = jax.nn.log_sigmoid(z).reshape(B, S, H, DK) / GLA_TAU

    def chunks(t):
        return t.astype(jnp.float32).reshape(B, n, C, H, t.shape[-1]).transpose(0, 3, 1, 2, 4)

    qc, kc, vc, la = chunks(q), chunks(k), chunks(v), chunks(log_a)
    b = jnp.cumsum(la, axis=3)
    q_e = qc * jnp.exp(b)
    k_e = kc * jnp.exp(-b)
    causal = jnp.tril(jnp.ones((C, C), dtype=bool))
    A = jnp.where(causal, jnp.einsum('bhnik,bhnjk->bhnij', q_e, k_e), 0.0)
    o_intra = jnp.einsum('bhnij,bhnjv->bhniv', A, vc)
    b_last = b[:, :, :, -1, :]
    k_end = kc * jnp.exp(b_last[:, :, :, None, :] - b)
    chunk_state = jnp.einsum('bhnjk,bhnjv->bhnkv', k_end, vc)
    decay = jnp.exp(b_last)

    def step(state, inp):
        dec, cs = inp
        return dec[..., None] * state + cs, state

    init = jnp.zeros((B, H, DK, DV), jnp.float32)
    _, before = lax.scan(step, init, (jnp.moveaxis(decay, 2, 0), jnp.moveaxis(chunk_state, 2, 0)))
    before = jnp.moveaxis(before, 0, 2)
    o = o_intra + jnp.einsum('bhnik,bhnkv->bhniv', q_e, before)
    return o.transpose(0, 2, 3, 1, 4).reshape(B, S, H, DV)

def dilated_pattern(q, k, v, window, dilation):
    B, S, H, hd = q.shape
    lb = window // dilation
    span = lb * dilation
    s_pad = -(-S // span) * span
    pad = s_pad - S
    L = s_pad // dilation
    nb = L // lb

    def to_blocks(t):
        t = jnp.pad(t, ((0, 0), (0, pad), (0, 0), (0, 0)))
        t = t.reshape(B, L, dilation, H, hd).transpose(0, 3, 2, 1, 4)
        return t.reshape(B, H, dilation, nb, lb, hd)

    def with_prev(t):
        prev = jnp.concatenate([jnp.zeros_like(t[:, :, :, :1]), t[:, :, :, :-1]], axis=3)
        return jnp.concatenate([prev, t], axis=4)

    qb = to_blocks(q)
    kk = with_prev(to_blocks(k))
    vv = with_prev(to_blocks(v))
    s = jnp.einsum('bhrnqd,bhrnkd->bhrnqk', qb, kk) * (hd ** -0.5)
    qi = jnp.arange(lb)[:, None]
    ki = jnp.arange(2 * lb)[None, :]
    dist = qi + lb - ki
    blk = jnp.arange(nb)[:, None, None]
    valid = (dist >= 0) & (dist <= lb) & ((blk > 0) | (ki >= lb)[None])
    s = jnp.where(valid, s, -jnp.inf)
    m = jnp.max(s, axis=-1, keepdims=True)
    p = jnp.exp(s - m)
    den = jnp.sum(p, axis=-1)
    o = jnp.einsum('bhrnqk,bhrnkd->bhrnqd', p, vv) / den[..., None]
    lse = m[..., 0] + jnp.log(den)
    o = o.reshape(B, H, dilation, L, hd).transpose(0, 3, 2, 1, 4).reshape(B, s_pad, H, hd)[:, :S]
    lse = lse.reshape(B, H, dilation, L).transpose(0, 3, 2, 1).reshape(B, s_pad, H)[:, :S]
    return o, lse

def dilated_mixer(q, k, v):
    v = v.astype(jnp.float32)
    outs, lses = [], []
    for window, dilation in DIL_PATTERNS:
        o, lse = dilated_pattern(q, k, v, window, dilation)
        outs.append(o)
        lses.append(lse)
    w = jax.nn.softmax(jnp.stack(lses, axis=0), axis=0)
    return jnp.sum(w[..., None] * jnp.stack(outs, axis=0), axis=0)

def hybrid_layer(x, c, w_ada, b_ada, g_pre, w_in, w_gate_up, b_gate_up, g_gla, g_dil, w_out, g_post):
    B, S, D = x.shape
    mod = jnp.einsum('bd,de->be', jax.nn.silu(c), w_ada) + b_ada
    shift, scale, gate = jnp.split(mod, 3, axis=-1)
    h = rmsnorm(x, g_pre) * (1 + scale[:, None, :]) + shift[:, None, :]
    proj = jnp.einsum('bsd,de->bse', h, w_in)
    offs = [int(o) for o in np.cumsum(IN_SIZES)[:-1]]
    q_a, k_a, v_a, z_a, lr, q_b, k_b, v_b, z_b = jnp.split(proj, offs, axis=-1)
    q_a = q_a.reshape(B, S, GLA_HEADS, GLA_DK) * (GLA_DK ** -0.5)
    k_a = k_a.reshape(B, S, GLA_HEADS, GLA_DK)
    v_a = v_a.reshape(B, S, GLA_HEADS, GLA_DV)
    o_a = gla_mixer(q_a, k_a, v_a, lr, w_gate_up, b_gate_up)
    y_a = head_rmsnorm(o_a, g_gla) * jax.nn.silu(z_a.astype(jnp.float32))
    q_b = rope(q_b.reshape(B, S, DIL_HEADS, DIL_HD))
    k_b = rope(k_b.reshape(B, S, DIL_HEADS, DIL_HD))
    v_b = v_b.reshape(B, S, DIL_HEADS, DIL_HD)
    o_b = dilated_mixer(q_b, k_b, v_b)
    y_b = head_rmsnorm(o_b, g_dil) * jax.nn.silu(z_b.astype(jnp.float32))
    y = jnp.concatenate([y_a, y_b], axis=-1).astype(x.dtype)
    y = jnp.einsum('bse,ed->bsd', y, w_out)
    return x + gate[:, None, :] * rmsnorm(y, g_post)

def setup_inputs(seed: int = 0) -> dict:
    key = jax.random.key(seed)
    ks = jax.random.split(key, 14)
    f = jnp.float32
    nrm = lambda k, shape, s: jax.random.normal(k, shape, f) * s
    return {
        "x": nrm(ks[0], (BATCH, SEQ, D_MODEL), 1.0),
        "c": nrm(ks[1], (BATCH, D_MODEL), 1.0),
        "w_ada": nrm(ks[2], (DEPTH, D_MODEL, 3 * D_MODEL), D_MODEL ** -0.5),
        "b_ada": nrm(ks[3], (DEPTH, 3 * D_MODEL), 0.02),
        "g_pre": 1.0 + nrm(ks[4], (DEPTH, D_MODEL), 0.02),
        "w_in": nrm(ks[5], (DEPTH, D_MODEL, IN_COLS), D_MODEL ** -0.5),
        "w_gate_up": nrm(ks[6], (DEPTH, GLA_LOWRANK, GLA_HEADS * GLA_DK), GLA_LOWRANK ** -0.5),
        "b_gate_up": nrm(ks[7], (DEPTH, GLA_HEADS * GLA_DK), 0.1),
        "g_gla": 1.0 + nrm(ks[8], (DEPTH, GLA_WIDTH), 0.02),
        "g_dil": 1.0 + nrm(ks[9], (DEPTH, DIL_WIDTH), 0.02),
        "w_out": nrm(ks[10], (DEPTH, D_MIX, D_MODEL), D_MIX ** -0.5),
        "g_post": 1.0 + nrm(ks[11], (DEPTH, D_MODEL), 0.02),
    }

def reference(x, c, w_ada, b_ada, g_pre, w_in, w_gate_up, b_gate_up, g_gla, g_dil, w_out, g_post):
    for l in range(DEPTH):
        x = hybrid_layer(x, c, w_ada[l], b_ada[l], g_pre[l], w_in[l], w_gate_up[l], b_gate_up[l],
                         g_gla[l], g_dil[l], w_out[l], g_post[l])
    return x


_drawn_inputs = setup_inputs


def setup_inputs(seed=0):
    import zlib

    import numpy as np

    out = dict(_drawn_inputs(seed))
    spreads = {}
    factors = {'g_gla': 4.886, 'g_dil': 5.12, 'g_post': 3.809}
    for name, (base, spread) in spreads.items():
        noise = np.random.default_rng([zlib.crc32(name.encode()), seed]).standard_normal(out[name].shape)
        drawn = base * np.exp(spread * noise) if base else spread * noise
        out[name] = __import__('jax').numpy.asarray(drawn.astype(out[name].dtype))
    for name, factor in factors.items():
        out[name] = (out[name] * factor).astype(out[name].dtype)
    return out
```

```python
import numpy as np
import concourse.bass as bass
from concourse import mybir
from contextlib import ExitStack

P = 128
D = 1024
S = 1024
DEPTH = 2
KT = D // P
NT = S // P
HALF = S // 2
GLA_H, DK, DV, LOWRANK = 4, 64, 128, 16
CHUNK = 64
PAIRS = GLA_H // 2
DIL_H, HD = 4, 128
EPS = 1e-6
SCORE_SCALE = HD ** -0.5
ADA_TILES = 2 * D // P
GATE_TILES = D // P
VT = GLA_H * DV // P
NEG = -1e30

T_TILES = (["lr"] + [f"{n}{j}" for j in range(PAIRS) for n in ("qa", "ka", "za", "zA")]
           + [f"{n}{h}" for h in range(DIL_H) for n in ("qb", "kb", "zb")])
STREAM = (["ada"] * ADA_TILES + ["va"] * VT + T_TILES[:1 + 4 * PAIRS] + ["vb"] * VT
          + T_TILES[1 + 4 * PAIRS:] + ["gate"] * GATE_TILES + ["wo"] * KT)
RING = 4
BY_PE = [k in ("ada", "gate") for k in STREAM]
SPLIT = [n for n, pe in enumerate(BY_PE) if not pe]
VA0, VB0, WO0 = (STREAM.index(k) - sum(BY_PE[:STREAM.index(k)]) for k in ("va", "vb", "wo"))


def split_index(t):
    return VA0 + VT + t if t < 1 + 4 * PAIRS else VB0 + VT + t - (1 + 4 * PAIRS)


def low_on_vector(j):
    return (j < VA0 + VT and (j - VA0) % 2 == 1) or (j >= WO0 and (j - WO0) % 2 == 1)


def low_count(j):
    return sum(low_on_vector(i) == low_on_vector(j) for i in range(j + 1))


def units():
    u = {}
    n = 0
    def add(*key):
        nonlocal n
        u[key] = n
        n += 1
    for t in range(NT):
        add("va", t)
    for k in range(1 + 4 * PAIRS):
        add(k, 0)
        add(k, 1)
    for t in range(NT):
        add("vb", t)
    for k in range(1 + 4 * PAIRS, len(T_TILES)):
        add(k, 0)
        add(k, 1)
    return u


UNIT = units()
N_UNITS = len(UNIT)
UNIT_STEPS = (0, 2, 4, 5, 6, 7)


def hybrid_trunk(nc, x, tiles, vecs, rows, w_gate_up, c_cols, rope_cos, rope_sin, log_count, ident, causal, out):
    f32, f32r, i32 = mybir.dt.float32, mybir.dt.float32r, mybir.dt.int32
    ACT, ALU = mybir.ActivationFunctionType, mybir.AluOpType
    MULT, ADD, SUB, MAX, MIN = ALU.mult, ALU.add, ALU.subtract, ALU.max, ALU.min

    ctx = ExitStack()
    with ctx:
        def sb(name, shape, dt=f32):
            return ctx.enter_context(nc.sbuf_tensor(name, shape, dt))

        KB = 1024
        arena_at = -(-nc.sbuf_base // 32) * 32
        sb("arena", [P, 76 * KB // 4])

        def at(name, kb, shape, dt=f32):
            return nc.alloc_sbuf_tensor_at(name, shape, dt, offset=arena_at + kb * KB)

        act_hi = sb("act_hi", [P, KT, S], f32r)
        act_lo = sb("act_lo", [P, KT, S], f32r)
        yT = sb("yT", [P, GLA_H + DIL_H, S])
        wt_hi = sb("wt_hi", [P, 2, KT, P], f32r)
        wt_lo = sb("wt_lo", [P, 2, KT, P], f32r)
        raw = sb("raw", [P, RING, KT, P])
        idn = sb("idn", [P, P])
        ones = sb("ones", [P, P])
        causal_sb = sb("causal_sb", [P, P], i32)
        vec = sb("vec", [P, 34])
        b_ada_c, g_pre_c, b_gu_c, g_head = vec[:, 0:16], vec[:, 16:24], vec[:, 24:26], vec[:, 26:34]
        small = sb("small", [P, 112])
        c_sb, c_e, silu_c = small[:, 0:8], small[:, 8:16], small[:, 16:24]
        mod, h_scale = small[:, 24:40], small[:, 40:48]
        ss, rstd = small[:, 48:50], small[:, 50:52]
        ss2, rstd2 = small[:, 52:54], small[:, 54:56]
        decay = small[:, 56:72]
        nmax, den, rden = small[:, 72:74], small[:, 74:76], small[:, 76:78]
        lnt, lnt2 = small[:, 78:80], small[:, 80:82]
        h_shift = mod[:, 0:8]
        ss8, ln8, rs8 = small[:, 84:92], small[:, 92:100], small[:, 100:108]


        h_junk = at("h_junk", 60, [P, S])
        h_tmp = at("h_tmp", 64, [P, 4, HALF])
        wv_hi = at("wv_hi", 0, [P, KT, VT * P], f32r)
        wv_lo = at("wv_lo", 16, [P, KT, VT * P], f32r)
        va = at("va", 32, [P, NT, GLA_H * DV])
        cum = at("cum", 48, [P, S])
        q_e = at("q_e", 52, [P, S])
        k_e = at("k_e", 56, [P, S])
        k_dT = at("k_dT", 60, [P, S])
        za_s = at("za_s", 64, [P, 2, S])
        k_end = at("k_end", 72, [P, NT, P])
        w_gu = yT[0:LOWRANK, 4, 0:GLA_H * DK]
        state = yT[:, 4, 256:256 + 6 * DV].rearrange("p (r v) -> p r v", r=6)
        at_sb = yT[:, 5, 0:4 * P].rearrange("p (b e i) -> p b e i", b=2, e=2)
        sq_a = yT[:, 6, :]
        lrT = yT[0:LOWRANK, 7, :]
        cos_t = at("cos_t", 0, [P, S])
        sin_t = at("sin_t", 4, [P, S])
        cnt_t = at("cnt_t", 8, [P, S])
        pT = at("pT", 12, [P, NT, 2 * P])
        sq_b = at("sq_b", 20, [P, S])
        r_tmp = at("r_tmp", 24, [P, 2, HALF])
        zb_0 = at("zb_0", 28, [P, S])
        vb = at("vb", 32, [P, NT, DIL_H * HD])
        qkT = at("qkT", 48, [P, 4, S])
        pr = at("pr", 64, [P, 2, S])
        zb_1 = at("zb_1", 72, [P, S])
        sq_last = at("sq_last", 64, [P, S])
        wo_hi = at("wo_hi", 0, [P, KT, D], f32r)
        wo_lo = at("wo_lo", 32, [P, KT, D], f32r)
        gate_t = at("gate_t", 64, [P, D])
        x_t = at("x_t", 68, [P, 2, D])

        def bank(n, count=1):
            return ps[:, n:n + count, :].rearrange("p b n -> p (b n)") if count > 1 else ps[:, n, :]

        ps = ctx.enter_context(nc.psum_tensor("ps", [P, 8, HALF], f32))

        names = []

        def sem(name):
            names.append(nc.alloc_semaphore(name))
            return names[-1]

        const_in = [sem(f"const_in{i}") for i in range(4)]
        x_in = [sem(f"x_in{t}") for t in range(NT)]
        sq_x, rstd_x, silu_seq = sem("sq_x"), sem("rstd_x"), sem("silu_seq")
        raw_in = [sem(f"raw_in{i}") for i in range(RING)]
        vec_in, gu_in, tab_in, row_in = sem("vec_in"), sem("gu_in"), sem("tab_in"), sem("row_in")
        resid_in = sem("resid_in")
        raw_used = sem("raw_used")
        w_hi, w_lo_pool, w_lo_dve = sem("w_hi"), sem("w_lo_pool"), sem("w_lo_dve")
        mods_ready = sem("mods_ready")
        xnT_done, h_hi, h_full, h_lo_dve, h_lo_pool = (sem(n) for n in (
            "xnT_done", "h_hi", "h_full", "h_lo_dve", "h_lo_pool"))
        unit_done = sem("unit_done")
        unit_free = [sem("unit_free0"), sem("unit_free1")]
        z_exp = sem("z_exp")
        dk_z, dk_abs, dk_soft, dk_cum, dk_rest, dk_exp = (sem(n) for n in (
            "dk_z", "dk_abs", "dk_soft", "dk_cum", "dk_rest", "dk_exp"))
        kd_done, kend_ready, at_done, at_masked, cs_done, state_done, o_done, o_evac = (sem(n) for n in (
            "kd_done", "kend_ready", "at_done", "at_masked", "cs_done", "state_done", "o_done", "o_evac"))
        sq_done, norm_done, ln_done, rs_done, y_done = (sem(n) for n in (
            "sq_done", "norm_done", "ln_done", "rs_done", "y_done"))
        s_done, s_masked, exp_done, p_ready, pt_done, pt_evac, pv_done, pv_evac = (sem(n) for n in (
            "s_done", "s_masked", "exp_done", "p_ready", "pt_done", "pt_evac", "pv_done", "pv_evac"))
        y_hi, y_lo_dve, y_lo_pool = sem("y_hi"), sem("y_lo_dve"), sem("y_lo_pool")
        gate_ready, yp_done, sqy_done, rstd_y, yp_free, x_new, rstd_n, xn_done = (sem(n) for n in (
            "gate_ready", "yp_done", "sqy_done", "rstd_y", "yp_free", "x_new", "rstd_n", "xn_done"))
        x_load = [sem("x_load0"), sem("x_load1")]
        x_store = [sem("x_store0"), sem("x_store1")]
        dve_seq, act_seq, pro_seq = sem("dve_seq"), sem("act_seq"), sem("pro_seq")

        def wait_low(eng, j):
            eng.wait_ge(w_lo_dve if low_on_vector(j) else w_lo_pool, low_count(j))

        def wait_h_low(eng, n):
            eng.wait_ge(h_lo_pool if n % 2 else h_lo_dve, n // 2 + 1)

        def wait_unit_evacuated(eng, u):
            eng.wait_ge(unit_free[u % 2], u // 2 + 1)

        def pt_chunk(h, i, part):
            return 12 * h + (i if i < 4 else 4 + 2 * (i - 4) + part)

        def pt_parts(i):
            return [(0, i + 1)] if i < 4 else [(0, 4), (4, i + 1)]

        def states(j, c):
            return (2 * NT - 1) * j + c

        TU = lambda t, half: UNIT[(t, half)]
        T_LR = 0
        T_A = lambda j, n: 1 + 4 * j + n
        T_B = lambda h, n: 1 + 4 * PAIRS + 3 * h + n
        VB_LAST = UNIT[("vb", NT - 1)]

        with nc.Block() as block:
            @block.sync
            def _(sp):
                sp.dma_start(c_sb, c_cols).then_inc(const_in[0], 16)
                sp.dma_start(idn[:, :], ident).then_inc(const_in[1], 16)
                sp.dma_start(causal_sb[:, :], causal).then_inc(const_in[2], 16)
                for t in range(NT):
                    sp.dma_start(yT[:, t, :], x[0, t * P:(t + 1) * P, :]).then_inc(x_in[t], 16)
                sp.wait_ge(const_in[1], 16)
                sp.wait_ge(const_in[2], 16)

            @block.scalar
            def _(act):
                act.preload_act_table_set("natural_log_exp_and_others")
                act.wait_ge(const_in[0], 16)
                nc.scalar.activation(c_e, c_sb, ACT.Exp, scale=-1.0).then_inc(silu_seq, 1)
                for t in range(NT):
                    act.wait_ge(x_in[t], 16)
                    nc.scalar.activation(h_junk[:, :], yT[:, t, :],
                                         ACT.Square, accum_out=ss8[:, t:t + 1]).then_inc(sq_x, 1)
                    act.wait_ge(sq_x, 2 * t + 1)
                    nc.scalar.activation(ln8[:, t:t + 1], ss8[:, t:t + 1], ACT.Ln, bias=EPS, scale=1.0 / D)\
                        .then_inc(sq_x, 1)
                    act.wait_ge(sq_x, 2 * t + 2)
                    nc.scalar.activation(rs8[:, t:t + 1], ln8[:, t:t + 1], ACT.Exp, scale=-0.5).then_inc(rstd_x, 1)

            @block.vector
            def _(dve):
                nc.vector.memset(ones[:, :], 1.0).then_inc(pro_seq, 1)
                dve.wait_ge(silu_seq, 1)
                nc.vector.tensor_scalar_add(c_e, c_e, 1.0).then_inc(silu_seq, 1)
                dve.wait_ge(silu_seq, 2)
                nc.vector.reciprocal(c_e, c_e).then_inc(silu_seq, 1)
                dve.wait_ge(silu_seq, 3)
                nc.vector.tensor_tensor(silu_c, c_sb, c_e, MULT).then_inc(silu_seq, 1)
                for t in range(NT):
                    dve.wait_ge(rstd_x, t + 1)
                    nc.vector.tensor_scalar(yT[:, t, :], yT[:, t, :], rs8[:, t:t + 1], None, MULT)\
                        .then_inc(pro_seq, 1)

        with nc.Fori(0, DEPTH) as layer:
            with nc.Block() as block:
                @block.sync
                def _(sp):
                    sp.dma_start(vec[:, :], vecs[bass.ds(layer, 1), :, :].rearrange("l p n -> (l p) n"))\
                        .then_inc(vec_in, 16)
                    for n, kind in enumerate(STREAM):
                        if n >= RING:
                            m = n - RING
                            if BY_PE[m]:
                                sp.wait_ge(raw_used, sum(BY_PE[:m + 1]))
                            else:
                                wait_low(sp, m - sum(BY_PE[:m]))
                        sp.dma_start(raw[:, n % RING, :, :],
                                     tiles[bass.ds(layer * len(STREAM) + n, 1), :, :]
                                     .rearrange("o p (k c) -> (o p) k c", k=KT)).then_inc(raw_in[n % RING], 16)
                        if n == STREAM.index("lr") + 4:
                            sp.wait_ge(xnT_done, 2 * KT)
                            sp.dma_start(w_gu, w_gate_up[bass.ds(layer * LOWRANK, LOWRANK), :]).then_inc(gu_in, 16)
                        if n == STREAM.index("vb") + VT + 5:
                            sp.wait_ge(unit_done, VB_LAST + 1)
                            sp.dma_start(cos_t[:, :], rope_cos).then_inc(tab_in, 16)
                            sp.dma_start(sin_t[:, :], rope_sin).then_inc(tab_in, 16)
                            sp.dma_start(cnt_t[:, :], log_count).then_inc(tab_in, 16)
                            with sp.If(layer < 1):
                                sp.dma_start(out, x).then_inc(resid_in, 16)
                                sp.wait_ge(resid_in, 16)
                    sp.wait_ge(pt_done, pt_chunk(DIL_H, 0, 0))
                    sp.dma_start(x_t[:, 0, :], rows[bass.ds(2 * layer, 1), :].broadcast_to([P, D])).then_inc(row_in, 16)
                    sp.wait_ge(y_done, GLA_H + DIL_H)
                    sp.dma_start(gate_t[:, :], rows[bass.ds(2 * layer + 1, 1), :].broadcast_to([P, D])).then_inc(row_in, 16)
                    for t in range(NT + 1):
                        if t < NT:
                            if t == 0:
                                sp.wait_ge(gate_ready, 2)
                            if t >= 2:
                                sp.wait_ge(x_store[t % 2], 16 * (t // 2))
                                sp.wait_ge(xn_done, t - 1)
                            sp.dma_start(x_t[:, t % 2, :], out[0, t * P:(t + 1) * P, :]).then_inc(x_load[t % 2], 16)
                        if t >= 1:
                            sp.wait_ge(x_new, t)
                            sp.dma_start(out[0, (t - 1) * P:t * P, :], x_t[:, (t - 1) % 2, :])\
                                .then_inc(x_store[(t - 1) % 2], 16)
                    for b in range(2):
                        sp.wait_ge(x_store[b], 16 * (NT // 2))

                @block.gpsimd
                def _(pool):
                    def low(j, dst, src_hi):
                        pool.wait_ge(w_hi, j + 1)
                        n = SPLIT[j]
                        nc.gpsimd.tensor_tensor(dst, raw[:, n % RING, :, :], src_hi.bitcast(f32), SUB)\
                            .then_inc(w_lo_pool, 1)

                    def low_h(n):
                        half, k = divmod(n, KT)
                        cols = slice(half * HALF, (half + 1) * HALF)
                        pool.wait_ge(h_full, n + 1)
                        pool.wait_ge(h_hi, n + 1)
                        nc.gpsimd.tensor_tensor(act_lo[:, k, cols], h_tmp[:, n % 4, :],
                                                act_hi[:, k, cols].bitcast(f32), SUB).then_inc(h_lo_pool, 1)

                    def low_t(t):
                        low(split_index(t), wt_lo[:, t % 2], wt_hi[:, t % 2])

                    def low_cols(j, lo, hi, v):
                        low(j, lo[:, :, v * P:(v + 1) * P], hi[:, :, v * P:(v + 1) * P])

                    for n in range(1, KT, 2):
                        low_h(n)
                    for v in range(VT):
                        if not low_on_vector(VA0 + v):
                            low_cols(VA0 + v, wv_lo, wv_hi, v)
                    low_t(0)
                    low_t(1)
                    for n in range(KT + 1, 2 * KT, 2):
                        low_h(n)
                    for t in range(2, T_B(0, 0)):
                        low_t(t)
                    for v in range(VT):
                        low_cols(VB0 + v, wv_lo, wv_hi, v)
                    for t in range(T_B(0, 0), len(T_TILES)):
                        low_t(t)
                    for h in range(0, GLA_H + DIL_H, 2):
                        pool.wait_ge(y_hi, h + 1)
                        nc.gpsimd.tensor_tensor(act_lo[:, h, :], yT[:, h, :], act_hi[:, h, :].bitcast(f32), SUB)\
                            .then_inc(y_lo_pool, 1)
                    for v in range(KT):
                        if not low_on_vector(WO0 + v):
                            low_cols(WO0 + v, wo_lo, wo_hi, v)

                @block.scalar
                def _(act):
                    def high(j, dst):
                        n = SPLIT[j]
                        act.wait_ge(raw_in[n % RING], 16 * (n // RING + 1))
                        nc.scalar.copy(dst, raw[:, n % RING, :, :]).then_inc(w_hi, 1)

                    def high_t(t):
                        if t >= len(T_TILES):
                            return
                        if t >= 2:
                            act.wait_ge(unit_done, TU(t - 2, 1) + 1)
                        high(split_index(t), wt_hi[:, t % 2])

                    def high_h(n):
                        half, k = divmod(n, KT)
                        act.wait_ge(xnT_done, n + 1)
                        nc.scalar.activation(act_hi[:, k, half * HALF:(half + 1) * HALF], bank(2 + n % 6),
                                             ACT.Identity, scale=h_scale[:, k:k + 1], bias=h_shift[:, k:k + 1])\
                            .then_inc(h_hi, 1)

                    def evacuate(u, dst, rows_=P):
                        act.wait_ge(unit_done, u + 1)
                        nc.scalar.copy(dst, bank(u % 2)[0:rows_, :]).then_inc(unit_free[u % 2], 1)

                    def z_unit(head, t, half, dst):
                        if head >= 2:
                            act.wait_ge(y_done, head - 1)
                        act.wait_ge(unit_done, TU(t, half) + 1)
                        nc.scalar.activation(dst[:, half * HALF:(half + 1) * HALF], bank(TU(t, half) % 2), ACT.Exp,
                                             scale=-1.0).then_inc(z_exp, 1)

                    def norm_square(head, buf):
                        if head:
                            act.wait_ge(y_done, head)
                        if head < GLA_H:
                            act.wait_ge(o_evac, NT * (head // 2 + 1))
                        else:
                            act.wait_ge(pv_evac, 4 * (head - GLA_H + 1))
                        nc.scalar.activation(buf[:, :], yT[:, head, :], ACT.Square).then_inc(sq_done, 1)

                    def norm_rs(head, buf, b):
                        act.wait_ge(norm_done, head + 1)
                        nc.scalar.activation(buf[:, :], bank(b, 2), ACT.Ln, scale=1.0 / DV, bias=EPS)\
                            .then_inc(ln_done, 1)
                        act.wait_ge(ln_done, head + 1)
                        nc.scalar.activation(buf[:, :], buf[:, :], ACT.Exp, scale=-0.5).then_inc(rs_done, 1)

                    act.wait_ge(mods_ready, 3)
                    for n in range(KT):
                        high_h(n)
                    for v in range(VT):
                        high(VA0 + v, wv_hi[:, :, v * P:(v + 1) * P])
                    high_t(0)
                    high_t(1)
                    for t in range(NT):
                        evacuate(UNIT[("va", t)], va[:, t, :])
                        if t < NT // 2:
                            high_h(KT + 2 * t)
                            high_h(KT + 2 * t + 1)
                    for half in range(2):
                        evacuate(TU(T_LR, half), lrT[:, half * HALF:(half + 1) * HALF], LOWRANK)
                    high_t(2)

                    for j in range(PAIRS):
                        act.wait_ge(dk_abs, j + 1)
                        nc.scalar.activation(k_e[:, :], k_e[:, :], ACT.Exp, scale=-1.0).then_inc(dk_soft, 1)
                        act.wait_ge(dk_soft, 2 * j + 1)
                        nc.scalar.activation(k_e[:, :], k_e[:, :], ACT.Ln, bias=1.0).then_inc(dk_soft, 1)
                        act.wait_ge(dk_cum, j + 1)
                        nc.scalar.activation(q_e[:, :], cum[:, :], ACT.Exp).then_inc(dk_exp, 1)
                        nc.scalar.activation(k_e[:, :], cum[:, :], ACT.Exp, scale=-1.0).then_inc(dk_exp, 1)
                        act.wait_ge(dk_rest, j + 1)
                        nc.scalar.activation(k_dT[:, :], k_dT[:, :], ACT.Exp).then_inc(dk_exp, 1)
                        nc.scalar.activation(decay, cum[:, CHUNK - 1:S:CHUNK], ACT.Exp).then_inc(dk_exp, 1)
                        if j:
                            for e in range(2):
                                norm_square(2 * (j - 1) + e, sq_a)
                                norm_rs(2 * (j - 1) + e, sq_a, 2)
                        high_t(T_A(j, 2))
                        high_t(T_A(j, 3))
                        for q in range(2):
                            act.wait_ge(kd_done, 2 * j + q + 1)
                            nc.scalar.copy(k_end[:, 4 * q:4 * q + 4, :].rearrange("p t k -> p (t k)"), bank(6 + q))\
                                .then_inc(kend_ready, 1)
                        for p in range(NT):
                            if p % 2:
                                z = p // 2
                                z_unit(2 * j + z // 2, T_A(j, 2 + z // 2), z % 2, za_s[:, z // 2, :])
                                if z == 1:
                                    if j == PAIRS - 1:
                                        for v in range(VT):
                                            high(VB0 + v, wv_hi[:, :, v * P:(v + 1) * P])
                                    high_t(T_A(j, 4))
                            act.wait_ge(o_done, NT * j + p + 1)
                            nc.scalar.copy(yT[:, 2 * j:2 * j + 2, p * P:(p + 1) * P], ps[:, 6:8, 0:P])\
                                .then_inc(o_evac, 1)
                            if p == NT - 1 and j == 0:
                                high_t(T_A(j, 5))
                    high_t(T_B(0, 1))
                    for t in range(NT):
                        evacuate(UNIT[("vb", t)], vb[:, t, :])
                        if t == 0:
                            for head in (2, 3):
                                norm_square(head, sq_a)
                                norm_rs(head, sq_a, 2)

                    def attend(h, i, unit_work):
                        if i < NT:
                            n = NT * h + i
                            act.wait_ge(s_masked, n + 1)
                            nc.scalar.activation(pr[:, i % 2, 0:(i + 1) * P], pr[:, i % 2, 0:(i + 1) * P], ACT.Exp,
                                                 scale=-1.0, bias=nmax[:, i % 2:i % 2 + 1],
                                                 accum_out=den[:, i % 2:i % 2 + 1]).then_inc(exp_done, 1)
                        def evacuate_pt(part, j0, j1):
                            q = i - 1
                            c = pt_chunk(h, q, part)
                            act.wait_ge(pt_done, c + 1)
                            if q % 2 == 0 and part == 0 and (h or q):
                                act.wait_ge(pv_done, 4 * h + q // 2)
                            nc.scalar.copy(pT[:, j0:j1, (q % 2) * P:(q % 2 + 1) * P],
                                           bank(6)[:, 0:(j1 - j0) * P].rearrange("p (j q) -> p j q", q=P))\
                                .then_inc(pt_evac, 1)
                        if 3 <= i and i % 2:
                            g = (i - 3) // 2
                            act.wait_ge(pv_done, 4 * h + g + 1)
                            nc.scalar.copy(yT[:, GLA_H + h, 2 * P * g:2 * P * (g + 1)], bank(7)[:, 0:2 * P])\
                                .then_inc(pv_evac, 1)
                        if 1 <= i <= NT:
                            evacuate_pt(0, *pt_parts(i - 1)[0])
                        unit_work()
                        if 5 <= i <= NT:
                            evacuate_pt(1, *pt_parts(i - 1)[1])

                    def slot_unit(h, n):
                        kind, half = divmod(n, 2)
                        t = T_B(h, kind)
                        if kind == 2:
                            z_unit(GLA_H + h, t, half, zb_1 if h % 2 else zb_0)
                        if half:
                            high_t(t + 2)

                    for h in range(DIL_H + 1):
                        done_units = 0
                        for i in range(NT + 2):
                            def unit_work(i=i, h=h):
                                if h < DIL_H and i in UNIT_STEPS:
                                    slot_unit(h, UNIT_STEPS.index(i))
                                if i == 0 and h >= 2:
                                    norm_square(GLA_H + h - 2, sq_b)
                                    norm_rs(GLA_H + h - 2, sq_b, 4)
                                if h == DIL_H and 1 <= i <= 7:
                                    high_y(i - 1)
                            def high_y(n):
                                act.wait_ge(unit_done, N_UNITS)
                                act.wait_ge(y_done, n + 1)
                                nc.scalar.copy(act_hi[:, n, :], yT[:, n, :]).then_inc(y_hi, 1)
                            if h:
                                attend(h - 1, i, unit_work)
                            else:
                                unit_work()
                    norm_square(GLA_H + DIL_H - 1, sq_last)
                    act.wait_ge(pv_done, 4 * DIL_H)
                    high(WO0, wo_hi[:, :, 0:P])
                    high(WO0 + 1, wo_hi[:, :, P:2 * P])
                    norm_rs(GLA_H + DIL_H - 1, sq_last, 4)
                    high(WO0 + 2, wo_hi[:, :, 2 * P:3 * P])
                    high_y(GLA_H + DIL_H - 1)
                    for v in range(3, KT):
                        high(WO0 + v, wo_hi[:, :, v * P:(v + 1) * P])

                    for t in range(NT):
                        b = 0 if t % 2 else 2
                        act.wait_ge(yp_done, t + 1)
                        if t == 0:
                            act.wait_ge(y_lo_pool, 4)
                            act.wait_ge(y_lo_dve, 4)
                            act.wait_ge(y_hi, 8)
                        nc.scalar.activation(yT[:, t, :], bank(b, 2), ACT.Square, accum_out=ss[:, t % 2:t % 2 + 1])\
                            .then_inc(sqy_done, 1)
                        act.wait_ge(sqy_done, t + 1)
                        nc.scalar.activation(lnt[:, t % 2:t % 2 + 1], ss[:, t % 2:t % 2 + 1], ACT.Ln, scale=1.0 / D,
                                             bias=EPS).then_inc(act_seq, 1)
                        act.wait_ge(act_seq, 3 * t + 1)
                        nc.scalar.activation(rstd[:, t % 2:t % 2 + 1], lnt[:, t % 2:t % 2 + 1], ACT.Exp, scale=-0.5)\
                            .then_inc(rstd_y, 1)
                        act.wait_ge(x_new, t + 1)
                        nc.scalar.activation(yT[:, t, :], x_t[:, t % 2, :], ACT.Square,
                                             accum_out=ss2[:, t % 2:t % 2 + 1]).then_inc(act_seq, 1)
                        act.wait_ge(act_seq, 3 * t + 2)
                        nc.scalar.activation(lnt2[:, t % 2:t % 2 + 1], ss2[:, t % 2:t % 2 + 1], ACT.Ln, scale=1.0 / D,
                                             bias=EPS).then_inc(act_seq, 1)
                        act.wait_ge(act_seq, 3 * t + 3)
                        nc.scalar.activation(rstd2[:, t % 2:t % 2 + 1], lnt2[:, t % 2:t % 2 + 1], ACT.Exp,
                                             scale=-0.5).then_inc(rstd_n, 1)

                @block.vector
                def _(dve):
                    count = [0]

                    def link(ins):
                        count[0] += 1
                        ins.then_inc(dve_seq, 1)
                        dve.wait_ge(dve_seq, count[0])

                    V = nc.vector

                    def low(j, dst, src_hi):
                        dve.wait_ge(w_hi, j + 1)
                        n = SPLIT[j]
                        V.tensor_tensor(dst, raw[:, n % RING, :, :], src_hi.bitcast(f32), SUB).then_inc(w_lo_dve, 1)

                    def h_group(n):
                        half, k = divmod(n, KT)
                        cols = slice(half * HALF, (half + 1) * HALF)
                        dve.wait_ge(h_hi, n + 1)
                        if n >= 4:
                            wait_h_low(dve, n - 4)
                        V.tensor_scalar(h_tmp[:, n % 4, :], bank(2 + n % 6), h_scale[:, k:k + 1],
                                        h_shift[:, k:k + 1], MULT, ADD).then_inc(h_full, 1)
                        if n % 2 == 0:
                            dve.wait_ge(h_full, n + 1)
                            V.tensor_tensor(act_lo[:, k, cols], h_tmp[:, n % 4, :], act_hi[:, k, cols].bitcast(f32),
                                            SUB).then_inc(h_lo_dve, 1)

                    def z_unit(head, t, half, dst, zn):
                        cols = slice(half * HALF, (half + 1) * HALF)
                        u = TU(t, half)
                        dve.wait_ge(z_exp, zn)
                        link(V.tensor_scalar_add(dst[:, cols], dst[:, cols], 1.0))
                        link(V.reciprocal(dst[:, cols], dst[:, cols]))
                        V.scalar_tensor_tensor(out=dst[:, cols], in0=bank(u % 2), scalar=g_head[:, head:head + 1],
                                               in1=dst[:, cols], op0=MULT, op1=MULT).then_inc(unit_free[u % 2], 1)

                    def finish_y(head, buf, z):
                        dve.wait_ge(rs_done, head + 1)
                        link(V.tensor_tensor(yT[:, head, :], yT[:, head, :], buf[:, :], MULT))
                        V.tensor_tensor(yT[:, head, :], yT[:, head, :], z[:, :], MULT).then_inc(y_done, 1)

                    dve.wait_ge(raw_used, ADA_TILES)
                    dve.wait_ge(vec_in, 16)
                    V.tensor_tensor(mod, bank(0)[:, 0:ADA_TILES], b_ada_c, ADD).then_inc(mods_ready, 1)
                    dve.wait_ge(mods_ready, 1)
                    V.tensor_scalar_add(h_scale, mod[:, KT:2 * KT], 1.0).then_inc(mods_ready, 1)
                    dve.wait_ge(mods_ready, 2)
                    V.tensor_tensor(h_scale, h_scale, g_pre_c, MULT).then_inc(mods_ready, 1)
                    dve.wait_ge(mods_ready, 3)
                    for n in range(KT):
                        h_group(n)
                    for v in range(VT):
                        if low_on_vector(VA0 + v):
                            low(VA0 + v, wv_lo[:, :, v * P:(v + 1) * P], wv_hi[:, :, v * P:(v + 1) * P])
                    for n in range(KT, 2 * KT):
                        h_group(n)
                    link(V.memset(yT[:, 5, 0:4 * P], 0.0))

                    zn = 0
                    for j in range(PAIRS):
                        dve.wait_ge(dk_z, 2 * (j + 1))
                        if j:
                            dve.wait_ge(o_done, NT * j)
                            dve.wait_ge(kd_done, 2 * j)
                        link(V.tensor_scalar(q_e[:, :], bank(4, 2), b_gu_c[:, j:j + 1], None, ADD))
                        V.scalar_tensor_tensor(out=k_e[:, :], in0=q_e[:, :], scalar=-1.0, in1=q_e[:, :],
                                               op0=MULT, op1=MAX).then_inc(dk_abs, 1)
                        link(V.tensor_scalar(k_dT[:, :], q_e[:, :], 0.0, 1.0 / 16.0, MIN, MULT))
                        dve.wait_ge(dk_soft, 2 * (j + 1))
                        link(V.scalar_tensor_tensor(out=q_e[:, :], in0=k_e[:, :], scalar=-1.0 / 16.0,
                                                    in1=k_dT[:, :], op0=MULT, op1=ADD))
                        for c in range(S // CHUNK):
                            cs = slice(c * CHUNK, (c + 1) * CHUNK)
                            last = V.tensor_tensor_scan(cum[:, cs], ones[:, 0:CHUNK], q_e[:, cs], 0.0, MULT, ADD)
                        last.then_inc(dk_cum, 1)
                        dve.wait_ge(dk_cum, j + 1)
                        cum3 = cum[:, :].rearrange("p (c i) -> p c i", i=CHUNK)
                        V.tensor_tensor(k_dT[:, :].rearrange("p (c i) -> p c i", i=CHUNK),
                                        cum3[:, :, CHUNK - 1:CHUNK].broadcast_to([P, S // CHUNK, CHUNK]), cum3,
                                        SUB).then_inc(dk_rest, 1)
                        if j:
                            for e in range(2):
                                finish_y(2 * (j - 1) + e, sq_a, za_s[:, e, :])
                        for half in range(2):
                            cols = slice(half * HALF, (half + 1) * HALF)
                            u = TU(T_A(j, 0), half)
                            dve.wait_ge(dk_exp, 4 * j + 1)
                            dve.wait_ge(unit_done, u + 1)
                            V.scalar_tensor_tensor(out=q_e[:, cols], in0=bank(u % 2), scalar=DK ** -0.5,
                                                   in1=q_e[:, cols], op0=MULT, op1=MULT).then_inc(unit_free[u % 2], 1)
                        for half in range(2):
                            cols = slice(half * HALF, (half + 1) * HALF)
                            u = TU(T_A(j, 1), half)
                            dve.wait_ge(dk_exp, 4 * j + 4)
                            dve.wait_ge(unit_done, u + 1)
                            V.tensor_tensor(k_e[:, cols], bank(u % 2), k_e[:, cols], MULT).then_inc(dve_seq, 1)
                            count[0] += 1
                            V.tensor_tensor(k_dT[:, cols], bank(u % 2), k_dT[:, cols], MULT)\
                                .then_inc(unit_free[u % 2], 1)

                        def mask_and_states(p):
                            s = NT * j + p
                            dve.wait_ge(at_done, s + 1)
                            if s >= 2:
                                dve.wait_ge(o_done, s - 1)
                            V.copy_predicated(at_sb[:, p % 2, :, :],
                                              causal_sb[:, :].rearrange("p (a i) -> p a i", a=1)
                                              .broadcast_to([P, 2, P]),
                                              ps[:, 2:4, 0:P]).then_inc(at_masked, 1)
                            dve.wait_ge(cs_done, s + 1)
                            if p == 0 and j:
                                dve.wait_ge(o_done, NT * j)
                            for e in range(2):
                                c = 2 * p + e
                                if c == 2 * NT - 1:
                                    continue
                                new = state[:, (c + 1) % 6, :]
                                if c == 0:
                                    V.tensor_copy(new, bank(4)[:, 0:DV]).then_inc(state_done, 1)
                                else:
                                    dve.wait_ge(state_done, states(j, c))
                                    V.scalar_tensor_tensor(out=new, in0=state[:, c % 6, :], scalar=decay[:, c:c + 1],
                                                           in1=bank(4 + e)[:, 0:DV], op0=MULT, op1=ADD)\
                                        .then_inc(state_done, 1)

                        mask_and_states(0)
                        for p in range(NT):
                            if p + 1 < NT:
                                mask_and_states(p + 1)
                            if p % 2:
                                z = p // 2
                                zn += 1
                                z_unit(2 * j + z // 2, T_A(j, 2 + z // 2), z % 2, za_s[:, z // 2, :], zn)
                    for head in (2, 3):
                        finish_y(head, sq_a, za_s[:, head % 2, :])

                    dve.wait_ge(tab_in, 48)

                    def rope(h, n):
                        kind, half = divmod(n, 2)
                        cols = slice(half * HALF, (half + 1) * HALF)
                        dst = qkT[:, 2 * (h % 2) + kind, cols]
                        u = TU(T_B(h, kind), half)
                        dve.wait_ge(unit_done, u + 1)
                        V.tensor_tensor(dst, bank(u % 2), cos_t[:, cols], MULT).then_inc(dve_seq, 1)
                        m = 4 * h + n
                        tmp = r_tmp[:, m % 2, :]
                        if m >= 2:
                            wait_unit_evacuated(dve, TU(T_B((m - 2) // 4, (m - 2) % 4 // 2), m % 2))
                        V.tensor_tensor(tmp[0:64, :], bank(u % 2)[64:128, :], sin_t[64:128, cols], MULT)\
                            .then_inc(dve_seq, 1)
                        V.tensor_tensor(tmp[64:128, :], bank(u % 2)[0:64, :], sin_t[0:64, cols], MULT)\
                            .then_inc(dve_seq, 1)
                        count[0] += 3
                        dve.wait_ge(dve_seq, count[0])
                        V.tensor_tensor(dst, dst, tmp, ADD).then_inc(unit_free[u % 2], 1)

                    for h in range(DIL_H + 1):
                        for i in range(NT + 2):
                            if h and i < NT:
                                n = NT * (h - 1) + i
                                w = (i + 1) * P
                                dve.wait_ge(s_done, n + 1)
                                if n >= 2:
                                    last = pt_chunk(h - 1, i - 2, 1 if i >= 6 else 0) if i >= 2 else \
                                        pt_chunk(h - 2, NT + i - 2, 1)
                                    dve.wait_ge(pt_done, last + 1)
                                V.tensor_tensor_reduce(out=pr[:, i % 2, 0:w], in0=bank(2 + 2 * (i % 2), 2)[:, 0:w],
                                                       in1=cnt_t[:, S - w:S], scale=-SCORE_SCALE, scalar=-NEG,
                                                       op0=ADD, op1=MIN, accum_out=nmax[:, i % 2:i % 2 + 1])\
                                    .then_inc(s_masked, 1)
                                dve.wait_ge(exp_done, n + 1)
                                link(V.reciprocal(rden[:, i % 2:i % 2 + 1], den[:, i % 2:i % 2 + 1]))
                                V.tensor_scalar(pr[:, i % 2, 0:w], pr[:, i % 2, 0:w], rden[:, i % 2:i % 2 + 1], None,
                                                MULT).then_inc(p_ready, 1)
                            if h < DIL_H and i in UNIT_STEPS:
                                n = UNIT_STEPS.index(i)
                                if n < 4:
                                    rope(h, n)
                                else:
                                    zn += 1
                                    z_unit(GLA_H + h, T_B(h, 2), n % 2, zb_1 if h % 2 else zb_0, zn)
                            if i == 0 and h >= 2:
                                head = GLA_H + h - 2
                                finish_y(head, sq_b, zb_1 if head % 2 else zb_0)
                            if h == DIL_H and i in (2, 4, 6):
                                dve.wait_ge(y_hi, i)
                                V.tensor_tensor(act_lo[:, i - 1, :], yT[:, i - 1, :], act_hi[:, i - 1, :].bitcast(f32),
                                                SUB).then_inc(y_lo_dve, 1)
                    low(WO0 + 1, wo_lo[:, :, P:2 * P], wo_hi[:, :, P:2 * P])
                    finish_y(GLA_H + DIL_H - 1, sq_last, zb_1)
                    dve.wait_ge(y_hi, GLA_H + DIL_H)
                    V.tensor_tensor(act_lo[:, 7, :], yT[:, 7, :], act_hi[:, 7, :].bitcast(f32), SUB)\
                        .then_inc(y_lo_dve, 1)
                    for v in range(3, KT, 2):
                        low(WO0 + v, wo_lo[:, :, v * P:(v + 1) * P], wo_hi[:, :, v * P:(v + 1) * P])
                    dve.wait_ge(raw_used, ADA_TILES + GATE_TILES)
                    dve.wait_ge(row_in, 32)
                    V.tensor_tensor(x_t[:, 0, :], bank(0, 2), x_t[:, 0, :], ADD).then_inc(gate_ready, 1)
                    dve.wait_ge(gate_ready, 1)
                    V.tensor_tensor(gate_t[:, :], gate_t[:, :], x_t[:, 0, :], MULT).then_inc(gate_ready, 1)
                    dve.wait_ge(gate_ready, 2)
                    for t in range(NT):
                        b = 0 if t % 2 else 2
                        dve.wait_ge(rstd_y, t + 1)
                        V.scalar_tensor_tensor(out=yT[:, t, :], in0=bank(b, 2), scalar=rstd[:, t % 2:t % 2 + 1],
                                               in1=gate_t[:, :], op0=MULT, op1=MULT).then_inc(yp_free, 1)
                        dve.wait_ge(yp_free, t + 1)
                        dve.wait_ge(x_load[t % 2], 16 * (t // 2 + 1))
                        V.tensor_tensor(x_t[:, t % 2, :], x_t[:, t % 2, :], yT[:, t, :], ADD).then_inc(x_new, 1)
                        dve.wait_ge(rstd_n, t + 1)
                        V.tensor_scalar(yT[:, t, :], x_t[:, t % 2, :], rstd2[:, t % 2:t % 2 + 1], None, MULT)\
                            .then_inc(xn_done, 1)

                @block.tensor
                def _(pe):
                    mm = nc.tensor.matmul

                    def wait_raw(n):
                        pe.wait_ge(raw_in[n % RING], 16 * (n // RING + 1))

                    def wait_split(j):
                        wait_low(pe, j)

                    def wait_bank(u):
                        if u >= 2:
                            pe.wait_ge(unit_free[u % 2], u // 2)

                    def product(dst, pairs):
                        n = len(pairs)
                        for k, (shi, slo, mhi, mlo) in enumerate(pairs):
                            mm(dst, shi, mhi, start=(k == 0), stop=False)
                            mm(dst, shi, mlo, start=False, stop=False)
                            last = mm(dst, slo, mhi, start=False, stop=(k == n - 1))
                        return last

                    def natural(dst, t, hi, lo, cols):
                        tok = slice(t * P, (t + 1) * P)
                        return product(dst, [(act_hi[:, k, tok], act_lo[:, k, tok], hi[:, k, cols], lo[:, k, cols])
                                             for k in range(KT)])

                    def v_unit(kind, t):
                        u = UNIT[(kind, t)]
                        wait_bank(u)
                        natural(bank(u % 2), t, wv_hi, wv_lo, slice(0, VT * P)).then_inc(unit_done, 1)

                    def t_unit(t, half):
                        u = TU(t, half)
                        wait_bank(u)
                        wait_split(split_index(t))
                        tok = slice(half * HALF, (half + 1) * HALF)
                        product(bank(u % 2), [(wt_hi[:, t % 2, k, :], wt_lo[:, t % 2, k, :], act_hi[:, k, tok],
                                               act_lo[:, k, tok]) for k in range(KT)]).then_inc(unit_done, 1)

                    def norm(head, buf, b):
                        pe.wait_ge(sq_done, head + 1)
                        if head:
                            pe.wait_ge(ln_done, head)
                        for half in range(2):
                            last = mm(bank(b + half), ones[:, :], buf[:, half * HALF:(half + 1) * HALF], start=True,
                                      stop=True)
                        last.then_inc(norm_done, 1)

                    def gate_tile(n):
                        s = STREAM.index("gate") + n
                        wait_raw(s)
                        if n == 0:
                            wait_unit_evacuated(pe, N_UNITS - 2)
                            wait_unit_evacuated(pe, N_UNITS - 1)
                        for k in range(KT):
                            last = mm(bank(n // 4)[:, (n % 4) * P:(n % 4 + 1) * P],
                                      silu_c[:, k:k + 1].broadcast_to([P, P]), raw[:, s % RING, k, :],
                                      start=(k == 0), stop=(k == KT - 1))
                        last.then_inc(raw_used, 1)

                    for n in range(ADA_TILES):
                        wait_raw(n)
                        for k in range(KT):
                            last = mm(bank(0)[:, n:n + 1], raw[:, n % RING, k, :], silu_c[:, k:k + 1],
                                      start=(k == 0), stop=(k == KT - 1))
                        last.then_inc(raw_used, 1)

                    def xn_group(n):
                        half, k = divmod(n, KT)
                        if n >= 6:
                            pe.wait_ge(h_full, n - 5)
                        for t in range(4):
                            last = nc.tensor.transpose(bank(2 + n % 6)[:, t * P:(t + 1) * P],
                                                       yT[:, 4 * half + t, k * P:(k + 1) * P], idn[:, :])
                        last.then_inc(xnT_done, 1)

                    for n in range(KT):
                        xn_group(n)
                    for n in (KT - 1, KT - 2):
                        wait_h_low(pe, n)
                    for v in range(VT):
                        wait_split(VA0 + v)
                    for t in range(NT):
                        if t == NT // 2:
                            for n in (2 * KT - 1, 2 * KT - 2):
                                wait_h_low(pe, n)
                        v_unit("va", t)
                        if t < NT // 2:
                            xn_group(KT + 2 * t)
                            xn_group(KT + 2 * t + 1)
                    t_unit(T_LR, 0)
                    t_unit(T_LR, 1)

                    for j in range(PAIRS):
                        if j == 0:
                            wait_unit_evacuated(pe, TU(T_LR, 0))
                            wait_unit_evacuated(pe, TU(T_LR, 1))
                            pe.wait_ge(gu_in, 16)
                        else:
                            pe.wait_ge(state_done, states(j, 0))
                        for half in range(2):
                            mm(bank(4 + half), w_gu[:, j * P:(j + 1) * P], lrT[:, half * HALF:(half + 1) * HALF],
                               start=True, stop=True).then_inc(dk_z, 1)
                        t_unit(T_A(j, 0), 0)
                        if j:
                            pe.wait_ge(at_masked, NT * j)
                            norm(2 * (j - 1), sq_a, 2)
                        t_unit(T_A(j, 0), 1)
                        if j:
                            norm(2 * (j - 1) + 1, sq_a, 2)
                        t_unit(T_A(j, 1), 0)
                        t_unit(T_A(j, 1), 1)
                        wait_unit_evacuated(pe, TU(T_A(j, 1), 0))
                        wait_unit_evacuated(pe, TU(T_A(j, 1), 1))
                        if j:
                            pe.wait_ge(o_evac, NT * j)
                            pe.wait_ge(ln_done, 2 * j)
                        for q in range(2):
                            for t in range(4):
                                last = nc.tensor.transpose(bank(6 + q)[:, t * P:(t + 1) * P],
                                                           k_dT[:, (4 * q + t) * P:(4 * q + t + 1) * P], idn[:, :])
                            last.then_inc(kd_done, 1)
                        pe.wait_ge(kend_ready, 2 * (j + 1))

                        def scores_and_chunk_states(p):
                            s = NT * j + p
                            tok = slice(p * P, (p + 1) * P)
                            if s:
                                pe.wait_ge(at_masked, s)
                            for e in range(2):
                                rows_ = slice(e * DK, (e + 1) * DK)
                                last = mm(bank(2 + e)[:, 0:P], k_e[rows_, tok], q_e[rows_, tok], start=True, stop=True)
                            last.then_inc(at_done, 1)
                            pe.wait_ge(dk_abs, j + 1)
                            if s:
                                pe.wait_ge(state_done, states(j, 2 * p))
                            for c in range(2):
                                in_chunk = slice(c * CHUNK, (c + 1) * CHUNK)
                                for e in range(2):
                                    if p == NT - 1 and c == 1:
                                        continue
                                    g = 2 * j + e
                                    last = mm(bank(4 + c)[e * DK:(e + 1) * DK, 0:DV],
                                              k_end[in_chunk, p, e * DK:(e + 1) * DK],
                                              va[in_chunk, p, g * DV:(g + 1) * DV], start=True, stop=True)
                            last.then_inc(cs_done, 1)

                        def outputs(p):
                            s = NT * j + p
                            pe.wait_ge(at_masked, s + 1)
                            pe.wait_ge(state_done, states(j, 2 * p + 1))
                            if s:
                                pe.wait_ge(o_evac, s)
                            for e in range(2):
                                g = 2 * j + e
                                rows_ = slice(e * DK, (e + 1) * DK)
                                mm(bank(6 + e)[:, 0:P], va[:, p, g * DV:(g + 1) * DV], at_sb[:, p % 2, e, :],
                                   start=True, stop=False)
                                for c in (2 * p, 2 * p + 1):
                                    if c:
                                        i0 = (c % 2) * CHUNK
                                        last = mm(bank(6 + e)[:, i0:i0 + CHUNK], state[rows_, c % 6, :],
                                                  q_e[rows_, c * CHUNK:(c + 1) * CHUNK], start=False,
                                                  stop=(c == 2 * p + 1))
                            last.then_inc(o_done, 1)

                        scores_and_chunk_states(0)
                        for p in range(NT):
                            if p + 1 < NT:
                                scores_and_chunk_states(p + 1)
                            if p % 2:
                                t_unit(T_A(j, 2 + p // 4), (p // 2) % 2)
                            outputs(p)

                    for v in range(VT):
                        wait_split(VB0 + v)
                    for t in range(NT):
                        v_unit("vb", t)
                        if t in (1, 2):
                            norm(t + 1, sq_a, 2)

                    def attend(h, i, unit_work):
                        q_t, k_t = qkT[:, 2 * (h % 2), :], qkT[:, 2 * (h % 2) + 1, :]
                        if i < NT:
                            n = NT * h + i
                            b = 2 + 2 * (i % 2)
                            if n >= 2:
                                pe.wait_ge(s_masked, n - 1)
                            pe.wait_ge(ln_done, GLA_H + h if i else GLA_H + max(h - 1, 0))
                            for half in range(-(-(i + 1) // 4)):
                                w = min((i + 1) * P - half * HALF, HALF)
                                last = mm(bank(b + half)[:, 0:w], q_t[:, i * P:(i + 1) * P],
                                          k_t[:, half * HALF:half * HALF + w], start=True, stop=True)
                            last.then_inc(s_done, 1)
                        if i >= 3 and i % 2:
                            g = (i - 3) // 2
                            pe.wait_ge(pt_evac, pt_chunk(h, 2 * g + 1, 1 if g >= 2 else 0) + 1)
                            if 4 * h + g:
                                pe.wait_ge(pv_evac, 4 * h + g)
                            for j in range(2 * g + 2):
                                c0 = P if j == 2 * g + 1 else 0
                                last = mm(bank(7)[:, c0:2 * P], vb[:, j, h * HD:(h + 1) * HD], pT[:, j, c0:2 * P],
                                          start=(j == 0), stop=(j == 2 * g + 1))
                            last.then_inc(pv_done, 1)

                        def transpose_p(part, j0, j1):
                            q = i - 1
                            c = pt_chunk(h, q, part)
                            pe.wait_ge(p_ready, NT * h + q + 1)
                            if c:
                                pe.wait_ge(pt_evac, c)
                            for j in range(j0, j1):
                                last = nc.tensor.transpose(bank(6)[:, (j - j0) * P:(j - j0 + 1) * P],
                                                           pr[:, q % 2, j * P:(j + 1) * P], idn[:, :])
                            last.then_inc(pt_done, 1)
                        if 1 <= i <= NT:
                            transpose_p(0, *pt_parts(i - 1)[0])
                        unit_work()
                        if 5 <= i <= NT:
                            transpose_p(1, *pt_parts(i - 1)[1])

                    for h in range(DIL_H + 1):
                        if h:
                            for kind in range(2):
                                for half in range(2):
                                    wait_unit_evacuated(pe, TU(T_B(h - 1, kind), half))
                        for i in range(NT + 2):
                            def unit_work(i=i, h=h):
                                if h < DIL_H and i in UNIT_STEPS:
                                    kind, half = divmod(UNIT_STEPS.index(i), 2)
                                    t_unit(T_B(h, kind), half)
                                if h == DIL_H and i in (1, 3, 5, 7):
                                    gate_tile(i // 2)
                                if i == 0 and h >= 2:
                                    pe.wait_ge(s_masked, NT * (h - 1))
                                    norm(GLA_H + h - 2, sq_b, 4)
                            if h:
                                attend(h - 1, i, unit_work)
                            else:
                                unit_work()
                    gate_tile(4)
                    pe.wait_ge(s_masked, NT * DIL_H)
                    norm(GLA_H + DIL_H - 1, sq_last, 4)
                    for n in range(5, GATE_TILES):
                        gate_tile(n)

                    pe.wait_ge(y_lo_pool, 4)
                    pe.wait_ge(y_lo_dve, 4)
                    pe.wait_ge(s_masked, NT * DIL_H)
                    for t in range(NT):
                        b = 0 if t % 2 else 2
                        if t >= 2:
                            pe.wait_ge(yp_free, t - 1)
                        if t == 1:
                            pe.wait_ge(gate_ready, 1)
                        for half in range(2):
                            if t == 0:
                                for v in range(4 * half, 4 * half + 4):
                                    wait_split(WO0 + v)
                            last = natural(bank(b + half), t, wo_hi, wo_lo, slice(half * HALF, (half + 1) * HALF))
                        last.then_inc(yp_done, 1)
            nc.all_engine_barrier(sems_to_clear=range(names[0].num, names[-1].num + 1))


def kernel(**inputs):
    import concourse.bacc as bacc
    from concourse.bass_utils import run_bass_kernel_spmd as run

    def arr(name):
        return np.asarray(inputs[name])

    def cols(v):
        return v.reshape(-1, P).T

    w_ada, w_in, w_out = arr("w_ada"), arr("w_in"), arr("w_out")
    lr0 = 2 * GLA_H * DK + 2 * GLA_H * DV
    b0 = lr0 + LOWRANK
    wb = DIL_H * HD

    def column_tiles(layer):
        kz = {"qa": 0, "ka": GLA_H * DK}
        z0 = 2 * GLA_H * DK + GLA_H * DV
        out = [(w_ada, n * P) for n in range(ADA_TILES)]
        out += [(w_in, 2 * GLA_H * DK + v * P) for v in range(VT)]
        out.append((w_in, lr0))
        for j in range(PAIRS):
            out += [(w_in, j * P), (w_in, GLA_H * DK + j * P), (w_in, z0 + 2 * j * P), (w_in, z0 + (2 * j + 1) * P)]
        out += [(w_in, b0 + 2 * wb + v * P) for v in range(VT)]
        for h in range(DIL_H):
            out += [(w_in, b0 + h * P), (w_in, b0 + wb + h * P), (w_in, b0 + 3 * wb + h * P)]
        out += [(w_ada, (ADA_TILES + n) * P) for n in range(GATE_TILES)]
        out += [(w_out, n * P) for n in range(KT)]
        return [w[layer, :, c:c + P].reshape(KT, P, P).transpose(1, 0, 2).reshape(P, KT * P) for w, c in out]

    b_ada, g_pre, b_gu, g_gla, g_dil, g_post = (arr(n) for n in ("b_ada", "g_pre", "b_gate_up", "g_gla", "g_dil",
                                                                 "g_post"))
    inv = (10000.0 ** (-np.arange(0, HD, 2, dtype=np.float32) / HD)).astype(np.float32)
    ang = inv[:, None] * np.arange(S, dtype=np.float32)[None, :]
    cos, sin = np.cos(ang).astype(np.float32), np.sin(ang).astype(np.float32)
    dist = np.arange(P)[:, None] + (S - P) - np.arange(S)[None, :]
    times = sum(((dist >= 0) & (dist <= w) & (dist % d == 0)).astype(np.int64)
                for w, d in ((128, 1), (512, 4), (2048, 16)))
    with np.errstate(divide="ignore"):
        cnt = np.where(times > 0, np.log(np.maximum(times, 1)) / SCORE_SCALE, NEG).astype(np.float32)
    j, i = np.arange(P)[:, None], np.arange(P)[None, :]
    data = {
        "x": arr("x"),
        "tiles": np.stack([t for layer in range(DEPTH) for t in column_tiles(layer)]),
        "vecs": np.stack([np.concatenate([cols(b_ada[l, :2 * D]), cols(g_pre[l]), cols(b_gu[l]), cols(g_gla[l]),
                                          cols(g_dil[l])], axis=1) for l in range(DEPTH)]),
        "rows": np.stack([r for l in range(DEPTH) for r in (b_ada[l, 2 * D:], g_post[l])]),
        "w_gate_up": arr("w_gate_up").reshape(DEPTH * LOWRANK, GLA_H * DK),
        "c_cols": cols(arr("c")[0]),
        "rope_cos": np.concatenate([cos, cos]),
        "rope_sin": np.concatenate([sin, -sin]),
        "log_count": cnt,
        "ident": np.eye(P, dtype=np.float32),
        "causal": ((j <= i) & (j // CHUNK == i // CHUNK)).astype(np.int32),
    }
    data = {k: np.ascontiguousarray(v) for k, v in data.items()}
    nc = bacc.Bacc("TRN2", target_bir_lowering=False, num_devices=1)
    aps = {k: nc.dram_tensor(f"{k}_dram", v.shape, mybir.dt.from_np(v.dtype), kind="ExternalInput").ap()
           for k, v in data.items()}
    out = nc.dram_tensor("out_dram", (1, S, D), mybir.dt.float32, kind="ExternalOutput").ap()
    hybrid_trunk(nc, out=out, **aps)
    r = run(nc, [{f"{k}_dram": v for k, v in data.items()}], core_ids=[0])
    return r.results[0]["out_dram"]
```

```python
import numpy as np
import concourse.bass as bass
from concourse import mybir
from contextlib import ExitStack

P = 128
D = 1024
S = 1024
DEPTH = 2
KT = D // P
NT = S // P
HALF = S // 2
GLA_H, DK, DV, LOWRANK = 4, 64, 128, 16
CHUNK = 64
PAIRS = GLA_H // 2
DIL_H, HD = 4, 128
EPS = 1e-6
SCORE_SCALE = HD ** -0.5
ADA_TILES = 2 * D // P
GATE_TILES = D // P
VT = GLA_H * DV // P
NEG = -1e30

T_TILES = (["z0", "z1", "qa0", "ka0", "qa1", "ka1", "z2", "z3"]
           + [f"{n}{h}" for h in range(DIL_H) for n in ("qb", "kb", "zb")])
T_GLA = 8
FIRST_T = 2
NEXT = ["t"] * FIRST_T + ["va"] * VT
STREAM = (["t"] * (T_GLA - FIRST_T) + ["vb"] * VT + ["t"] * 3
          + ["t", "ada", "t", "ada", "t", "ada", "ada", "ada"] * (DIL_H - 1)
          + ["ada"] + ["gate"] * GATE_TILES + ["wo"] * KT)
RING = 4
assert VT == RING and (len(STREAM) + FIRST_T) % RING == 0 and FIRST_T < RING
VA0, VB0, WO0 = -VT, T_GLA - FIRST_T, len(STREAM) - KT


def positions(kind):
    return [n for n, k in enumerate(STREAM) if k == kind]


ADA_POS, GATE_POS = positions("ada"), positions("gate")


def position(t):
    return positions("t")[t - FIRST_T]


def slot(n):
    return n % RING


def lap(n):
    return n // RING + 1


def user(n):
    kind = "va" if n < 0 else (STREAM + NEXT)[n]
    if kind in ("gate", "ada"):
        return kind
    if kind == "va":
        return "dve" if n % 2 else "pool"
    if kind == "wo":
        return "dve" if (n - WO0) % 2 else "pool"
    return "pool"


def used(n):
    return sum(user(i) == user(n) for i in range(VA0, n + 1))


V_COLS = (GLA_H * DV + LOWRANK) // 2


def units():
    order = [(0, half) for half in range(2)]
    order += [("va", t, part) for part in (1, 0) for t in range(NT)]
    order += [(t, half) for t in range(1, T_GLA) for half in range(2)]
    order += [("vb", t) for t in range(NT)]
    order += [(t, half) for t in range(T_GLA, len(T_TILES)) for half in range(2)]
    return {key: n for n, key in enumerate(order)}


UNIT = units()
N_UNITS = len(UNIT)
MM = 3 * KT
STEP_MM = [14, 12, 14, 14, 16, 18, 16, 16, 12, 12]
assert sum(STEP_MM) == 6 * MM
FILL = {0: [12] * NT, 1: [9] * NT}
GATE_MM = [8, 6, 6, 8, 8, 8, 8, 8, 4, 0]
ADA_STEPS = ([(slot_, step) for slot_ in range(1, DIL_H) for step in (1, 3, 5, 7, 8)]
             + [(DIL_H, 0)])
POOL_Y = 4


def h_after(t):
    return {3: [0], 5: [1], 7: [2, 3]}.get(t, [])


def o_bank(t):
    return 0 if t % 2 else 4 if t == 2 else 2


def completed(budget, i):
    return range(sum(budget[:i]) // MM, sum(budget[:i + 1]) // MM)


def hybrid_trunk(nc, x, tiles, w_low, vecs, mods_in, rows, w_gate_up, c_cols, rope_cos, rope_sin, log_count, ident, causal, out):
    f32, f32r, i32 = mybir.dt.float32, mybir.dt.float32r, mybir.dt.int32
    ACT, ALU = mybir.ActivationFunctionType, mybir.AluOpType
    MULT, ADD, SUB, MAX, MIN = ALU.mult, ALU.add, ALU.subtract, ALU.max, ALU.min

    ctx = ExitStack()
    with ctx:
        def sb(name, shape, dt=f32):
            return ctx.enter_context(nc.sbuf_tensor(name, shape, dt))

        KB = 1024
        arena_at = -(-nc.sbuf_base // 32) * 32
        sb("arena", [P, 77 * KB // 4])

        def at(name, kb, shape, dt=f32):
            return nc.alloc_sbuf_tensor_at(name, shape, dt, offset=arena_at + int(kb * KB))

        act_hi = sb("act_hi", [P, KT, S], f32r)
        act_lo = sb("act_lo", [P, KT, S], f32r)
        yT = sb("yT", [P, GLA_H + DIL_H, S])
        wt_hi = sb("wt_hi", [P, 2, KT, P], f32r)
        wt_lo = sb("wt_lo", [P, 2, KT, P], f32r)
        raw = sb("raw", [P, RING, KT, P])
        raw_low = sb("raw_low", [P, KT, LOWRANK])
        idn = sb("idn", [P, P])
        ones = sb("ones", [P, P])
        causal_sb = sb("causal_sb", [P, P], i32)
        vec = sb("vec", [P, PAIRS + GLA_H + DIL_H])
        b_gu_c, g_head = vec[:, 0:PAIRS], vec[:, PAIRS:]
        vec_m = sb("vec_m", [P, ADA_TILES + KT])
        b_ada_c, g_pre_c = vec_m[:, 0:ADA_TILES], vec_m[:, ADA_TILES:]
        small = sb("small", [P, 128])
        c_sb, c_e, silu_c = small[:, 0:8], small[:, 8:16], small[:, 16:24]
        mod, h_scale = small[:, 24:40], small[:, 40:48]
        ss, rstd = small[:, 48:50], small[:, 50:52]
        ss2, rstd2 = small[:, 52:54], small[:, 54:56]
        decay = [small[:, 56:72], small[:, 112:128]]
        nmax, den, rden = small[:, 72:74], small[:, 74:76], small[:, 76:78]
        lnt, lnt2 = small[:, 78:80], small[:, 80:82]
        h_shift = mod[:, 0:8]
        ss8, ln8, rs8 = small[:, 84:92], small[:, 92:100], small[:, 100:108]


        silu_first = at("silu_first", 0, [P, D])
        h_junk = at("h_junk", 4, [P, D])
        WV = GLA_H * DV + LOWRANK
        wv_hi = at("wv_hi", 0, [P, KT, WV], f32r)
        wv_lo = at("wv_lo", 16.5, [P, KT, WV], f32r)
        va = at("va", 33, [P, NT, GLA_H * DV])
        cum_0 = at("cum_0", 49, [P, S])[:, :]
        za_s = at("za_s", 65, [P, 2, S])
        k_end = at("k_end", 73, [P, NT, P])
        w_gu = yT[0:LOWRANK, 4, 0:GLA_H * DK]
        state = yT[:, 4, 256:256 + 6 * DV].rearrange("p (r v) -> p r v", r=6)
        at_sb = yT[:, 5, 0:4 * P].rearrange("p (b e i) -> p b e i", b=2, e=2)
        low_n = yT[:, 5, 512:512 + NT * LOWRANK].rearrange("p (t r) -> p t r", t=NT)
        sq_a = yT[:, 6, :]
        lrT = yT[0:LOWRANK, 7, :]
        cum_1 = yT[:, 7, :]
        q_e = [at("q_e", 53, [P, S])[:, :], cum_0]
        k_e = [at("k_e", 57, [P, S])[:, :], yT[:, 2, :]]
        k_dT = [at("k_dT", 61, [P, S])[:, :], yT[:, 3, :]]
        cums = [cum_0, cum_1]
        za = [za_s[:, 0, :], za_s[:, 1, :], q_e[0], k_e[0]]
        silu_b = yT[:, 7, :]
        cos_t = at("cos_t", 0, [P, S])
        sin_t = at("sin_t", 4, [P, S])
        cnt_t = at("cnt_t", 8, [P, S])
        pT = at("pT", 12, [P, NT, 2 * P])
        sq_b = at("sq_b", 20, [P, S])
        r_tmp = at("r_tmp", 24, [P, 2, HALF])
        zb_0 = at("zb_0", 28, [P, S])
        vb = at("vb", 33, [P, NT, DIL_H * HD])
        qkT = at("qkT", 49, [P, 4, S])
        pr = at("pr", 65, [P, 2, S])
        zb_1 = at("zb_1", 73, [P, S])
        sq_last = at("sq_last", 65, [P, S])
        wo_hi = at("wo_hi", 0, [P, KT, D], f32r)
        wo_lo = at("wo_lo", 32, [P, KT, D], f32r)
        gate_t = at("gate_t", 65, [P, D])
        x_t = at("x_t", 69, [P, 2, D])
        r_tmp2 = r_tmp[:, :, :].rearrange("p a b -> p (a b)")

        def bank(n, count=1):
            return ps[:, n:n + count, :].rearrange("p b n -> p (b n)") if count > 1 else ps[:, n, :]

        ps = ctx.enter_context(nc.psum_tensor("ps", [P, 8, HALF], f32))

        sems = []

        def sem(name):
            sems.append(nc.alloc_semaphore(name))
            return sems[-1]

        const_in = [sem(f"const_in{i}") for i in range(4)]
        x_in = [sem(f"x_in{t}") for t in range(NT)]
        raw_in = [sem(f"raw_in{i}") for i in range(RING)]
        low_in, vec_in, mods_in_sem, gu_in, tab_in = (sem(n) for n in ("low_in", "vec_in", "vecm_in", "gu_in", "tab_in"))
        bias_in, post_in = sem("bias_in"), sem("post_in")
        gate_used, ada_used = sem("gate_used"), sem("ada_used")
        w_hi, w_lo_pool, w_lo_dve = sem("w_hi"), sem("w_lo_pool"), sem("w_lo_dve")
        low_split, silu_mm, silu_ready, mods_ready = (sem(n) for n in ("low_split", "silu_mm", "silu_ready", "mods_ready"))
        xnT_done, h_hi, h_lo = sem("xnT_done"), sem("h_hi"), sem("h_lo")
        xn_pool, h_full, h_lo_pool = sem("xn_pool"), sem("h_full"), sem("h_lo_pool")
        unit_done = sem("unit_done")
        unit_free = [sem("unit_free0"), sem("unit_free1")]
        z_abs, z_soft, z_arg, z_sig, z_done = (sem(n) for n in ("z_abs", "z_soft", "z_arg", "z_sig", "z_done"))
        lowT_done, lowT_evac, dk_z, dk_abs, dk_soft, dk_cum, dk_rest, dk_exp = (sem(n) for n in (
            "lowT_done", "lowT_evac", "dk_z", "dk_abs", "dk_soft", "dk_cum", "dk_rest", "dk_exp"))
        kd_done, kend_ready, at_done, at_masked, cs_done, state_done, o_done, o_evac = (sem(n) for n in (
            "kd_done", "kend_ready", "at_done", "at_masked", "cs_done", "state_done", "o_done", "o_evac"))
        sq_done, norm_done, ln_done, rs_done, y_done = (sem(n) for n in (
            "sq_done", "norm_done", "ln_done", "rs_done", "y_done"))
        s_done, s_masked, exp_done, p_ready, pt_done, pt_evac, pv_done, pv_evac = (sem(n) for n in (
            "s_done", "s_masked", "exp_done", "p_ready", "pt_done", "pt_evac", "pv_done", "pv_evac"))
        y_hi, y_lo_dve, y_lo_pool = sem("y_hi"), sem("y_lo_dve"), sem("y_lo_pool")
        gate_ready, yp_done, sqy_done, rstd_y, yp_free, x_new, sqx_done, rstd_x, xn_done = (sem(n) for n in (
            "gate_ready", "yp_done", "sqy_done", "rstd_y", "yp_free", "x_new", "sqx_done", "rstd_x", "xn_done"))
        x_load = [sem("x_load0"), sem("x_load1")]
        x_store = [sem("x_store0"), sem("x_store1")]
        dve_seq, act_seq = sem("dve_seq"), sem("act_seq")

        user_sem = {"gate": gate_used, "ada": ada_used, "pool": w_lo_pool, "dve": w_lo_dve}

        def wait_used(eng, n):
            eng.wait_ge(user_sem[user(n)], used(n))

        def highs(n):
            return sum(user(i) in ("pool", "dve") for i in range(VA0, n + 1))

        def wait_unit_evacuated(eng, u):
            eng.wait_ge(unit_free[u % 2], u // 2 + 1)

        def pt_chunk(h, i, part):
            return 12 * h + (i if i < 4 else 4 + 2 * (i - 4) + part)

        def pt_parts(i):
            return [(0, i + 1)] if i < 4 else [(0, 4), (4, i + 1)]

        def states(j, c):
            return (2 * NT - 1) * j + c

        T_Z = (0, 1, 6, 7)
        T_QA, T_KA = (2, 4), (3, 5)
        T_B = lambda h, n: T_GLA + 3 * h + n
        gla_fill = {0: [(t, half) for t in (T_QA[1], T_KA[1], T_Z[2]) for half in range(2)][:5],
                    1: [(t, half) for t in T_Z[2:] for half in range(2)][1:]}
        z_fill = [(2, gla_fill[1][0]), (3, gla_fill[1][1]), (3, gla_fill[1][2])]
        Z_ARG = 3
        VB_SPLIT = 3
        dil_units = lambda h: [(T_B(h, kind), half) for kind in range(3) for half in range(2)]
        PROLOGUE_RAW = 2

        def raw_tile(n):
            return raw[:, slot(n), :, :]

        def load_tile(sp, n, index):
            sp.dma_start(raw_tile(n), tiles[bass.ds(index, 1), :, :].rearrange("o p (k c) -> (o p) k c", k=KT))\
                .then_inc(raw_in[slot(n)], 16)

        def load_next(sp, n, first, wait):
            for i in range(len(NEXT)):
                wait(n + i)
                load_tile(sp, n + i, first + i)

        def mods(dve, k0, k1, seq):
            cols = slice(2 * k0, 2 * k1)
            nc.vector.tensor_tensor(mod[:, cols], mod[:, cols], b_ada_c[:, cols], ADD).then_inc(mods_ready, 1)
            dve.wait_ge(mods_ready, seq + 1)
            nc.vector.scalar_tensor_tensor(out=h_scale[:, k0:k1], in0=mod[:, 2 * k0 + 1:2 * k1:2], scalar=1.0,
                                           in1=g_pre_c[:, k0:k1], op0=ADD, op1=MULT).then_inc(mods_ready, 1)

        def ada_tile(n, silu):
            t = raw[:, slot(n[0]), :, :].rearrange("p k c -> p (k c)")
            nc.vector.tensor_tensor_reduce(out=t, in0=t, in1=silu[:, :], scale=1.0, scalar=0.0, op0=MULT, op1=ADD,
                                           accum_out=mod[:, n[1]:n[1] + 1]).then_inc(ada_used, 1)

        def h_bank(b, k):
            return ps[:, b + k // 2, (k % 2) * 2 * P:(k % 2 + 1) * 2 * P]

        def h_transpose(m, b, k):
            for t in range(2):
                last = nc.tensor.transpose(h_bank(b, k)[:, t * P:(t + 1) * P], yT[:, 2 * m + t, k * P:(k + 1) * P],
                                           idn[:, :])
            return last

        def h_high(m, b, k):
            nc.scalar.activation(act_hi[:, k, 2 * P * m:2 * P * (m + 1)], h_bank(b, k), ACT.Identity,
                                 scale=h_scale[:, k:k + 1], bias=mod[:, 2 * k:2 * k + 1]).then_inc(h_hi, 1)

        def h_low(dve, m, b, k, done, tmp):
            dst = act_lo[:, k, 2 * P * m:2 * P * (m + 1)]
            src_hi = act_hi[:, k, 2 * P * m:2 * P * (m + 1)].bitcast(f32)
            nc.vector.scalar_tensor_tensor(out=tmp, in0=h_bank(b, k), scalar=h_scale[:, k:k + 1], in1=src_hi,
                                           op0=MULT, op1=SUB).then_inc(h_lo, 1)
            dve.wait_ge(h_lo, 2 * done + 1)
            nc.vector.tensor_scalar(dst, tmp, mod[:, 2 * k:2 * k + 1], None, ADD).then_inc(h_lo, 1)

        def h_tmp(m, k):
            return yT[:, 2 * m + k // 4, (k % 4) * 2 * P:(k % 4 + 1) * 2 * P]

        def norm_x(act, t, buf, junk, n):
            nc.scalar.activation(junk, buf, ACT.Square, accum_out=ss8[:, t:t + 1]).then_inc(sqx_done, 1)
            act.wait_ge(sqx_done, 2 * n + 1)
            nc.scalar.activation(ln8[:, t:t + 1], ss8[:, t:t + 1], ACT.Ln, bias=EPS, scale=1.0 / D)\
                .then_inc(sqx_done, 1)
            act.wait_ge(sqx_done, 2 * n + 2)
            nc.scalar.activation(rs8[:, t:t + 1], ln8[:, t:t + 1], ACT.Exp, scale=-0.5).then_inc(rstd_x, 1)

        def high(act, n, dst, laps):
            act.wait_ge(raw_in[slot(n)], 16 * laps)
            nc.scalar.copy(dst, raw_tile(n)).then_inc(w_hi, 1)

        def silu_rows(b):
            for k in range(KT):
                last = nc.tensor.matmul(ps[:, b + k // 4, (k % 4) * P:(k % 4 + 1) * P],
                                        silu_c[:, k:k + 1].broadcast_to([P, P]), idn[:, :], start=True, stop=True)
            last.then_inc(silu_mm, 1)

        ADA_AT = lambda n: PROLOGUE_RAW + n
        NEXT_AT = PROLOGUE_RAW + ADA_TILES

        def laps_from(start, n):
            return sum(slot(i) == slot(n) for i in range(start, n + 1))

        with nc.Block() as block:
            @block.sync
            def _(sp):
                sp.dma_start(c_sb, c_cols).then_inc(const_in[0], 16)
                sp.dma_start(idn[:, :], ident).then_inc(const_in[1], 16)
                sp.dma_start(vec_m[:, :], mods_in[0]).then_inc(mods_in_sem, 16)
                def load_x(t):
                    sp.dma_start(yT[:, t, :], x[0, t * P:(t + 1) * P, :]).then_inc(x_in[t], 16)

                for t in range(4):
                    load_x(t)
                for n in range(ADA_TILES):
                    if n >= RING:
                        sp.wait_ge(ada_used, n - RING + 1)
                    load_tile(sp, ADA_AT(n), n)
                    if RING <= n + 1 < RING + 4:
                        load_x(n + 5 - RING)
                def wait(i):
                    if i < NEXT_AT + RING:
                        sp.wait_ge(ada_used, ADA_TILES - RING + i - NEXT_AT + 1)
                    else:
                        sp.wait_ge(w_lo_pool, i - NEXT_AT - RING + 1)
                load_next(sp, NEXT_AT, ADA_TILES, wait)
                sp.dma_start(raw_low[:, :, :], w_low[0].rearrange("p (k c) -> p k c", k=KT)).then_inc(low_in, 16)
                sp.dma_start(causal_sb[:, :], causal).then_inc(const_in[2], 16)
                sp.wait_ge(const_in[2], 16)
                sp.wait_ge(low_in, 16)
                for i in range(RING):
                    sp.wait_ge(raw_in[i], 16 * laps_from(PROLOGUE_RAW, NEXT_AT + FIRST_T + i))

            @block.gpsimd
            def _(pool):
                for t in range(4, NT):
                    pool.wait_ge(rstd_x, t + 1)
                    nc.gpsimd.tensor_scalar(yT[:, t, :], yT[:, t, :], rs8[:, t:t + 1], None, MULT)\
                        .then_inc(xn_pool, 1)
                for t in range(FIRST_T):
                    pool.wait_ge(w_hi, t + 1)
                    nc.gpsimd.tensor_tensor(wt_lo[:, t % 2], raw_tile(NEXT_AT + t), wt_hi[:, t % 2].bitcast(f32), SUB)\
                        .then_inc(w_lo_pool, 1)
                for k in range(KT):
                    pool.wait_ge(h_full, k + 1)
                    nc.gpsimd.tensor_tensor(act_lo[:, k, 6 * P:8 * P], h_tmp(3, k),
                                            act_hi[:, k, 6 * P:8 * P].bitcast(f32), SUB).then_inc(h_lo_pool, 1)

            @block.scalar
            def _(act):
                act.preload_act_table_set("natural_log_exp_and_others")
                act.wait_ge(const_in[0], 16)
                nc.scalar.activation(c_e, c_sb, ACT.Exp, scale=-1.0).then_inc(act_seq, 1)
                act.wait_ge(silu_mm, 1)
                nc.scalar.copy(silu_first[:, :], bank(0, 2)).then_inc(silu_ready, 1)
                for t in range(NT):
                    act.wait_ge(x_in[t], 16)
                    norm_x(act, t, yT[:, t, :], h_junk[:, :], t)
                for ms in (range(2), range(2, 4)):
                    for k in range(KT):
                        act.wait_ge(mods_ready, 2 * k + 2)
                        for m in ms:
                            act.wait_ge(xnT_done, m + 1)
                            h_high(m, 4 * (1 - m % 2), k)
                            if m == 3:
                                nc.scalar.activation(h_tmp(m, k), h_bank(0, k), ACT.Identity,
                                                     scale=h_scale[:, k:k + 1], bias=mod[:, 2 * k:2 * k + 1])\
                                    .then_inc(h_full, 1)
                    if 0 in ms:
                        for t in range(FIRST_T):
                            high(act, NEXT_AT + t, wt_hi[:, t % 2], laps_from(PROLOGUE_RAW, NEXT_AT + t))

            @block.vector
            def _(dve):
                nc.vector.memset(ones[:, :], 1.0).then_inc(dve_seq, 1)
                dve.wait_ge(act_seq, 1)
                nc.vector.tensor_scalar_add(c_e, c_e, 1.0).then_inc(act_seq, 1)
                dve.wait_ge(act_seq, 2)
                nc.vector.reciprocal(c_e, c_e).then_inc(act_seq, 1)
                dve.wait_ge(act_seq, 3)
                nc.vector.tensor_tensor(silu_c, c_sb, c_e, MULT).then_inc(act_seq, 1)

                def normalise(t):
                    dve.wait_ge(rstd_x, t + 1)
                    nc.vector.tensor_scalar(yT[:, t, :], yT[:, t, :], rs8[:, t:t + 1], None, MULT)\
                        .then_inc(xn_done, 1)

                for t in range(4):
                    normalise(t)
                dve.wait_ge(silu_ready, 1)
                dve.wait_ge(mods_in_sem, 16)
                done = 0
                for k in range(KT):
                    for n in (2 * k, 2 * k + 1):
                        dve.wait_ge(raw_in[slot(ADA_AT(n))], 16 * laps_from(PROLOGUE_RAW, ADA_AT(n)))
                        ada_tile((ADA_AT(n), n), silu_first)
                    dve.wait_ge(ada_used, 2 * k + 2)
                    mods(dve, k, k + 1, 2 * k)
                    for kk in ((k - 3, k - 2) if k % 2 and k > 2 else ()):
                        dve.wait_ge(h_hi, 2 * (k - 1))
                        for m in range(2):
                            h_low(dve, m, 4 * (1 - m), kk, done, h_tmp(m, kk))
                            done += 1
                for kk in (KT - 2, KT - 1):
                    dve.wait_ge(h_hi, 2 * KT)
                    for m in range(2):
                        h_low(dve, m, 4 * (1 - m), kk, done, h_tmp(m, kk))
                        done += 1
                for k in range(KT):
                    dve.wait_ge(h_hi, 2 * KT + 2 * (k // 2 * 2) + 3)
                    h_low(dve, 2, 4, k, done, h_tmp(2, k))
                    done += 1

            @block.tensor
            def _(pe):
                pe.wait_ge(const_in[1], 16)
                pe.wait_ge(act_seq, 4)
                silu_rows(0)
                for m in range(4):
                    if m < 2:
                        pe.wait_ge(xn_done, 2 * m + 2)
                    else:
                        pe.wait_ge(xn_pool, 2 * m - 2)
                    if m == 1:
                        pe.wait_ge(silu_ready, 1)
                    if m >= 2:
                        pe.wait_ge(h_lo, 4 * KT)
                    for k in range(KT):
                        last = h_transpose(m, 4 * (1 - m % 2), k)
                    last.then_inc(xnT_done, 1)
        nc.all_engine_barrier(sems_to_clear=range(sems[0].num, sems[-1].num + 1))

        TAB_POS = position(T_B(0, 2)) + 3
        GU_POS = 2

        with nc.Fori(0, DEPTH) as layer:
            with nc.Block() as block:
                @block.sync
                def _(sp):
                    per_layer = len(STREAM) + len(NEXT)
                    first = ADA_TILES + len(NEXT)
                    sp.dma_start(vec[:, :], vecs[bass.ds(layer, 1), :, :].rearrange("l p n -> (l p) n"))\
                        .then_inc(vec_in, 16)
                    sp.dma_start(w_gu, w_gate_up[bass.ds(layer * LOWRANK, LOWRANK), :]).then_inc(gu_in, 16)
                    for n, kind in enumerate(STREAM):
                        wait_used(sp, n - RING)
                        if kind == "ada":
                            with sp.If(layer < DEPTH - 1):
                                load_tile(sp, n, layer * per_layer + first + n)
                            with sp.Else():
                                sp.sem_inc(raw_in[slot(n)], 16)
                        else:
                            load_tile(sp, n, layer * per_layer + first + n)
                        if n == ADA_POS[0]:
                            with sp.If(layer < DEPTH - 1):
                                sp.dma_start(vec_m[:, :], mods_in[bass.ds(layer + 1, 1), :, :]
                                             .rearrange("l p n -> (l p) n")).then_inc(mods_in_sem, 16)
                            with sp.Else():
                                sp.sem_inc(mods_in_sem, 16)
                        if n == TAB_POS:
                            sp.wait_ge(unit_done, UNIT[("vb", NT - 1)] + 1)
                            sp.dma_start(cos_t[:, :], rope_cos).then_inc(tab_in, 16)
                            sp.dma_start(sin_t[:, :], rope_sin).then_inc(tab_in, 16)
                            sp.dma_start(cnt_t[:, :], log_count).then_inc(tab_in, 16)
                    sp.wait_ge(pt_done, pt_chunk(DIL_H, 0, 0))
                    sp.dma_start(x_t[:, 0, :], rows[bass.ds(2 * layer, 1), :].broadcast_to([P, D]))\
                        .then_inc(bias_in, 16)
                    sp.wait_ge(y_done, GLA_H + DIL_H)
                    sp.dma_start(gate_t[:, :], rows[bass.ds(2 * layer + 1, 1), :].broadcast_to([P, D]))\
                        .then_inc(post_in, 16)

                    def load_x(t):
                        tok = slice(t * P, (t + 1) * P)
                        with sp.If(layer < 1):
                            sp.dma_start(x_t[:, t % 2, :], x[0, tok, :]).then_inc(x_load[t % 2], 16)
                        with sp.Else():
                            sp.dma_start(x_t[:, t % 2, :], out[0, tok, :]).then_inc(x_load[t % 2], 16)

                    load_x(1)
                    sp.wait_ge(gate_ready, 2)
                    load_x(0)
                    for t in range(NT):
                        sp.wait_ge(x_new, t + 1)
                        sp.dma_start(out[0, t * P:(t + 1) * P, :], x_t[:, t % 2, :]).then_inc(x_store[t % 2], 16)
                        if t == 1:
                            with sp.If(layer < DEPTH - 1):
                                load_next(sp, len(STREAM), layer * per_layer + first + len(STREAM),
                                          lambda i: wait_used(sp, i - RING))
                                sp.dma_start(raw_low[:, :, :], w_low[bass.ds(layer + 1, 1), :, :]
                                             .rearrange("l p (k c) -> (l p) k c", k=KT)).then_inc(low_in, 16)
                                sp.wait_ge(low_in, 16)
                        if t + 2 < NT:
                            sp.wait_ge(x_store[t % 2], 16 * (t // 2 + 1))
                            with sp.If(layer < DEPTH - 1):
                                sp.wait_ge(xn_done, t + 1)
                            load_x(t + 2)
                    for b in range(2):
                        sp.wait_ge(x_store[b], 16 * (NT // 2))
                    with sp.If(layer < DEPTH - 1):
                        for i in range(RING):
                            sp.wait_ge(raw_in[i], 16 * lap(len(STREAM) + FIRST_T + i))

                @block.gpsimd
                def _(pool):
                    def low(n, dst, src_hi):
                        pool.wait_ge(w_hi, highs(n))
                        nc.gpsimd.tensor_tensor(dst, raw_tile(n), src_hi.bitcast(f32), SUB).then_inc(w_lo_pool, 1)

                    def low_cols(n, lo, hi, v):
                        if user(n) == "pool":
                            low(n, lo[:, :, v * P:(v + 1) * P], hi[:, :, v * P:(v + 1) * P])

                    for v in range(VT):
                        low_cols(VA0 + v, wv_lo, wv_hi, v)
                    for t in range(FIRST_T, len(T_TILES)):
                        if t == T_GLA:
                            for v in range(VT):
                                low_cols(VB0 + v, wv_lo, wv_hi, v)
                        low(position(t), wt_lo[:, t % 2], wt_hi[:, t % 2])
                    for h in range(POOL_Y):
                        pool.wait_ge(y_hi, h + 1)
                        nc.gpsimd.tensor_tensor(act_lo[:, h, :], yT[:, h, :], act_hi[:, h, :].bitcast(f32), SUB)\
                            .then_inc(y_lo_pool, 1)
                    for v in range(KT):
                        low_cols(WO0 + v, wo_lo, wo_hi, v)
                    with pool.If(layer < DEPTH - 1):
                        for t in range(FIRST_T):
                            low(len(STREAM) + t, wt_lo[:, t % 2], wt_hi[:, t % 2])

                @block.scalar
                def _(act):
                    def split(n, dst):
                        high(act, n, dst, lap(n))

                    def split_t(t):
                        if t < len(T_TILES):
                            act.wait_ge(unit_done, UNIT[(t - 2, 1)] + 1)
                            split(position(t), wt_hi[:, t % 2])

                    def z_abs_unit(head, key, tmp):
                        half = key[1]
                        act.wait_ge(unit_done, UNIT[key] + 1)
                        if head:
                            act.wait_ge(z_done, head)
                        nc.scalar.activation(tmp[:, half * HALF:(half + 1) * HALF], bank(UNIT[key] % 2), ACT.Abs)\
                            .then_inc(z_abs, 1)

                    def z_softplus(head, tmp):
                        act.wait_ge(z_abs, 2 * (head + 1))
                        nc.scalar.activation(tmp, tmp, ACT.Exp, scale=-1.0).then_inc(z_soft, 1)
                        act.wait_ge(z_soft, 2 * head + 1)
                        nc.scalar.activation(tmp, tmp, ACT.Ln, bias=1.0).then_inc(z_soft, 1)

                    def z_sigmoid(head, tmp):
                        act.wait_ge(z_arg, head + 1)
                        nc.scalar.activation(tmp, tmp, ACT.Exp).then_inc(z_sig, 1)

                    def norm_square(head, buf):
                        if head:
                            act.wait_ge(y_done, head)
                        if head < GLA_H:
                            act.wait_ge(o_evac, NT * (head // 2 + 1))
                            act.wait_ge(z_done, GLA_H)
                        else:
                            act.wait_ge(pv_evac, 4 * (head - GLA_H + 1))
                        nc.scalar.activation(buf, yT[:, head, :], ACT.Square).then_inc(sq_done, 1)

                    def norm_rs(head, buf, b, step=1):
                        act.wait_ge(norm_done, head + 1)
                        for half in range(2 if step > 1 else 1):
                            cols = slice(half * HALF, (half + 1) * HALF) if step > 1 else slice(0, S)
                            src = bank(b + step * half) if step > 1 else bank(b, 2)
                            last = nc.scalar.activation(buf[:, cols], src, ACT.Ln, scale=1.0 / DV, bias=EPS)
                        last.then_inc(ln_done, 1)
                        act.wait_ge(ln_done, head + 1)
                        nc.scalar.activation(buf, buf, ACT.Exp, scale=-0.5).then_inc(rs_done, 1)

                    for v in range(VT):
                        nc.scalar.copy(wv_hi[:, :, v * P:(v + 1) * P], raw_tile(VA0 + v)).then_inc(w_hi, 1)
                    nc.scalar.copy(wv_hi[:, :, GLA_H * DV:WV], raw_low[:, :, :]).then_inc(low_split, 1)
                    z_abs_unit(0, (T_Z[0], 0), sq_a)
                    z_abs_unit(0, (T_Z[0], 1), sq_a)
                    split_t(2)
                    z_softplus(0, sq_a)
                    z_sigmoid(0, sq_a)

                    def decay_soft(j):
                        act.wait_ge(dk_abs, 2 * j + 1)
                        nc.scalar.activation(k_e[j], k_e[j], ACT.Exp, scale=-1.0).then_inc(dk_soft, 1)
                        act.wait_ge(dk_soft, 2 * j + 1)
                        nc.scalar.activation(k_e[j], k_e[j], ACT.Ln, bias=1.0).then_inc(dk_soft, 1)

                    def decay_exps(j):
                        act.wait_ge(dk_cum, j + 1)
                        if j:
                            act.wait_ge(dk_exp, 4 * j)
                        nc.scalar.activation(q_e[j], cums[j], ACT.Exp).then_inc(dk_exp, 1)
                        nc.scalar.activation(k_e[j], cums[j], ACT.Exp, scale=-1.0).then_inc(dk_exp, 1)
                        act.wait_ge(dk_rest, j + 1)
                        nc.scalar.activation(k_dT[j], k_dT[j], ACT.Exp).then_inc(dk_exp, 1)
                        nc.scalar.activation(decay[j], cums[j][:, CHUNK - 1:S:CHUNK], ACT.Exp).then_inc(dk_exp, 1)

                    n_v = GLA_H * DV - V_COLS
                    for t in range(NT):
                        u = UNIT[("va", t, 1)]
                        act.wait_ge(unit_done, u + 1)
                        nc.scalar.copy(low_n[:, t, :], bank(u % 2)[:, n_v:V_COLS]).then_inc(act_seq, 1)
                        nc.scalar.copy(va[:, t, V_COLS:], bank(u % 2)[:, 0:n_v]).then_inc(unit_free[u % 2], 1)
                    for t in range(NT):
                        u = UNIT[("va", t, 0)]
                        act.wait_ge(unit_done, u + 1)
                        nc.scalar.copy(va[:, t, 0:V_COLS], bank(u % 2)[:, 0:V_COLS]).then_inc(unit_free[u % 2], 1)
                        if t == 0:
                            act.wait_ge(lowT_done, 1)
                            nc.scalar.copy(lrT, bank(2, 2)[0:LOWRANK, :]).then_inc(lowT_evac, 1)
                        if t in (2, 3):
                            decay_soft(t - 2)
                        if t in (4, 5):
                            decay_exps(t - 4)
                    z_abs_unit(1, (T_Z[1], 0), sq_a)
                    z_abs_unit(1, (T_Z[1], 1), sq_a)
                    split_t(T_Z[1] + 2)
                    z_softplus(1, sq_a)
                    z_sigmoid(1, sq_a)
                    split_t(T_QA[0] + 2)
                    split_t(T_KA[0] + 2)
                    for j in range(PAIRS):
                        if j:
                            z_abs_unit(2, gla_fill[0][4], sq_a)
                        for q in range(2):
                            act.wait_ge(kd_done, 2 * j + q + 1)
                            nc.scalar.copy(k_end[:, 4 * q:4 * q + 4, :].rearrange("p t k -> p (t k)"), bank(6 + q))\
                                .then_inc(kend_ready, 1)
                        for p in range(NT):
                            for n in completed(FILL[j], p):
                                key = gla_fill[j][n]
                                if j == 0 and key[1]:
                                    split_t(key[0] + 2)
                                if j:
                                    z_abs_unit(*z_fill[n], sq_a)
                                    if key[1]:
                                        z_softplus(z_fill[n][0], sq_a)
                            act.wait_ge(o_done, NT * j + p + 1)
                            nc.scalar.copy(yT[:, 2 * j:2 * j + 2, p * P:(p + 1) * P], ps[:, 6:8, 0:P])\
                                .then_inc(o_evac, 1)
                            if j and p == Z_ARG:
                                z_sigmoid(2, sq_a)
                            if j and VB_SPLIT <= p < VB_SPLIT + VT:
                                v = p - VB_SPLIT
                                split(VB0 + v, wv_hi[:, :, v * P:(v + 1) * P])
                    z_sigmoid(3, sq_a)
                    split_t(T_Z[2] + 2)
                    split_t(T_Z[3] + 2)
                    for t in range(NT):
                        u = UNIT[("vb", t)]
                        if t % 2 == 0:
                            norm_square(t // 2, sq_a)
                            norm_rs(t // 2, sq_a, 2)
                        act.wait_ge(unit_done, u + 1)
                        nc.scalar.copy(vb[:, t, :], bank(u % 2)).then_inc(unit_free[u % 2], 1)

                    def attend(h, i, unit_work):
                        if i < NT:
                            n = NT * h + i
                            act.wait_ge(s_masked, n + 1)
                            nc.scalar.activation(pr[:, i % 2, 0:(i + 1) * P], pr[:, i % 2, 0:(i + 1) * P], ACT.Exp,
                                                 scale=-1.0, bias=nmax[:, i % 2:i % 2 + 1],
                                                 accum_out=den[:, i % 2:i % 2 + 1]).then_inc(exp_done, 1)

                        def evacuate_pt(part, j0, j1):
                            q = i - 1
                            c = pt_chunk(h, q, part)
                            act.wait_ge(pt_done, c + 1)
                            if q % 2 == 0 and part == 0 and (h or q):
                                act.wait_ge(pv_done, 4 * h + q // 2)
                            nc.scalar.copy(pT[:, j0:j1, (q % 2) * P:(q % 2 + 1) * P],
                                           bank(6)[:, 0:(j1 - j0) * P].rearrange("p (j q) -> p j q", q=P))\
                                .then_inc(pt_evac, 1)
                        if 3 <= i and i % 2:
                            g = (i - 3) // 2
                            act.wait_ge(pv_done, 4 * h + g + 1)
                            if h == DIL_H - 1 and g == 0:
                                act.wait_ge(ada_used, ADA_TILES)
                            nc.scalar.copy(yT[:, GLA_H + h, 2 * P * g:2 * P * (g + 1)], bank(7)[:, 0:2 * P])\
                                .then_inc(pv_evac, 1)
                        if 1 <= i <= NT:
                            evacuate_pt(0, *pt_parts(i - 1)[0])
                        if 5 <= i <= NT:
                            evacuate_pt(1, *pt_parts(i - 1)[1])
                        unit_work()

                    def high_y(n):
                        act.wait_ge(unit_done, N_UNITS)
                        act.wait_ge(y_done, n + 1)
                        nc.scalar.copy(act_hi[:, n, :], yT[:, n, :]).then_inc(y_hi, 1)

                    for h in range(DIL_H + 1):
                        for i in range(NT + 2):
                            def unit_work(i=i, h=h):
                                for n in (completed(STEP_MM, i) if h < DIL_H else ()):
                                    t, half = dil_units(h)[n]
                                    if n == 4:
                                        wait_unit_evacuated(act, UNIT[(t - 1, 0)])
                                        wait_unit_evacuated(act, UNIT[(t - 1, 1)])
                                    if n >= 4:
                                        z_abs_unit(GLA_H + h, (t, half), r_tmp2)
                                    if n == 5:
                                        z_softplus(GLA_H + h, r_tmp2)
                                    if half:
                                        split_t(t + 2)
                                if i == 0 and h == 0:
                                    act.wait_ge(silu_mm, 1)
                                    nc.scalar.copy(silu_b, bank(2, 2)).then_inc(silu_ready, 1)
                                if i == 0 and h:
                                    z_sigmoid(GLA_H + h - 1, r_tmp2)
                                if i == 0 and h >= 2:
                                    norm_square(GLA_H + h - 2, sq_b[:, :])
                                if i == 1 and h >= 2:
                                    norm_rs(GLA_H + h - 2, sq_b[:, :], 3, 2)
                                if h == DIL_H and 1 <= i <= 7:
                                    high_y(i - 1)
                            if h:
                                attend(h - 1, i, unit_work)
                            else:
                                unit_work()
                    norm_square(GLA_H + DIL_H - 1, sq_last[:, :])
                    act.wait_ge(pv_done, 4 * DIL_H)
                    split(WO0, wo_hi[:, :, 0:P])
                    split(WO0 + 1, wo_hi[:, :, P:2 * P])
                    norm_rs(GLA_H + DIL_H - 1, sq_last[:, :], 4)
                    split(WO0 + 2, wo_hi[:, :, 2 * P:3 * P])
                    high_y(GLA_H + DIL_H - 1)
                    for v in range(3, KT):
                        split(WO0 + v, wo_hi[:, :, v * P:(v + 1) * P])

                    for t in range(NT):
                        act.wait_ge(yp_done, t + 1)
                        if t >= 2:
                            act.wait_ge(yp_free, t - 1)
                        if t == 0:
                            act.wait_ge(y_lo_pool, POOL_Y)
                            act.wait_ge(y_lo_dve, KT - POOL_Y)
                            act.wait_ge(y_hi, KT)
                        nc.scalar.activation(yT[:, t, :], bank(o_bank(t), 2), ACT.Square,
                                             accum_out=ss[:, t % 2:t % 2 + 1]).then_inc(sqy_done, 1)
                        act.wait_ge(sqy_done, t + 1)
                        nc.scalar.activation(lnt[:, t % 2:t % 2 + 1], ss[:, t % 2:t % 2 + 1], ACT.Ln, scale=1.0 / D,
                                             bias=EPS).then_inc(act_seq, 1)
                        act.wait_ge(act_seq, NT + t + 1)
                        nc.scalar.activation(rstd[:, t % 2:t % 2 + 1], lnt[:, t % 2:t % 2 + 1], ACT.Exp, scale=-0.5)\
                            .then_inc(rstd_y, 1)
                        with act.If(layer < DEPTH - 1):
                            act.wait_ge(x_new, t + 1)
                            norm_x(act, t, x_t[:, t % 2, :], yT[:, t, :], t)
                            if t == 1:
                                for v in range(FIRST_T):
                                    split(len(STREAM) + v, wt_hi[:, v])
                            for m in h_after(t):
                                act.wait_ge(mods_ready, 2)
                                act.wait_ge(xnT_done, m + 1)
                                for k in range(KT):
                                    h_high(m, 4, k)

                @block.vector
                def _(dve):
                    count = [0]

                    def link(ins):
                        count[0] += 1
                        ins.then_inc(dve_seq, 1)
                        dve.wait_ge(dve_seq, count[0])

                    V = nc.vector

                    def low(n, dst, src_hi):
                        dve.wait_ge(w_hi, highs(n))
                        V.tensor_tensor(dst, raw_tile(n), src_hi.bitcast(f32), SUB).then_inc(w_lo_dve, 1)

                    def low_cols(n, lo, hi, v):
                        if user(n) == "dve":
                            low(n, lo[:, :, v * P:(v + 1) * P], hi[:, :, v * P:(v + 1) * P])

                    def z_copy(head, key, dst):
                        u = UNIT[key]
                        cols = slice(key[1] * HALF, (key[1] + 1) * HALF)
                        if head in (2, 3):
                            dve.wait_ge(o_done, NT)
                        if head >= GLA_H + 2:
                            dve.wait_ge(y_done, head - 1)
                        dve.wait_ge(z_abs, 2 * head + key[1] + 1)
                        V.tensor_copy(dst[:, cols], bank(u % 2)).then_inc(unit_free[u % 2], 1)

                    def z_argument(head, key, dst, tmp):
                        dve.wait_ge(z_soft, 2 * (head + 1))
                        wait_unit_evacuated(dve, UNIT[key])
                        wait_unit_evacuated(dve, UNIT[key] - 1)
                        V.scalar_tensor_tensor(out=tmp, in0=dst, scalar=0.0, in1=tmp, op0=MIN, op1=SUB)\
                            .then_inc(z_arg, 1)

                    def z_gate(head, dst, tmp):
                        dve.wait_ge(z_sig, head + 1)
                        V.scalar_tensor_tensor(out=dst, in0=dst, scalar=g_head[:, head:head + 1], in1=tmp,
                                               op0=MULT, op1=MULT).then_inc(z_done, 1)

                    def finish_y(head, buf, z):
                        dve.wait_ge(rs_done, head + 1)
                        dve.wait_ge(z_done, head + 1)
                        link(V.tensor_tensor(yT[:, head, :], yT[:, head, :], buf, MULT))
                        V.tensor_tensor(yT[:, head, :], yT[:, head, :], z, MULT).then_inc(y_done, 1)

                    for v in range(VT):
                        low_cols(VA0 + v, wv_lo, wv_hi, v)
                    dve.wait_ge(low_split, 1)
                    V.tensor_tensor(wv_lo[:, :, GLA_H * DV:WV], raw_low[:, :, :],
                                    wv_hi[:, :, GLA_H * DV:WV].bitcast(f32), SUB).then_inc(low_split, 1)
                    dve.wait_ge(vec_in, 16)
                    z_copy(0, (T_Z[0], 0), za[0])
                    z_copy(0, (T_Z[0], 1), za[0])
                    z_argument(0, (T_Z[0], 1), za[0], sq_a)
                    z_gate(0, za[0], sq_a)
                    link(V.memset(yT[:, 5, 0:4 * P], 0.0))

                    def decay_start(j):
                        z = cums[j]
                        dve.wait_ge(dk_z, 4)
                        link(V.tensor_scalar(z, bank(4 + 2 * j, 2), b_gu_c[:, j:j + 1], None, ADD))
                        V.scalar_tensor_tensor(out=k_e[j], in0=z, scalar=-1.0, in1=z, op0=MULT, op1=MAX)\
                            .then_inc(dk_abs, 1)
                        V.tensor_scalar(k_dT[j], z, 0.0, 1.0 / 16.0, MIN, MULT).then_inc(dk_abs, 1)

                    def decay_cumulate(j):
                        dve.wait_ge(dk_soft, 2 * (j + 1))
                        dve.wait_ge(dk_abs, 2 * (j + 1))
                        link(V.scalar_tensor_tensor(out=k_e[j], in0=k_e[j], scalar=-1.0 / 16.0, in1=k_dT[j],
                                                    op0=MULT, op1=ADD))
                        for c in range(S // CHUNK):
                            cs = slice(c * CHUNK, (c + 1) * CHUNK)
                            last = V.tensor_tensor_scan(cums[j][:, cs], ones[:, 0:CHUNK], k_e[j][:, cs], 0.0, MULT,
                                                        ADD)
                        last.then_inc(dk_cum, 1)
                        dve.wait_ge(dk_cum, j + 1)
                        cum3 = cums[j].rearrange("p (c i) -> p c i", i=CHUNK)
                        V.tensor_tensor(k_dT[j].rearrange("p (c i) -> p c i", i=CHUNK),
                                        cum3[:, :, CHUNK - 1:CHUNK].broadcast_to([P, S // CHUNK, CHUNK]), cum3,
                                        SUB).then_inc(dk_rest, 1)

                    def q_half(j, half):
                        cols = slice(half * HALF, (half + 1) * HALF)
                        u = UNIT[(T_QA[j], half)]
                        dve.wait_ge(dk_exp, 4 * j + 1)
                        dve.wait_ge(unit_done, u + 1)
                        V.scalar_tensor_tensor(out=q_e[j][:, cols], in0=bank(u % 2), scalar=DK ** -0.5,
                                               in1=q_e[j][:, cols], op0=MULT, op1=MULT).then_inc(unit_free[u % 2], 1)

                    def k_half(j, half):
                        cols = slice(half * HALF, (half + 1) * HALF)
                        u = UNIT[(T_KA[j], half)]
                        dve.wait_ge(dk_exp, 4 * j + 4)
                        dve.wait_ge(unit_done, u + 1)
                        V.tensor_tensor(k_e[j][:, cols], bank(u % 2), k_e[j][:, cols], MULT).then_inc(dve_seq, 1)
                        count[0] += 1
                        V.tensor_tensor(k_dT[j][:, cols], bank(u % 2), k_dT[j][:, cols], MULT)\
                            .then_inc(unit_free[u % 2], 1)

                    for j in range(PAIRS):
                        decay_start(j)
                    for j in range(PAIRS):
                        decay_cumulate(j)
                    z_copy(1, (T_Z[1], 0), za[1])
                    z_copy(1, (T_Z[1], 1), za[1])
                    z_argument(1, (T_Z[1], 1), za[1], sq_a)
                    z_gate(1, za[1], sq_a)
                    q_half(0, 0)
                    q_half(0, 1)
                    k_half(0, 0)
                    k_half(0, 1)

                    for j in range(PAIRS):
                        if j:
                            z_copy(2, gla_fill[0][4], za[2])

                        def mask_and_states(p):
                            s = NT * j + p
                            dve.wait_ge(at_done, s + 1)
                            if s >= 2:
                                dve.wait_ge(o_done, s - 1)
                            V.copy_predicated(at_sb[:, p % 2, :, :],
                                              causal_sb[:, :].rearrange("p (a i) -> p a i", a=1)
                                              .broadcast_to([P, 2, P]),
                                              ps[:, 2:4, 0:P]).then_inc(at_masked, 1)
                            dve.wait_ge(cs_done, s + 1)
                            if p == 0 and j:
                                dve.wait_ge(o_done, NT * j)
                            for e in range(2):
                                c = 2 * p + e
                                if c == 2 * NT - 1:
                                    continue
                                new = state[:, (c + 1) % 6, :]
                                if c == 0:
                                    V.tensor_copy(new, bank(4)[:, 0:DV]).then_inc(state_done, 1)
                                else:
                                    dve.wait_ge(state_done, states(j, c))
                                    V.scalar_tensor_tensor(out=new, in0=state[:, c % 6, :], scalar=decay[j][:, c:c + 1],
                                                           in1=bank(4 + e)[:, 0:DV], op0=MULT, op1=ADD)\
                                        .then_inc(state_done, 1)

                        mask_and_states(0)
                        for p in range(NT):
                            if p + 1 < NT:
                                mask_and_states(p + 1)
                            if j and p == Z_ARG:
                                z_argument(2, gla_fill[1][0], za[2], sq_a)
                            if j and p == Z_ARG + 1:
                                z_gate(2, za[2], sq_a)
                            for n in completed(FILL[j], p):
                                if j:
                                    z_copy(*z_fill[n], za[z_fill[n][0]])
                                else:
                                    (q_half, k_half)[n // 2](1, n % 2)
                    z_argument(3, gla_fill[1][2], za[3], sq_a)
                    z_gate(3, za[3], sq_a)
                    for head in range(GLA_H):
                        finish_y(head, sq_a, za[head])

                    dve.wait_ge(tab_in, 48)
                    dve.wait_ge(y_done, GLA_H)

                    def rope(h, n):
                        kind, half = divmod(n, 2)
                        cols = slice(half * HALF, (half + 1) * HALF)
                        dst = qkT[:, 2 * (h % 2) + kind, cols]
                        u = UNIT[(T_B(h, kind), half)]
                        dve.wait_ge(unit_done, u + 1)
                        V.tensor_tensor(dst, bank(u % 2), cos_t[:, cols], MULT).then_inc(dve_seq, 1)
                        tmp = r_tmp[:, half, :]
                        if n >= 2:
                            wait_unit_evacuated(dve, u - 2)
                        elif h:
                            dve.wait_ge(z_done, GLA_H + h)
                        V.tensor_tensor(tmp[0:64, :], bank(u % 2)[64:128, :], sin_t[64:128, cols], MULT)\
                            .then_inc(dve_seq, 1)
                        V.tensor_tensor(tmp[64:128, :], bank(u % 2)[0:64, :], sin_t[0:64, cols], MULT)\
                            .then_inc(dve_seq, 1)
                        count[0] += 3
                        dve.wait_ge(dve_seq, count[0])
                        V.tensor_tensor(dst, dst, tmp, ADD).then_inc(unit_free[u % 2], 1)

                    def ada(n):
                        at_ = ADA_POS[n]
                        if n == 0:
                            dve.wait_ge(silu_ready, 1)
                            dve.wait_ge(mods_in_sem, 16)
                        dve.wait_ge(raw_in[slot(at_)], 16 * lap(at_))
                        ada_tile((at_, n), silu_b)

                    def low_y(n):
                        dve.wait_ge(y_hi, n + 1)
                        V.tensor_tensor(act_lo[:, n, :], yT[:, n, :], act_hi[:, n, :].bitcast(f32), SUB)\
                            .then_inc(y_lo_dve, 1)

                    n_ada = 0
                    for h in range(DIL_H + 1):
                        for i in range(NT + 2):
                            if h and i < NT:
                                n = NT * (h - 1) + i
                                w = (i + 1) * P
                                dve.wait_ge(s_done, n + 1)
                                if n >= 2:
                                    last = pt_chunk(h - 1, i - 2, 1 if i >= 6 else 0) if i >= 2 else \
                                        pt_chunk(h - 2, NT + i - 2, 1)
                                    dve.wait_ge(pt_done, last + 1)
                                V.tensor_tensor_reduce(out=pr[:, i % 2, 0:w], in0=bank(2 + 2 * (i % 2), 2)[:, 0:w],
                                                       in1=cnt_t[:, S - w:S], scale=-SCORE_SCALE, scalar=-NEG,
                                                       op0=ADD, op1=MIN, accum_out=nmax[:, i % 2:i % 2 + 1])\
                                    .then_inc(s_masked, 1)
                                dve.wait_ge(exp_done, n + 1)
                                link(V.reciprocal(rden[:, i % 2:i % 2 + 1], den[:, i % 2:i % 2 + 1]))
                                V.tensor_scalar(pr[:, i % 2, 0:w], pr[:, i % 2, 0:w], rden[:, i % 2:i % 2 + 1], None,
                                                MULT).then_inc(p_ready, 1)
                            for n in (completed(STEP_MM, i) if h < DIL_H else ()):
                                z = zb_1 if h % 2 else zb_0
                                if n < 4:
                                    rope(h, n)
                                else:
                                    z_copy(GLA_H + h, dil_units(h)[n], z)
                                if n == 5:
                                    z_argument(GLA_H + h, dil_units(h)[n], z[:, :], r_tmp2)
                            if i == 0 and h:
                                z_gate(GLA_H + h - 1, (zb_0 if h % 2 else zb_1)[:, :], r_tmp2)
                            if i == 2 and h >= 2:
                                head = GLA_H + h - 2
                                finish_y(head, sq_b[:, :], (zb_1 if head % 2 else zb_0)[:, :])
                            if (h, i) in ADA_STEPS:
                                ada(n_ada)
                                n_ada += 1
                                if n_ada == ADA_TILES:
                                    dve.wait_ge(ada_used, ADA_TILES)
                                    mods(dve, 0, KT, 0)
                            if h == DIL_H and i + 1 - 3 in range(POOL_Y, 7):
                                low_y(i + 1 - 3)
                    for n in range(max(POOL_Y, NT + 2 - 2), 7):
                        low_y(n)
                    low_cols(WO0 + 1, wo_lo, wo_hi, 1)
                    finish_y(GLA_H + DIL_H - 1, sq_last[:, :], zb_1[:, :])
                    low_y(7)
                    for v in range(3, KT):
                        low_cols(WO0 + v, wo_lo, wo_hi, v)
                    dve.wait_ge(gate_used, GATE_TILES)
                    dve.wait_ge(bias_in, 16)
                    V.tensor_tensor(x_t[:, 0, :], bank(0, 2), x_t[:, 0, :], ADD).then_inc(gate_ready, 1)
                    dve.wait_ge(gate_ready, 1)
                    dve.wait_ge(post_in, 16)
                    V.tensor_tensor(gate_t[:, :], gate_t[:, :], x_t[:, 0, :], MULT).then_inc(gate_ready, 1)
                    dve.wait_ge(gate_ready, 2)
                    for t in range(NT):
                        dve.wait_ge(rstd_y, t + 1)
                        V.scalar_tensor_tensor(out=yT[:, t, :], in0=bank(o_bank(t), 2),
                                               scalar=rstd[:, t % 2:t % 2 + 1],
                                               in1=gate_t[:, :], op0=MULT, op1=MULT).then_inc(yp_free, 1)
                        dve.wait_ge(yp_free, t + 1)
                        dve.wait_ge(x_load[t % 2], 16 * (t // 2 + 1))
                        V.tensor_tensor(x_t[:, t % 2, :], x_t[:, t % 2, :], yT[:, t, :], ADD).then_inc(x_new, 1)
                        with dve.If(layer < DEPTH - 1):
                            dve.wait_ge(rstd_x, t + 1)
                            V.tensor_scalar(yT[:, t, :], x_t[:, t % 2, :], rs8[:, t:t + 1], None, MULT)\
                                .then_inc(xn_done, 1)
                            for m in h_after(t):
                                for k in range(0, KT, 2):
                                    dve.wait_ge(h_hi, KT * m + k + 2)
                                    for kk in (k, k + 1):
                                        h_low(dve, m, 4, kk, KT * m + kk, h_tmp(m, kk))

                @block.tensor
                def _(pe):
                    mm = nc.tensor.matmul
                    parts = [(0, 0), (0, 1), (1, 0)]

                    def unit_mm(key, m):
                        u = UNIT[key]
                        k, part = divmod(m, 3)
                        s, v = parts[part]
                        if m == 0:
                            if u >= 2:
                                wait_unit_evacuated(pe, u - 2)
                        dst = bank(u % 2)
                        if key[0] == "va":
                            if m == 0 and key[1:] == (0, 1):
                                for n in range(VA0, 0):
                                    wait_used(pe, n)
                                pe.wait_ge(low_split, 2)
                            tok = slice(key[1] * P, (key[1] + 1) * P)
                            cols = slice(key[2] * V_COLS, (key[2] + 1) * V_COLS)
                            dst = dst[:, 0:V_COLS]
                            w, a = (wv_hi, wv_lo)[v][:, k, cols], (act_hi, act_lo)[s][:, k, tok]
                            last = mm(dst, a, w, start=(m == 0), stop=(m == MM - 1))
                        elif key[0] == "vb":
                            if m == 0 and key[1] == 0:
                                for n in range(VB0, VB0 + VT):
                                    wait_used(pe, n)
                            tok = slice(key[1] * P, (key[1] + 1) * P)
                            w, a = (wv_hi, wv_lo)[v][:, k, 0:VT * P], (act_hi, act_lo)[s][:, k, tok]
                            last = mm(dst, a, w, start=(m == 0), stop=(m == MM - 1))
                        else:
                            t, half = key
                            if m == 0 and half == 0 and t >= FIRST_T:
                                wait_used(pe, position(t))
                            w = (wt_hi, wt_lo)[s][:, t % 2, k, :]
                            a = (act_hi, act_lo)[v][:, k, half * HALF:(half + 1) * HALF]
                            last = mm(dst, w, a, start=(m == 0), stop=(m == MM - 1))
                        if m == MM - 1:
                            last.then_inc(unit_done, 1)

                    def unit(key):
                        for m in range(MM):
                            unit_mm(key, m)

                    def fill(keys, budget, i):
                        for m in range(sum(budget[:i]), sum(budget[:i + 1])):
                            unit_mm(keys[m // MM], m % MM)

                    def norm(head, buf, b, step=1):
                        pe.wait_ge(sq_done, head + 1)
                        if head:
                            pe.wait_ge(ln_done, head)
                        for half in range(2):
                            last = mm(bank(b + step * half), ones[:, :], buf[:, half * HALF:(half + 1) * HALF], start=True,
                                      stop=True)
                        last.then_inc(norm_done, 1)

                    def gate_mm(m):
                        n, k = divmod(m, KT)
                        at_ = GATE_POS[n]
                        if m == 0:
                            wait_unit_evacuated(pe, N_UNITS - 2)
                            wait_unit_evacuated(pe, N_UNITS - 1)
                        if k == 0:
                            pe.wait_ge(raw_in[slot(at_)], 16 * lap(at_))
                        last = mm(bank(n // 4)[:, (n % 4) * P:(n % 4 + 1) * P],
                                  silu_c[:, k:k + 1].broadcast_to([P, P]), raw[:, slot(at_), k, :],
                                  start=(k == 0), stop=(k == KT - 1))
                        if k == KT - 1:
                            last.then_inc(gate_used, 1)

                    unit((T_Z[0], 0))
                    unit((T_Z[0], 1))
                    for t in range(NT):
                        unit(("va", t, 1))
                    unit(("va", 0, 0))
                    pe.wait_ge(act_seq, NT)
                    for t in range(NT):
                        last = nc.tensor.transpose(bank(2 + t // 4)[0:LOWRANK, (t % 4) * P:(t % 4 + 1) * P],
                                                   low_n[:, t, :], idn[:, :])
                    last.then_inc(lowT_done, 1)
                    unit(("va", 1, 0))
                    pe.wait_ge(lowT_evac, 1)
                    pe.wait_ge(gu_in, 16)
                    for j in range(PAIRS):
                        for half in range(2):
                            mm(bank(4 + 2 * j + half), w_gu[:, j * P:(j + 1) * P],
                               lrT[:, half * HALF:(half + 1) * HALF], start=True, stop=True).then_inc(dk_z, 1)
                    for t in range(2, NT):
                        unit(("va", t, 0))
                    for key in [(t, half) for t in (T_Z[1], T_QA[0], T_KA[0]) for half in range(2)]:
                        unit(key)

                    for j in range(PAIRS):
                        if j:
                            for m in range(MM // 2):
                                unit_mm(gla_fill[0][4], m)
                            pe.wait_ge(o_evac, NT * j)
                        else:
                            pe.wait_ge(dk_abs, 4)
                        wait_unit_evacuated(pe, UNIT[(T_KA[j], 0)])
                        wait_unit_evacuated(pe, UNIT[(T_KA[j], 1)])
                        for q in range(2):
                            for t in range(4):
                                last = nc.tensor.transpose(bank(6 + q)[:, t * P:(t + 1) * P],
                                                           k_dT[j][:, (4 * q + t) * P:(4 * q + t + 1) * P],
                                                           idn[:, :])
                            last.then_inc(kd_done, 1)
                        if j:
                            for m in range(MM // 2, MM):
                                unit_mm(gla_fill[0][4], m)
                        pe.wait_ge(kend_ready, 2 * (j + 1))

                        def scores_and_chunk_states(p):
                            s = NT * j + p
                            tok = slice(p * P, (p + 1) * P)
                            if s:
                                pe.wait_ge(at_masked, s)
                            for e in range(2):
                                rows_ = slice(e * DK, (e + 1) * DK)
                                last = mm(bank(2 + e)[:, 0:P], k_e[j][rows_, tok], q_e[j][rows_, tok], start=True, stop=True)
                            last.then_inc(at_done, 1)
                            if s:
                                pe.wait_ge(state_done, states(j, 2 * p))
                            for c in range(2):
                                in_chunk = slice(c * CHUNK, (c + 1) * CHUNK)
                                for e in range(2):
                                    if p == NT - 1 and c == 1:
                                        continue
                                    g = 2 * j + e
                                    last = mm(bank(4 + c)[e * DK:(e + 1) * DK, 0:DV],
                                              k_end[in_chunk, p, e * DK:(e + 1) * DK],
                                              va[in_chunk, p, g * DV:(g + 1) * DV], start=True, stop=True)
                            last.then_inc(cs_done, 1)

                        def outputs(p):
                            s = NT * j + p
                            pe.wait_ge(at_masked, s + 1)
                            pe.wait_ge(state_done, states(j, 2 * p + 1))
                            if s:
                                pe.wait_ge(o_evac, s)
                            for e in range(2):
                                g = 2 * j + e
                                rows_ = slice(e * DK, (e + 1) * DK)
                                mm(bank(6 + e)[:, 0:P], va[:, p, g * DV:(g + 1) * DV], at_sb[:, p % 2, e, :],
                                   start=True, stop=False)
                                for c in (2 * p, 2 * p + 1):
                                    if c:
                                        i0 = (c % 2) * CHUNK
                                        last = mm(bank(6 + e)[:, i0:i0 + CHUNK], state[rows_, c % 6, :],
                                                  q_e[j][rows_, c * CHUNK:(c + 1) * CHUNK], start=False,
                                                  stop=(c == 2 * p + 1))
                            last.then_inc(o_done, 1)

                        scores_and_chunk_states(0)
                        for p in range(NT):
                            if p + 1 < NT:
                                scores_and_chunk_states(p + 1)
                            fill(gla_fill[j], FILL[j], p)
                            outputs(p)

                    for t in range(NT):
                        unit(("vb", t))
                        if t % 2 == 0:
                            pe.wait_ge(at_masked, NT * PAIRS)
                            norm(t // 2, sq_a, 2)

                    def attend(h, i, unit_work):
                        q_t, k_t = qkT[:, 2 * (h % 2), :], qkT[:, 2 * (h % 2) + 1, :]
                        if i < NT:
                            n = NT * h + i
                            b = 2 + 2 * (i % 2)
                            if n >= 2:
                                pe.wait_ge(s_masked, n - 1)
                            if i == 4:
                                pe.wait_ge(ln_done, GLA_H + h)
                            if n == 0:
                                pe.wait_ge(silu_ready, 1)
                                pe.wait_ge(state_done, states(PAIRS, 0))
                            for half in range(-(-(i + 1) // 4)):
                                w = min((i + 1) * P - half * HALF, HALF)
                                last = mm(bank(b + half)[:, 0:w], q_t[:, i * P:(i + 1) * P],
                                          k_t[:, half * HALF:half * HALF + w], start=True, stop=True)
                            last.then_inc(s_done, 1)
                        if i == NT + 1:
                            unit_work()
                        if i >= 3 and i % 2:
                            g = (i - 3) // 2
                            pe.wait_ge(pt_evac, pt_chunk(h, 2 * g + 1, 1 if g >= 2 else 0) + 1)
                            if 4 * h + g:
                                pe.wait_ge(pv_evac, 4 * h + g)
                            for j in range(2 * g + 2):
                                c0 = P if j == 2 * g + 1 else 0
                                last = mm(bank(7)[:, c0:2 * P], vb[:, j, h * HD:(h + 1) * HD], pT[:, j, c0:2 * P],
                                          start=(j == 0), stop=(j == 2 * g + 1))
                            last.then_inc(pv_done, 1)

                        def transpose_p(part, j0, j1):
                            q = i - 1
                            c = pt_chunk(h, q, part)
                            pe.wait_ge(p_ready, NT * h + q + 1)
                            if c:
                                pe.wait_ge(pt_evac, c)
                            else:
                                pe.wait_ge(o_evac, NT * PAIRS)
                            for j in range(j0, j1):
                                last = nc.tensor.transpose(bank(6)[:, (j - j0) * P:(j - j0 + 1) * P],
                                                           pr[:, q % 2, j * P:(j + 1) * P], idn[:, :])
                            last.then_inc(pt_done, 1)
                        if 1 <= i <= NT:
                            transpose_p(0, *pt_parts(i - 1)[0])
                        if i <= NT:
                            unit_work()
                        if 5 <= i <= NT:
                            transpose_p(1, *pt_parts(i - 1)[1])

                    for h in range(DIL_H + 1):
                        if h:
                            for kind in range(2):
                                for half in range(2):
                                    wait_unit_evacuated(pe, UNIT[(T_B(h - 1, kind), half)])
                        for i in range(NT + 2):
                            def unit_work(i=i, h=h):
                                if h < DIL_H:
                                    fill(dil_units(h), STEP_MM, i)
                                else:
                                    for m in range(sum(GATE_MM[:i]), sum(GATE_MM[:i + 1])):
                                        gate_mm(m)
                                if i == 0 and h == 0:
                                    pe.wait_ge(ln_done, GLA_H)
                                    pe.wait_ge(dk_exp, 4 * PAIRS)
                                    silu_rows(2)
                                if i == 1 and h >= 2:
                                    pe.wait_ge(s_masked, NT * (h - 1))
                                    norm(GLA_H + h - 2, sq_b, 3, 2)
                            if h:
                                attend(h - 1, i, unit_work)
                            else:
                                unit_work()
                    pe.wait_ge(s_masked, NT * DIL_H)
                    norm(GLA_H + DIL_H - 1, sq_last, 4)
                    for m in range(sum(GATE_MM), GATE_TILES * KT):
                        gate_mm(m)

                    def out_mm(t, half, k):
                        tok, cols = slice(t * P, (t + 1) * P), slice(half * HALF, (half + 1) * HALF)
                        for part in range(3):
                            s, v = parts[part]
                            last = mm(bank(o_bank(t) + half), (act_hi, act_lo)[s][:, k, tok],
                                      (wo_hi, wo_lo)[v][:, k, cols], start=(k == 0 and part == 0),
                                      stop=(k == KT - 1 and part == 2))
                        return last

                    pe.wait_ge(y_lo_pool, POOL_Y)
                    pe.wait_ge(y_lo_dve, KT - 1 - POOL_Y)
                    for half in range(2):
                        for v in range(4 * half, 4 * half + 4):
                            wait_used(pe, WO0 + v)
                        for t in range(2):
                            if t:
                                pe.wait_ge(gate_ready, 1)
                            for k in range(KT - 1):
                                out_mm(t, half, k)
                    for t in range(NT):
                        if t == 0:
                            pe.wait_ge(y_lo_dve, KT - POOL_Y)
                        if t == 3:
                            pe.wait_ge(yp_free, 2)
                        if t >= 4:
                            pe.wait_ge(yp_free, t - 1)
                        for half in range(2):
                            for k in range(KT - 1 if t < 2 else 0, KT):
                                last = out_mm(t, half, k)
                        last.then_inc(yp_done, 1)
                        with pe.If(layer < DEPTH - 1):
                            for m in h_after(t):
                                pe.wait_ge(xn_done, 2 * m + 2)
                                pe.wait_ge(ln_done, GLA_H + DIL_H)
                                pe.wait_ge(pv_evac, 4 * DIL_H)
                                if m:
                                    pe.wait_ge(h_lo, 2 * KT * m)
                                else:
                                    pe.wait_ge(yp_free, 3)
                                for k in range(KT):
                                    last = h_transpose(m, 4, k)
                                last.then_inc(xnT_done, 1)
            nc.all_engine_barrier(sems_to_clear=range(sems[0].num, sems[-1].num + 1))


def kernel(**inputs):
    import concourse.bacc as bacc
    from concourse.bass_utils import run_bass_kernel_spmd as run

    def arr(name):
        return np.asarray(inputs[name])

    def cols(v):
        return v.reshape(-1, P).T

    w_ada, w_in, w_out = arr("w_ada"), arr("w_in"), arr("w_out")
    q0, k0, v0 = 0, GLA_H * DK, 2 * GLA_H * DK
    z0 = v0 + GLA_H * DV
    lr0 = z0 + GLA_H * DV
    b0 = lr0 + LOWRANK
    wb = DIL_H * HD

    def tile(w, layer, c):
        return w[layer, :, c:c + P].reshape(KT, P, P).transpose(1, 0, 2).reshape(P, KT * P)

    def ada_tiles(layer):
        return [w_ada[layer, :, c + k * P:c + (k + 1) * P].T for k in range(KT) for c in (0, D)]

    def t_columns():
        gla = [z0, z0 + P, q0, k0, q0 + P, k0 + P, z0 + 2 * P, z0 + 3 * P]
        return gla + [b0 + n * wb + h * P for h in range(DIL_H) for n in (0, 1, 3)]

    def first_tiles(layer):
        return [tile(w_in, layer, c) for c in t_columns()[:FIRST_T] + [v0 + v * P for v in range(VT)]]

    def stream(layer):
        after = min(layer + 1, DEPTH - 1)
        kinds = {"t": [tile(w_in, layer, c) for c in t_columns()][FIRST_T:],
                 "vb": [tile(w_in, layer, b0 + 2 * wb + v * P) for v in range(VT)],
                 "ada": ada_tiles(after),
                 "gate": [tile(w_ada, layer, 2 * D + n * P) for n in range(GATE_TILES)],
                 "wo": [tile(w_out, layer, n * P) for n in range(KT)]}
        return [kinds[kind].pop(0) for kind in STREAM] + first_tiles(after)

    def turns(a):
        return a.reshape(2, KT, P).transpose(1, 0, 2).reshape(2 * KT, P).T

    b_ada, g_pre, b_gu, g_gla, g_dil, g_post = (arr(n) for n in ("b_ada", "g_pre", "b_gate_up", "g_gla", "g_dil",
                                                                 "g_post"))
    inv = (10000.0 ** (-np.arange(0, HD, 2, dtype=np.float32) / HD)).astype(np.float32)
    ang = inv[:, None] * np.arange(S, dtype=np.float32)[None, :]
    cos, sin = np.cos(ang).astype(np.float32), np.sin(ang).astype(np.float32)
    dist = np.arange(P)[:, None] + (S - P) - np.arange(S)[None, :]
    times = sum(((dist >= 0) & (dist <= w) & (dist % d == 0)).astype(np.int64)
                for w, d in ((128, 1), (512, 4), (2048, 16)))
    with np.errstate(divide="ignore"):
        cnt = np.where(times > 0, np.log(np.maximum(times, 1)) / SCORE_SCALE, NEG).astype(np.float32)
    j, i = np.arange(P)[:, None], np.arange(P)[None, :]
    with_next = list(range(DEPTH)) + [DEPTH - 1]
    data = {
        "x": arr("x"),
        "tiles": np.stack(ada_tiles(0) + first_tiles(0) + [t for layer in range(DEPTH) for t in stream(layer)]),
        "w_low": np.stack([w_in[n, :, lr0:b0].reshape(KT, P, LOWRANK).transpose(1, 0, 2).reshape(P, KT * LOWRANK)
                           for n in with_next]),
        "vecs": np.stack([np.concatenate([cols(b_gu[n]), cols(g_gla[n]), cols(g_dil[n])], axis=1)
                          for n in range(DEPTH)]),
        "mods_in": np.stack([np.concatenate([turns(b_ada[n, :2 * D]), cols(g_pre[n])], axis=1)
                             for n in with_next]),
        "rows": np.stack([r for l in range(DEPTH) for r in (b_ada[l, 2 * D:], g_post[l])]),
        "w_gate_up": arr("w_gate_up").reshape(DEPTH * LOWRANK, GLA_H * DK),
        "c_cols": cols(arr("c")[0]),
        "rope_cos": np.concatenate([cos, cos]),
        "rope_sin": np.concatenate([sin, -sin]),
        "log_count": cnt,
        "ident": np.eye(P, dtype=np.float32),
        "causal": ((j <= i) & (j // CHUNK == i // CHUNK)).astype(np.int32),
    }
    data = {k: np.ascontiguousarray(v) for k, v in data.items()}
    nc = bacc.Bacc("TRN2", target_bir_lowering=False, num_devices=1)
    aps = {k: nc.dram_tensor(f"{k}_dram", v.shape, mybir.dt.from_np(v.dtype), kind="ExternalInput").ap()
           for k, v in data.items()}
    out = nc.dram_tensor("out_dram", (1, S, D), mybir.dt.float32, kind="ExternalOutput").ap()
    hybrid_trunk(nc, out=out, **aps)
    r = run(nc, [{f"{k}_dram": v for k, v in data.items()}], core_ids=[0])
    return r.results[0]["out_dram"]
```

```python
import numpy as np
import concourse.bass as bass
from concourse import mybir
from contextlib import ExitStack

P = 128
D = 1024
S = 1024
DEPTH = 2
KT = D // P
NT = S // P
HALF = S // 2
GLA_H, DK, DV, LOWRANK = 4, 64, 128, 16
CHUNK = 64
PAIRS = GLA_H // 2
DIL_H, HD = 4, 128
EPS = 1e-6
SCORE_SCALE = HD ** -0.5
ADA_TILES = 2 * D // P
GATE_TILES = D // P
VT = GLA_H * DV // P
NEG = -1e30

T_TILES = (["z0", "z1", "qa0", "ka0", "qa1", "ka1", "z2", "z3"]
           + [f"{n}{h}" for h in range(DIL_H) for n in ("qb", "kb", "zb")])
T_GLA = 8
FIRST_T = 2
NEXT = ["t"] * FIRST_T + ["va"] * VT
STREAM = (["t"] * (T_GLA - FIRST_T) + ["vb"] * VT + ["t"] * 3
          + ["t", "mod", "t", "mod", "t"] + ["mod"] * 6
          + ["t", "mod", "t", "mod", "t"] + ["mod"] * 6
          + ["t", "mod", "t", "mod", "t"] + ["mod"] * 6 + ["wo"] * KT)
MOD = ["gate"] * GATE_TILES + ["ada"] * ADA_TILES
STREAM = [MOD[STREAM[:n].count("mod")] if kind == "mod" else kind for n, kind in enumerate(STREAM)]
RING = 4
assert VT == RING and (len(STREAM) + FIRST_T) % RING == 0 and FIRST_T < RING
VA0, VB0, WO0 = -VT, T_GLA - FIRST_T, len(STREAM) - KT


def positions(kind):
    return [n for n, k in enumerate(STREAM) if k == kind]


MOD_POS = positions("gate") + positions("ada")


def position(t):
    return positions("t")[t - FIRST_T]


def slot(n):
    return n % RING


def lap(n):
    return n // RING + 1


def va_column(n):
    return (n + VT // 2) % VT


def user(n):
    kind = "va" if n < 0 else (STREAM + NEXT)[n]
    if kind in ("gate", "ada"):
        return kind
    if kind == "va":
        return "pool" if n == VA0 + 2 else "dve"
    if kind == "wo":
        return "pool" if n - WO0 in (0, 1, 4, 6) else "dve"
    return "pool"


def used(n):
    return sum(user(i) == user(n) for i in range(VA0, n + 1))


V_COLS = (GLA_H * DV + LOWRANK) // 2


def units():
    order = [(0, half) for half in range(2)]
    order += [("va", t, part) for part in (1, 0) for t in range(NT)]
    order += [(t, half) for t in range(1, T_GLA) for half in range(2)]
    order += [("vb", t) for t in range(NT)]
    order += [(t, half) for t in range(T_GLA, len(T_TILES)) for half in range(2)]
    return {key: n for n, key in enumerate(order)}


UNIT = units()
N_UNITS = len(UNIT)
PARTS = [(0, 0), (0, 1), (1, 0)]
MM = 3 * KT
STEP_MM = [[18, 12, 12, 14, 16, 18, 16, 14, 12, 12]] * 3 + [[14, 12, 6, 6, 8, 10, 12, 12, 10, 6],
                                                            [14, 10, 8, 8, 8, 0, 0, 0, 0, 0]]
FILL = [9] * NT


def slot_units(h):
    return [(h, n) for n in range(6 if h < DIL_H - 1 else 4)] if h < DIL_H else [(h - 1, 4), (h - 1, 5)]


assert all(sum(STEP_MM[h]) == len(slot_units(h)) * MM for h in range(DIL_H + 1))


def completed_step(budget, n):
    return next(i for i in range(len(budget)) if sum(budget[:i + 1]) >= (n + 1) * MM)


NORM_STEPS = [1, 3, 5, 7]
MOD_STEPS = [(slot_, step) for slot_ in range(1, DIL_H) for step in (1, 2, 3, 4, 5, 6, 7, 7)]
assert len(MOD_STEPS) == len(MOD)
Y_STEPS_ACT = {5: [0], 6: [1, 2], 7: [3]}
Y_STEPS_DVE = {7: [4], 8: [5, 6]}
WO_STEPS = {1: [0], 2: [1], 8: [2]}
POOL_Y = 4


def h_after(t):
    return {3: [0], 5: [1], 6: [2], 7: [3]}.get(t, [])


def o_bank(t):
    return {0: 2, 1: 0, 2: 4}.get(t, 2 if t % 2 else 0)


def units_done(u):
    return u


def completed(budget, i):
    return range(sum(budget[:i]) // MM, sum(budget[:i + 1]) // MM)


def hybrid_trunk(nc, x, tiles, w_low, vecs, mods_in, w_gate_up, c_cols, rope_cos, rope_sin, log_count, ident, causal, out):
    f32, f32r, i32 = mybir.dt.float32, mybir.dt.float32r, mybir.dt.int32
    ACT, ALU = mybir.ActivationFunctionType, mybir.AluOpType
    MULT, ADD, SUB, MAX, MIN = ALU.mult, ALU.add, ALU.subtract, ALU.max, ALU.min

    ctx = ExitStack()
    with ctx:
        def sb(name, shape, dt=f32):
            return ctx.enter_context(nc.sbuf_tensor(name, shape, dt))

        KB = 1024
        arena_at = -(-nc.sbuf_base // 32) * 32
        sb("arena", [P, 77 * KB // 4])

        def at(name, kb, shape, dt=f32):
            return nc.alloc_sbuf_tensor_at(name, shape, dt, offset=arena_at + int(kb * KB))

        act_hi = sb("act_hi", [P, KT, S], f32r)
        act_lo = sb("act_lo", [P, KT, S], f32r)
        yT = sb("yT", [P, GLA_H + DIL_H, S])
        wt_hi = sb("wt_hi", [P, 2, KT, P], f32r)
        wt_lo = sb("wt_lo", [P, 2, KT, P], f32r)
        raw = sb("raw", [P, RING, KT, P])
        raw_low = sb("raw_low", [P, KT, LOWRANK])
        idn = sb("idn", [P, P])
        ones = sb("ones", [P, P])
        ones_r = sb("ones_r", [P, 1], f32r)
        causal_sb = sb("causal_sb", [P, P], i32)
        vec = sb("vec", [P, PAIRS + GLA_H + DIL_H + 2 * KT])
        b_gu_c, g_head = vec[:, 0:PAIRS], vec[:, PAIRS:PAIRS + GLA_H + DIL_H]
        b_gate_c, g_post_c = vec[:, PAIRS + GLA_H + DIL_H:PAIRS + GLA_H + DIL_H + KT], vec[:, PAIRS + GLA_H + DIL_H + KT:]
        vec_m = sb("vec_m", [P, ADA_TILES + KT])
        b_ada_c, g_pre_c = vec_m[:, 0:ADA_TILES], vec_m[:, ADA_TILES:]
        small = sb("small", [P, 136])
        c_sb, c_e, silu_c = small[:, 0:8], small[:, 8:16], small[:, 16:24]
        mod, h_scale = small[:, 24:40], small[:, 40:48]
        ss, rstd = small[:, 48:50], small[:, 50:52]
        ss2, rstd2 = small[:, 52:54], small[:, 54:56]
        decay = [small[:, 56:72], small[:, 112:128]]
        nmax, den, rden = small[:, 72:74], small[:, 74:76], small[:, 76:78]
        lnt, lnt2 = small[:, 78:80], small[:, 80:82]
        gate_c = small[:, 128:136]
        ss8, ln8, rs8 = small[:, 84:92], small[:, 92:100], small[:, 100:108]


        silu_first = at("silu_first", 0, [P, D])
        h_junk = at("h_junk", 4, [P, D])
        WV = GLA_H * DV + LOWRANK
        wv_hi = at("wv_hi", 0, [P, KT, WV], f32r)
        wv_lo = at("wv_lo", 16.5, [P, KT, WV], f32r)
        va = at("va", 33, [P, NT, GLA_H * DV])
        cum_0 = at("cum_0", 49, [P, S])[:, :]
        za_s = at("za_s", 65, [P, 2, S])
        k_end = at("k_end", 73, [P, NT, P])
        w_gu = yT[0:LOWRANK, 4, 0:GLA_H * DK]
        state = yT[:, 4, 256:256 + 6 * DV].rearrange("p (r v) -> p r v", r=6)
        at_sb = yT[:, 5, 0:4 * P].rearrange("p (b e i) -> p b e i", b=2, e=2)
        low_n = yT[:, 5, 512:512 + NT * LOWRANK].rearrange("p (t r) -> p t r", t=NT)
        sq_a = yT[:, 6, :]
        lrT = yT[0:LOWRANK, 7, :]
        cum_1 = yT[:, 7, :]
        q_e = [at("q_e", 53, [P, S])[:, :], cum_0]
        k_e = [at("k_e", 57, [P, S])[:, :], yT[:, 2, :]]
        k_dT = [at("k_dT", 61, [P, S])[:, :], yT[:, 3, :]]
        cums = [cum_0, cum_1]
        sq_hi = at("sq_hi", 61, [P, S], f32r)
        sq_lo = at("sq_lo", 49, [P, S], f32r)
        za = [za_s[:, 0, :], za_s[:, 1, :], q_e[0], k_e[0]]
        silu_b = yT[:, 7, :]
        cos_t = at("cos_t", 0, [P, S])
        sin_t = at("sin_t", 4, [P, S])
        cnt_t = at("cnt_t", 12, [P, S])
        pT = at("pT", 24, [P, NT, 2 * P])
        sq_b = at("sq_b", 8, [P, S])
        r_tmp = at("r_tmp", 16, [P, 2, HALF])
        zb_0 = at("zb_0", 20, [P, S])
        vb = at("vb", 33, [P, NT, DIL_H * HD])
        qkT = at("qkT", 49, [P, 4, S])
        pr = at("pr", 65, [P, 2, S])
        zb_1 = at("zb_1", 73, [P, S])
        sq_last = at("sq_last", 69, [P, S])
        wo_hi = [at("wo_hi_0", 0, [P, 4, KT, P], f32r), at("wo_hi_1", 16, [P, 4, KT, P], f32r)]
        wo_lo = [at("wo_lo_0", 49, [P, 4, KT, P], f32r), at("wo_lo_1", 33, [P, 4, KT, P], f32r)]
        gate_t = at("gate_t", 65, [P, D])
        x_t = at("x_t", 69, [P, 2, D])
        r_tmp2 = r_tmp[:, :, :].rearrange("p a b -> p (a b)")

        def bank(n, count=1):
            return ps[:, n:n + count, :].rearrange("p b n -> p (b n)") if count > 1 else ps[:, n, :]

        ps = ctx.enter_context(nc.psum_tensor("ps", [P, 8, HALF], f32))

        sems = []

        def sem(name):
            sems.append(nc.alloc_semaphore(name))
            return sems[-1]

        const_in = [sem(f"const_in{i}") for i in range(4)]
        x_in = [sem(f"x_in{t}") for t in range(NT)]
        raw_in = [sem(f"raw_in{i}") for i in range(RING)]
        low_in, vec_in, mods_in_sem, gu_in, tab_in = (sem(n) for n in ("low_in", "vec_in", "vecm_in", "gu_in", "tab_in"))
        gate_col, gate_mm = sem("gate_col"), sem("gate_mm")
        gate_used, ada_used = sem("gate_used"), sem("ada_used")
        w_hi, w_lo_pool, w_lo_dve = sem("w_hi"), sem("w_lo_pool"), sem("w_lo_dve")
        low_split, silu_mm, silu_ready, mods_ready = (sem(n) for n in ("low_split", "silu_mm", "silu_ready", "mods_ready"))
        xnT_done, h_hi, h_lo = sem("xnT_done"), sem("h_hi"), sem("h_lo")
        h_full, h_lo_pool, h_hi_dve = sem("h_full"), sem("h_lo_pool"), sem("h_hi_dve")
        unit_done = sem("unit_done")
        unit_free = [sem("unit_free0"), sem("unit_free1")]
        z_abs, z_soft, z_arg, z_sig, z_done = (sem(n) for n in ("z_abs", "z_soft", "z_arg", "z_sig", "z_done"))
        lowT_done, lowT_evac, dk_z, dk_abs, dk_soft, dk_cum, dk_rest, dk_exp = (sem(n) for n in (
            "lowT_done", "lowT_evac", "dk_z", "dk_abs", "dk_soft", "dk_cum", "dk_rest", "dk_exp"))
        kd_done, kend_ready, at_done, at_masked, cs_done, state_done, o_done, o_evac = (sem(n) for n in (
            "kd_done", "kend_ready", "at_done", "at_masked", "cs_done", "state_done", "o_done", "o_evac"))
        sq_done, norm_done, ln_done, rs_done, y_done = (sem(n) for n in (
            "sq_done", "norm_done", "ln_done", "rs_done", "y_done"))
        s_done, s_masked, exp_done, p_ready, pt_done, pt_evac, pv_done, pv_evac = (sem(n) for n in (
            "s_done", "s_masked", "exp_done", "p_ready", "pt_done", "pt_evac", "pv_done", "pv_evac"))
        y_scaled, sq_high, sq_low = sem("y_scaled"), sem("sq_high"), sem("sq_low")
        y_hi, y_hi_dve, y_lo_dve, y_lo_pool = sem("y_hi"), sem("y_hi_dve"), sem("y_lo_dve"), sem("y_lo_pool")
        gate_ready, yp_done, sqy_done, rstd_y, yp_free, x_new, sqx_done, rstd_x, xn_done = (sem(n) for n in (
            "gate_ready", "yp_done", "sqy_done", "rstd_y", "yp_free", "x_new", "sqx_done", "rstd_x", "xn_done"))
        x_load = [sem("x_load0"), sem("x_load1")]
        x_store = [sem("x_store0"), sem("x_store1")]
        dve_seq, act_seq = sem("dve_seq"), sem("act_seq")

        user_sem = {"gate": gate_used, "ada": ada_used, "pool": w_lo_pool, "dve": w_lo_dve}

        def wait_used(eng, n):
            eng.wait_ge(user_sem[user(n)], used(n))

        def highs(n):
            return sum(user(i) in ("pool", "dve") for i in range(VA0, n + 1))

        def wait_unit_evacuated(eng, u):
            eng.wait_ge(unit_free[u % 2], u // 2 + 1)

        def pt_chunk(h, i, part):
            return 12 * h + (i if i < 4 else 4 + 2 * (i - 4) + part)

        def pt_parts(i):
            return [(0, i + 1)] if i < 4 else [(0, 4), (4, i + 1)]

        def states(j, c):
            return (2 * NT - 1) * j + c

        T_Z = (0, 1, 6, 7)
        T_QA, T_KA = (2, 4), (3, 5)
        T_B = lambda h, n: T_GLA + 3 * h + n
        gla_fill = [[(t, half) for t in ts for half in range(2)] for ts in ((T_QA[1], T_KA[1]), T_Z[2:])]
        Z_ARG = 3
        VB_SPLIT = 3
        Z_ARG_STEPS = [(h, 0) for h in range(1, DIL_H)] + [(DIL_H, completed_step(STEP_MM[DIL_H], 1) + 1)]
        Z_STEPS = [(h, i + 1) for h, i in Z_ARG_STEPS]
        dil_units = lambda h: [(T_B(h, kind), half) for kind in range(3) for half in range(2)]
        PROLOGUE_RAW = 2

        def raw_tile(n):
            return raw[:, slot(n), :, :]

        def load_tile(sp, n, index):
            sp.dma_start(raw_tile(n), tiles[bass.ds(index, 1), :, :].rearrange("o p (k c) -> (o p) k c", k=KT))\
                .then_inc(raw_in[slot(n)], 16)

        def load_next(sp, n, first, wait):
            for i in range(len(NEXT)):
                wait(n + i)
                load_tile(sp, n + i, first + i)

        def mods(dve, k0, k1, seq):
            cols = slice(2 * k0, 2 * k1)
            nc.vector.tensor_tensor(mod[:, cols], mod[:, cols], b_ada_c[:, cols], ADD).then_inc(mods_ready, 1)
            dve.wait_ge(mods_ready, seq + 1)
            nc.vector.scalar_tensor_tensor(out=h_scale[:, k0:k1], in0=mod[:, 2 * k0 + 1:2 * k1:2], scalar=1.0,
                                           in1=g_pre_c[:, k0:k1], op0=ADD, op1=MULT).then_inc(mods_ready, 1)

        def mod_tile(at_, column, silu, used_sem):
            t = raw_tile(at_).rearrange("p k c -> p (k c)")
            nc.vector.tensor_tensor_reduce(out=t, in0=t, in1=silu[:, :], scale=1.0, scalar=0.0, op0=MULT, op1=ADD,
                                           accum_out=column).then_inc(used_sem, 1)

        def h_bank(b, k):
            return ps[:, b + k // 2, (k % 2) * 2 * P:(k % 2 + 1) * 2 * P]

        def h_transpose(m, b, k):
            for t in range(2):
                last = nc.tensor.transpose(h_bank(b, k)[:, t * P:(t + 1) * P], yT[:, 2 * m + t, k * P:(k + 1) * P],
                                           idn[:, :])
            return last

        def h_high(m, b, k):
            nc.scalar.activation(act_hi[:, k, 2 * P * m:2 * P * (m + 1)], h_bank(b, k), ACT.Identity,
                                 scale=h_scale[:, k:k + 1], bias=mod[:, 2 * k:2 * k + 1]).then_inc(h_hi, 1)

        def h_low(dve, m, b, k, done, tmp):
            dst = act_lo[:, k, 2 * P * m:2 * P * (m + 1)]
            src_hi = act_hi[:, k, 2 * P * m:2 * P * (m + 1)].bitcast(f32)
            nc.vector.scalar_tensor_tensor(out=tmp, in0=h_bank(b, k), scalar=h_scale[:, k:k + 1], in1=src_hi,
                                           op0=MULT, op1=SUB).then_inc(h_lo, 1)
            dve.wait_ge(h_lo, 2 * done + 1)
            nc.vector.tensor_scalar(dst, tmp, mod[:, 2 * k:2 * k + 1], None, ADD).then_inc(h_lo, 1)

        def h_tmp(m, k):
            return yT[:, 2 * m + k // 4, (k % 4) * 2 * P:(k % 4 + 1) * 2 * P]

        def norm_x(act, t, buf, junk, n):
            nc.scalar.activation(junk, buf, ACT.Square, accum_out=ss8[:, t:t + 1]).then_inc(sqx_done, 1)
            act.wait_ge(sqx_done, 2 * n + 1)
            nc.scalar.activation(ln8[:, t:t + 1], ss8[:, t:t + 1], ACT.Ln, bias=EPS, scale=1.0 / D)\
                .then_inc(sqx_done, 1)
            act.wait_ge(sqx_done, 2 * n + 2)
            nc.scalar.activation(rs8[:, t:t + 1], ln8[:, t:t + 1], ACT.Exp, scale=-0.5).then_inc(rstd_x, 1)

        def high(act, n, dst, laps):
            act.wait_ge(raw_in[slot(n)], 16 * laps)
            nc.scalar.copy(dst, raw_tile(n)).then_inc(w_hi, 1)

        def rows_of(columns, b, done):
            for k in range(KT):
                last = nc.tensor.matmul(ps[:, b + k // 4, (k % 4) * P:(k % 4 + 1) * P],
                                        columns[:, k:k + 1].broadcast_to([P, P]), idn[:, :], start=True, stop=True)
            last.then_inc(done, 1)

        def first_unit():
            for m in range(MM):
                k, part = divmod(m, 3)
                s, v = PARTS[part]
                nc.tensor.matmul(bank(0), (wt_hi, wt_lo)[s][:, 0, k, :], (act_hi, act_lo)[v][:, k, 0:HALF],
                                 start=(m == 0), stop=(m == MM - 1))

        ADA_AT = lambda n: PROLOGUE_RAW + n
        NEXT_AT = PROLOGUE_RAW + ADA_TILES

        H_TURNS = [(0, 0), (0, 1), (1, 0), (0, 2), (1, 1), (0, 3), (1, 2), (1, 3)]
        SPLIT_STEP = H_TURNS.index((0, 3))

        def h_turn_done(turn, kp):
            return H_TURNS.index((turn, kp)) + 1

        def full_done(turn, kp):
            return sum(4 if turn_ else 2 for turn_, _ in H_TURNS[:h_turn_done(turn, kp)])

        def laps_from(start, n):
            return sum(slot(i) == slot(n) for i in range(start, n + 1))

        with nc.Block() as block:
            @block.sync
            def _(sp):
                sp.dma_start(c_sb, c_cols).then_inc(const_in[0], 16)
                sp.dma_start(idn[:, :], ident).then_inc(const_in[1], 16)
                sp.dma_start(vec_m[:, :], mods_in[0]).then_inc(mods_in_sem, 16)
                def load_x(t):
                    sp.dma_start(yT[:, t, :], x[0, t * P:(t + 1) * P, :]).then_inc(x_in[t], 16)

                for n in range(ADA_TILES):
                    if n >= RING:
                        sp.wait_ge(ada_used, n - RING + 1)
                    load_tile(sp, ADA_AT(n), n)
                    for t in {1: (0, 1), 3: (2, 3, 4), 4: (5,), 5: (6,), 6: (7,)}.get(n, ()):
                        load_x(t)
                def wait(i):
                    if i < NEXT_AT + RING:
                        sp.wait_ge(ada_used, ADA_TILES - RING + i - NEXT_AT + 1)
                    else:
                        sp.wait_ge(w_lo_pool, i - NEXT_AT - RING + 1)
                load_next(sp, NEXT_AT, ADA_TILES, wait)
                sp.dma_start(raw_low[:, :, :], w_low[0].rearrange("p (k c) -> p k c", k=KT)).then_inc(low_in, 16)
                sp.dma_start(causal_sb[:, :], causal).then_inc(const_in[2], 16)
                sp.wait_ge(const_in[2], 16)
                sp.wait_ge(low_in, 16)
                for i in range(RING):
                    sp.wait_ge(raw_in[i], 16 * laps_from(PROLOGUE_RAW, NEXT_AT + FIRST_T + i))

            @block.gpsimd
            def _(pool):
                done = 0
                for step, (turn, kp) in enumerate(H_TURNS):
                    for k in (2 * kp, 2 * kp + 1):
                        for m in ((2, 3) if turn else (1,)):
                            pool.wait_ge(h_full, done + 1)
                            nc.gpsimd.tensor_tensor(act_lo[:, k, 2 * P * m:2 * P * (m + 1)], h_tmp(m % 2, k),
                                                    act_hi[:, k, 2 * P * m:2 * P * (m + 1)].bitcast(f32), SUB)\
                                .then_inc(h_lo_pool, 1)
                            done += 1
                    if step == SPLIT_STEP:
                        for t in range(FIRST_T):
                            pool.wait_ge(w_hi, t + 1)
                            nc.gpsimd.tensor_tensor(wt_lo[:, t % 2], raw_tile(NEXT_AT + t),
                                                    wt_hi[:, t % 2].bitcast(f32), SUB).then_inc(w_lo_pool, 1)

            @block.scalar
            def _(act):
                act.preload_act_table_set("natural_log_exp_and_others")
                act.wait_ge(const_in[0], 16)
                nc.scalar.activation(c_e, c_sb, ACT.Exp, scale=-1.0).then_inc(act_seq, 1)
                act.wait_ge(silu_mm, 1)
                nc.scalar.copy(silu_first[:, :], bank(0, 2)).then_inc(silu_ready, 1)
                def norm(t):
                    act.wait_ge(x_in[t], 16)
                    norm_x(act, t, yT[:, t, :], h_junk[:, :], t)

                for t in range(4):
                    norm(t)
                for step, (turn, kp) in enumerate(H_TURNS):
                    if turn:
                        act.wait_ge(h_lo_pool, full_done(0, kp))
                    for k in (2 * kp, 2 * kp + 1):
                        act.wait_ge(mods_ready, 2 * k + 2)
                        for m in (2 * turn, 2 * turn + 1):
                            act.wait_ge(xnT_done, 2 + 2 * kp + m - 1 if turn else m + 1)
                            h_high(m, 4 * (1 - m % 2), k)
                            if m:
                                nc.scalar.activation(h_tmp(m % 2, k), h_bank(4 * (1 - m % 2), k), ACT.Identity,
                                                     scale=h_scale[:, k:k + 1], bias=mod[:, 2 * k:2 * k + 1])\
                                    .then_inc(h_full, 1)
                    for t in range(4, NT) if step == 0 else ():
                        norm(t)
                    if step == SPLIT_STEP:
                        for t in range(FIRST_T):
                            high(act, NEXT_AT + t, wt_hi[:, t % 2], laps_from(PROLOGUE_RAW, NEXT_AT + t))

            @block.vector
            def _(dve):
                nc.vector.memset(ones[:, :], 1.0).then_inc(dve_seq, 1)
                dve.wait_ge(dve_seq, 1)
                nc.vector.tensor_copy(ones_r[:, :], ones[:, 0:1]).then_inc(dve_seq, 1)
                dve.wait_ge(act_seq, 1)
                nc.vector.tensor_scalar_add(c_e, c_e, 1.0).then_inc(act_seq, 1)
                dve.wait_ge(act_seq, 2)
                nc.vector.reciprocal(c_e, c_e).then_inc(act_seq, 1)
                dve.wait_ge(act_seq, 3)
                nc.vector.tensor_tensor(silu_c, c_sb, c_e, MULT).then_inc(act_seq, 1)

                def normalise(t):
                    dve.wait_ge(rstd_x, t + 1)
                    nc.vector.tensor_scalar(yT[:, t, :], yT[:, t, :], rs8[:, t:t + 1], None, MULT)\
                        .then_inc(xn_done, 1)

                dve.wait_ge(silu_ready, 1)
                dve.wait_ge(mods_in_sem, 16)
                def lows(kp):
                    dve.wait_ge(h_hi, 4 * h_turn_done(0, kp))
                    for k in (2 * kp, 2 * kp + 1):
                        h_low(dve, 0, 4, k, k, h_tmp(0, k))

                for kp in range(KT // 2):
                    for k in (2 * kp, 2 * kp + 1):
                        for n in (2 * k, 2 * k + 1):
                            dve.wait_ge(raw_in[slot(ADA_AT(n))], 16 * laps_from(PROLOGUE_RAW, ADA_AT(n)))
                            mod_tile(ADA_AT(n), mod[:, n:n + 1], silu_first, ada_used)
                        dve.wait_ge(ada_used, 2 * k + 2)
                        mods(dve, k, k + 1, 2 * k)
                        for t in (2 * k, 2 * k + 1) if kp == 0 else ():
                            normalise(t)
                    if kp:
                        for t in range(4, NT) if kp == 1 else ():
                            normalise(t)
                        lows(kp - 1)
                lows(KT // 2 - 1)

            @block.tensor
            def _(pe):
                pe.wait_ge(const_in[1], 16)
                pe.wait_ge(act_seq, 4)
                rows_of(silu_c, 0, silu_mm)
                for m in range(2):
                    pe.wait_ge(xn_done, 2 * m + 2)
                    if m == 1:
                        pe.wait_ge(silu_ready, 1)
                    for k in range(KT):
                        last = h_transpose(m, 4 * (1 - m), k)
                    last.then_inc(xnT_done, 1)
                for kp in range(KT // 2):
                    for m in (2, 3):
                        pe.wait_ge(xn_done, 2 * m + 2)
                        if m == 2:
                            pe.wait_ge(h_lo, 4 * (kp + 1))
                        else:
                            pe.wait_ge(h_full, full_done(0, kp))
                        for k in (2 * kp, 2 * kp + 1):
                            last = h_transpose(m, 4 * (1 - m % 2), k)
                        last.then_inc(xnT_done, 1)
                pe.wait_ge(w_lo_pool, 1)
                pe.wait_ge(h_lo, 2 * KT)
                pe.wait_ge(h_lo_pool, full_done(0, 3))
                pe.wait_ge(h_full, full_done(1, 0))
                first_unit()
        nc.all_engine_barrier(sems_to_clear=range(sems[0].num, sems[-1].num + 1))

        TAB_POS = position(T_B(0, 2)) + 3
        GU_POS = 2

        with nc.Fori(0, DEPTH) as layer:
            with nc.Block() as block:
                @block.sync
                def _(sp):
                    per_layer = len(STREAM) + len(NEXT)
                    first = ADA_TILES + len(NEXT)
                    sp.dma_start(vec[:, :], vecs[bass.ds(layer, 1), :, :].rearrange("l p n -> (l p) n"))\
                        .then_inc(vec_in, 16)
                    sp.dma_start(w_gu, w_gate_up[bass.ds(layer * LOWRANK, LOWRANK), :]).then_inc(gu_in, 16)
                    for n, kind in enumerate(STREAM):
                        wait_used(sp, n - RING)
                        if kind == "ada":
                            with sp.If(layer < DEPTH - 1):
                                load_tile(sp, n, layer * per_layer + first + n)
                            with sp.Else():
                                sp.sem_inc(raw_in[slot(n)], 16)
                        else:
                            load_tile(sp, n, layer * per_layer + first + n)
                        if n == MOD_POS[GATE_TILES]:
                            with sp.If(layer < DEPTH - 1):
                                sp.dma_start(vec_m[:, :], mods_in[bass.ds(layer + 1, 1), :, :]
                                             .rearrange("l p n -> (l p) n")).then_inc(mods_in_sem, 16)
                            with sp.Else():
                                sp.sem_inc(mods_in_sem, 16)
                        if n == TAB_POS:
                            sp.wait_ge(unit_done, units_done(UNIT[("vb", NT - 1)]))
                            sp.dma_start(cos_t[:, :], rope_cos).then_inc(tab_in, 16)
                            sp.dma_start(sin_t[:, :], rope_sin).then_inc(tab_in, 16)
                            sp.dma_start(cnt_t[:, :], log_count).then_inc(tab_in, 16)
                    sp.wait_ge(y_done, GLA_H + DIL_H)

                    def load_x(t):
                        tok = slice(t * P, (t + 1) * P)
                        with sp.If(layer < 1):
                            sp.dma_start(x_t[:, t % 2, :], x[0, tok, :]).then_inc(x_load[t % 2], 16)
                        with sp.Else():
                            sp.dma_start(x_t[:, t % 2, :], out[0, tok, :]).then_inc(x_load[t % 2], 16)

                    load_x(0)
                    load_x(1)
                    for t in range(NT):
                        sp.wait_ge(x_new, t + 1)
                        sp.dma_start(out[0, t * P:(t + 1) * P, :], x_t[:, t % 2, :]).then_inc(x_store[t % 2], 16)
                        if t == 1:
                            with sp.If(layer < DEPTH - 1):
                                load_next(sp, len(STREAM), layer * per_layer + first + len(STREAM),
                                          lambda i: wait_used(sp, i - RING))
                                sp.dma_start(raw_low[:, :, :], w_low[bass.ds(layer + 1, 1), :, :]
                                             .rearrange("l p (k c) -> (l p) k c", k=KT)).then_inc(low_in, 16)
                                sp.wait_ge(low_in, 16)
                        if t + 2 < NT:
                            sp.wait_ge(x_store[t % 2], 16 * (t // 2 + 1))
                            with sp.If(layer < DEPTH - 1):
                                sp.wait_ge(xn_done, t + 1)
                            load_x(t + 2)
                    for b in range(2):
                        sp.wait_ge(x_store[b], 16 * (NT // 2))
                    with sp.If(layer < DEPTH - 1):
                        for i in range(RING):
                            sp.wait_ge(raw_in[i], 16 * lap(len(STREAM) + FIRST_T + i))

                @block.gpsimd
                def _(pool):
                    def low(n, dst, src_hi):
                        pool.wait_ge(w_hi, highs(n))
                        nc.gpsimd.tensor_tensor(dst, raw_tile(n), src_hi.bitcast(f32), SUB).then_inc(w_lo_pool, 1)

                    def low_cols(n, lo, hi, v):
                        if user(n) == "pool":
                            low(n, lo[:, :, v * P:(v + 1) * P], hi[:, :, v * P:(v + 1) * P])

                    for v in range(VT):
                        low_cols(VA0 + v, wv_lo, wv_hi, va_column(v))
                    for t in range(FIRST_T, len(T_TILES)):
                        if t == T_GLA:
                            for v in range(VT):
                                low_cols(VB0 + v, wv_lo, wv_hi, v)
                        low(position(t), wt_lo[:, t % 2], wt_hi[:, t % 2])
                    def low_wo(v):
                        low(WO0 + v, wo_lo[v // 4][:, v % 4], wo_hi[v // 4][:, v % 4])

                    pool.wait_ge(s_done, NT * (DIL_H - 1))
                    low_wo(0)
                    low_wo(1)
                    for h in range(POOL_Y):
                        pool.wait_ge(y_hi, h + 1)
                        nc.gpsimd.tensor_tensor(act_lo[:, h, :], yT[:, h, :], act_hi[:, h, :].bitcast(f32), SUB)\
                            .then_inc(y_lo_pool, 1)
                    pool.wait_ge(pv_done, 4 * DIL_H)
                    low_wo(4)
                    low_wo(6)
                    with pool.If(layer < DEPTH - 1):
                        for t in range(FIRST_T):
                            low(len(STREAM) + t, wt_lo[:, t % 2], wt_hi[:, t % 2])
                        for k in range(KT // 2, KT):
                            pool.wait_ge(h_full, k - KT // 2 + 1)
                            nc.gpsimd.tensor_tensor(act_lo[:, k, 6 * P:8 * P], h_tmp(3, k),
                                                    act_hi[:, k, 6 * P:8 * P].bitcast(f32), SUB)\
                                .then_inc(h_lo_pool, 1)

                @block.scalar
                def _(act):
                    def split(n, dst):
                        high(act, n, dst, lap(n))

                    def split_t(t):
                        if t < len(T_TILES):
                            act.wait_ge(unit_done, units_done(UNIT[(t - 2, 1)]))
                            split(position(t), wt_hi[:, t % 2])

                    def z_abs_unit(head, key, tmp):
                        half = key[1]
                        if UNIT[key]:
                            act.wait_ge(unit_done, units_done(UNIT[key]))
                        if head:
                            act.wait_ge(z_done, head)
                        nc.scalar.activation(tmp[:, half * HALF:(half + 1) * HALF], bank(UNIT[key] % 2), ACT.Abs)\
                            .then_inc(z_abs, 1)

                    def z_softplus(head, tmp):
                        act.wait_ge(z_abs, 2 * (head + 1))
                        nc.scalar.activation(tmp, tmp, ACT.Exp, scale=-1.0).then_inc(z_soft, 1)
                        act.wait_ge(z_soft, 2 * head + 1)
                        nc.scalar.activation(tmp, tmp, ACT.Ln, bias=1.0).then_inc(z_soft, 1)

                    def z_sigmoid(head, tmp):
                        act.wait_ge(z_arg, head + 1)
                        nc.scalar.activation(tmp, tmp, ACT.Exp).then_inc(z_sig, 1)

                    def norm_square(head, buf):
                        if head:
                            act.wait_ge(y_done, head)
                        if head < GLA_H:
                            act.wait_ge(o_evac, NT * (head // 2 + 1))
                            act.wait_ge(z_done, GLA_H)
                        else:
                            act.wait_ge(pv_evac, 4 * (head - GLA_H + 1))
                        nc.scalar.activation(buf, yT[:, head, :], ACT.Square).then_inc(sq_done, 1)
                        if head < GLA_H:
                            act.wait_ge(sq_done, head + 1)
                            if head:
                                act.wait_ge(norm_done, head)
                            nc.scalar.copy(sq_hi[:, :], buf).then_inc(sq_high, 1)

                    def norm_rs(head, buf, b, step=1):
                        act.wait_ge(norm_done, head + 1)
                        for half in range(2 if step > 1 else 1):
                            cols = slice(half * HALF, (half + 1) * HALF) if step > 1 else slice(0, S)
                            src = bank(b + step * half) if step > 1 else bank(b, 2)
                            last = nc.scalar.activation(buf[:, cols], src, ACT.Ln, scale=1.0 / DV, bias=EPS)
                        last.then_inc(ln_done, 1)
                        act.wait_ge(ln_done, head + 1)
                        nc.scalar.activation(buf, buf, ACT.Exp, scale=-0.5).then_inc(rs_done, 1)

                    for n in range(VT):
                        v = va_column(n)
                        nc.scalar.copy(wv_hi[:, :, v * P:(v + 1) * P], raw_tile(VA0 + n)).then_inc(w_hi, 1)
                        if n == 1:
                            nc.scalar.copy(wv_hi[:, :, GLA_H * DV:WV], raw_low[:, :, :]).then_inc(low_split, 1)
                            z_abs_unit(0, (T_Z[0], 0), sq_a)
                    z_abs_unit(0, (T_Z[0], 1), sq_a)
                    split_t(2)
                    z_softplus(0, sq_a)

                    def decay_soft(j):
                        act.wait_ge(dk_abs, 2 * j + 1)
                        nc.scalar.activation(k_e[j], k_e[j], ACT.Exp, scale=-1.0).then_inc(dk_soft, 1)
                        act.wait_ge(dk_soft, 2 * j + 1)
                        nc.scalar.activation(k_e[j], k_e[j], ACT.Ln, bias=1.0).then_inc(dk_soft, 1)

                    def decay_exps(j):
                        act.wait_ge(dk_cum, j + 1)
                        if j:
                            act.wait_ge(dk_exp, 4 * j)
                        nc.scalar.activation(q_e[j], cums[j], ACT.Exp).then_inc(dk_exp, 1)
                        nc.scalar.activation(k_e[j], cums[j], ACT.Exp, scale=-1.0).then_inc(dk_exp, 1)
                        act.wait_ge(dk_rest, j + 1)
                        nc.scalar.activation(k_dT[j], k_dT[j], ACT.Exp).then_inc(dk_exp, 1)
                        nc.scalar.activation(decay[j], cums[j][:, CHUNK - 1:S:CHUNK], ACT.Exp).then_inc(dk_exp, 1)

                    n_v = GLA_H * DV - V_COLS
                    for t in range(NT):
                        u = UNIT[("va", t, 1)]
                        act.wait_ge(unit_done, units_done(u))
                        nc.scalar.copy(low_n[:, t, :], bank(u % 2)[:, n_v:V_COLS]).then_inc(act_seq, 1)
                        nc.scalar.copy(va[:, t, V_COLS:], bank(u % 2)[:, 0:n_v]).then_inc(unit_free[u % 2], 1)
                        if t == 1:
                            z_sigmoid(0, sq_a)
                    for t in range(NT):
                        u = UNIT[("va", t, 0)]
                        act.wait_ge(unit_done, units_done(u))
                        nc.scalar.copy(va[:, t, 0:V_COLS], bank(u % 2)[:, 0:V_COLS]).then_inc(unit_free[u % 2], 1)
                        if t == 0:
                            act.wait_ge(lowT_done, 1)
                            nc.scalar.copy(lrT, bank(2, 2)[0:LOWRANK, :]).then_inc(lowT_evac, 1)
                        if t in (2, 3):
                            decay_soft(t - 2)
                        if t in (4, 5):
                            decay_exps(t - 4)
                    z_abs_unit(1, (T_Z[1], 0), sq_a)
                    z_abs_unit(1, (T_Z[1], 1), sq_a)
                    split_t(T_Z[1] + 2)
                    z_softplus(1, sq_a)
                    z_sigmoid(1, sq_a)
                    split_t(T_QA[0] + 2)
                    split_t(T_KA[0] + 2)
                    for j in range(PAIRS):
                        for q in range(2):
                            act.wait_ge(kd_done, 2 * j + q + 1)
                            nc.scalar.copy(k_end[:, 4 * q:4 * q + 4, :].rearrange("p t k -> p (t k)"), bank(6 + q))\
                                .then_inc(kend_ready, 1)
                        if j:
                            z_abs_unit(2, gla_fill[1][0], sq_a)
                        for p in range(NT):
                            for n in completed(FILL, p):
                                key = gla_fill[j][n + 1]
                                if j == 0 and key[1]:
                                    split_t(key[0] + 2)
                                if j:
                                    z_abs_unit(2 + (n + 1) // 2, key, sq_a)
                                    if key[1]:
                                        z_softplus(2 + (n + 1) // 2, sq_a)
                            act.wait_ge(o_done, NT * j + p + 1)
                            nc.scalar.copy(yT[:, 2 * j:2 * j + 2, p * P:(p + 1) * P], ps[:, 6:8, 0:P])\
                                .then_inc(o_evac, 1)
                            if j and p == Z_ARG:
                                z_sigmoid(2, sq_a)
                            if j and VB_SPLIT <= p < VB_SPLIT + VT:
                                v = p - VB_SPLIT
                                split(VB0 + v, wv_hi[:, :, v * P:(v + 1) * P])
                    z_sigmoid(3, sq_a)
                    split_t(T_Z[2] + 2)
                    split_t(T_Z[3] + 2)
                    for t in range(NT):
                        u = UNIT[("vb", t)]
                        if t in NORM_STEPS:
                            norm_square(NORM_STEPS.index(t), sq_a)
                            norm_rs(NORM_STEPS.index(t), sq_a, 2)
                        act.wait_ge(unit_done, units_done(u))
                        nc.scalar.copy(vb[:, t, :], bank(u % 2)).then_inc(unit_free[u % 2], 1)

                    def split_wo(v):
                        if v < 2:
                            for half in range(2):
                                wait_unit_evacuated(act, UNIT[(T_B(DIL_H - 1, 1), half)])
                        if v in (2, 5):
                            act.wait_ge(y_done, GLA_H + DIL_H - 1)
                        if v == 3:
                            act.wait_ge(s_masked, NT * DIL_H)
                        if v == 4:
                            act.wait_ge(z_done, GLA_H + DIL_H)
                        if v > 5:
                            act.wait_ge(pv_done, 4 * DIL_H)
                        split(WO0 + v, wo_hi[v // 4][:, v % 4])

                    def attend(h, i, unit_work):
                        if i < NT:
                            n = NT * h + i
                            act.wait_ge(s_masked, n + 1)
                            nc.scalar.activation(pr[:, i % 2, 0:(i + 1) * P], pr[:, i % 2, 0:(i + 1) * P], ACT.Exp,
                                                 scale=-1.0, bias=nmax[:, i % 2:i % 2 + 1],
                                                 accum_out=den[:, i % 2:i % 2 + 1]).then_inc(exp_done, 1)

                        def evacuate_pt(part, j0, j1):
                            q = i - 1
                            c = pt_chunk(h, q, part)
                            act.wait_ge(pt_done, c + 1)
                            if q % 2 == 0 and part == 0 and (h or q):
                                act.wait_ge(pv_done, 4 * h + q // 2)
                            nc.scalar.copy(pT[:, j0:j1, (q % 2) * P:(q % 2 + 1) * P],
                                           bank(6)[:, 0:(j1 - j0) * P].rearrange("p (j q) -> p j q", q=P))\
                                .then_inc(pt_evac, 1)
                        if h == DIL_H - 1 and i == NT + 1:
                            split_wo(3)
                            act.wait_ge(gate_mm, 1)
                            act.wait_ge(pt_done, pt_chunk(DIL_H, 0, 0))
                            nc.scalar.copy(gate_t[:, :], bank(0, 2)).then_inc(gate_ready, 1)
                            split_wo(4)
                            split_wo(5)
                        if 3 <= i and i % 2:
                            g = (i - 3) // 2
                            act.wait_ge(pv_done, 4 * h + g + 1)
                            if h == DIL_H - 1 and g == 0:
                                act.wait_ge(ada_used, ADA_TILES)
                                act.wait_ge(gate_used, GATE_TILES)
                            nc.scalar.copy(yT[:, GLA_H + h, 2 * P * g:2 * P * (g + 1)], bank(7)[:, 0:2 * P])\
                                .then_inc(pv_evac, 1)
                        if 1 <= i <= NT:
                            evacuate_pt(0, *pt_parts(i - 1)[0])
                        if 5 <= i <= NT:
                            evacuate_pt(1, *pt_parts(i - 1)[1])
                        unit_work()

                    def high_y(n):
                        act.wait_ge(unit_done, units_done(N_UNITS - 1))
                        act.wait_ge(y_done, n + 1)
                        nc.scalar.copy(act_hi[:, n, :], yT[:, n, :]).then_inc(y_hi, 1)

                    for h in range(DIL_H + 1):
                        for i in range(NT + 2):
                            def unit_work(i=i, h=h):
                                if (h, i) in Z_ARG_STEPS:
                                    z_sigmoid(GLA_H + h - 1, r_tmp2)
                                for h_, n in [slot_units(h)[c] for c in completed(STEP_MM[h], i)]:
                                    t, half = dil_units(h_)[n]
                                    if n == 4:
                                        wait_unit_evacuated(act, UNIT[(t - 1, 0)])
                                        wait_unit_evacuated(act, UNIT[(t - 1, 1)])
                                    if n >= 4:
                                        z_abs_unit(GLA_H + h_, (t, half), r_tmp2)
                                    if n == 5:
                                        z_softplus(GLA_H + h_, r_tmp2)
                                    if half:
                                        split_t(t + 2)
                                if i == 0 and h == 0:
                                    act.wait_ge(silu_mm, 1)
                                    nc.scalar.copy(silu_b, bank(2, 2)).then_inc(silu_ready, 1)
                                if i == 0 and h >= 2:
                                    norm_square(GLA_H + h - 2, sq_b[:, :])
                                if i == 2 and h >= 2:
                                    norm_rs(GLA_H + h - 2, sq_b[:, :], 3, 2)
                                if h == DIL_H:
                                    for n in Y_STEPS_ACT.get(i, ()):
                                        high_y(n)
                                    for v in WO_STEPS.get(i, ()):
                                        split_wo(v)
                            if h:
                                attend(h - 1, i, unit_work)
                            else:
                                unit_work()
                    norm_square(GLA_H + DIL_H - 1, sq_last[:, :])
                    split_wo(6)
                    split_wo(7)
                    norm_rs(GLA_H + DIL_H - 1, sq_last[:, :], 4)
                    high_y(GLA_H + DIL_H - 1)

                    for t in range(NT):
                        act.wait_ge(yp_done, t + 1)
                        if t >= 2:
                            act.wait_ge(yp_free, t - 1)
                        if t == 0:
                            act.wait_ge(y_lo_pool, POOL_Y)
                            act.wait_ge(y_lo_dve, KT - POOL_Y)
                            act.wait_ge(y_hi, POOL_Y + 1)
                        nc.scalar.activation(yT[:, t, :], bank(o_bank(t), 2), ACT.Square,
                                             accum_out=ss[:, t % 2:t % 2 + 1]).then_inc(sqy_done, 1)
                        act.wait_ge(sqy_done, t + 1)
                        nc.scalar.activation(lnt[:, t % 2:t % 2 + 1], ss[:, t % 2:t % 2 + 1], ACT.Ln, scale=1.0 / D,
                                             bias=EPS).then_inc(act_seq, 1)
                        act.wait_ge(act_seq, NT + t + 1)
                        nc.scalar.activation(rstd[:, t % 2:t % 2 + 1], lnt[:, t % 2:t % 2 + 1], ACT.Exp, scale=-0.5)\
                            .then_inc(rstd_y, 1)
                        with act.If(layer < DEPTH - 1):
                            act.wait_ge(x_new, t + 1)
                            norm_x(act, t, x_t[:, t % 2, :], yT[:, t, :], t)
                            if t == 1:
                                for v in range(FIRST_T):
                                    split(len(STREAM) + v, wt_hi[:, v])
                            for m in h_after(t):
                                act.wait_ge(mods_ready, 2)
                                act.wait_ge(xnT_done, m + 1)
                                for k in range(KT if m < 3 else 0):
                                    h_high(m, 4, k)
                                for k in range(KT // 2, KT if m == 3 else 0):
                                    h_high(m, 4, k)
                                    nc.scalar.activation(h_tmp(m, k), h_bank(4, k), ACT.Identity,
                                                         scale=h_scale[:, k:k + 1], bias=mod[:, 2 * k:2 * k + 1])\
                                        .then_inc(h_full, 1)

                @block.vector
                def _(dve):
                    count = [0]

                    def link(ins):
                        count[0] += 1
                        ins.then_inc(dve_seq, 1)
                        dve.wait_ge(dve_seq, count[0])

                    V = nc.vector

                    def low(n, dst, src_hi):
                        dve.wait_ge(w_hi, highs(n))
                        V.tensor_tensor(dst, raw_tile(n), src_hi.bitcast(f32), SUB).then_inc(w_lo_dve, 1)

                    def low_cols(n, lo, hi, v):
                        if user(n) == "dve":
                            low(n, lo[:, :, v * P:(v + 1) * P], hi[:, :, v * P:(v + 1) * P])

                    def z_copy(head, key, dst):
                        u = UNIT[key]
                        cols = slice(key[1] * HALF, (key[1] + 1) * HALF)
                        if head in (2, 3):
                            dve.wait_ge(o_done, NT)
                        if head >= GLA_H + 2:
                            dve.wait_ge(y_done, head - 1)
                        dve.wait_ge(z_abs, 2 * head + key[1] + 1)
                        V.tensor_copy(dst[:, cols], bank(u % 2)).then_inc(unit_free[u % 2], 1)

                    def z_argument(head, key, dst, tmp):
                        dve.wait_ge(z_soft, 2 * (head + 1))
                        wait_unit_evacuated(dve, UNIT[key])
                        wait_unit_evacuated(dve, UNIT[key] - 1)
                        V.scalar_tensor_tensor(out=tmp, in0=dst, scalar=0.0, in1=tmp, op0=MIN, op1=SUB)\
                            .then_inc(z_arg, 1)

                    def z_gate(head, dst, tmp):
                        dve.wait_ge(z_sig, head + 1)
                        V.scalar_tensor_tensor(out=dst, in0=dst, scalar=g_head[:, head:head + 1], in1=tmp,
                                               op0=MULT, op1=MULT).then_inc(z_done, 1)

                    def finish_y(head, buf, z, steps=(0, 1)):
                        if 0 in steps:
                            dve.wait_ge(rs_done, head + 1)
                            dve.wait_ge(z_done, head + 1)
                            V.tensor_tensor(yT[:, head, :], yT[:, head, :], buf, MULT).then_inc(y_scaled, 1)
                        if 1 in steps:
                            dve.wait_ge(y_scaled, head + 1)
                            V.tensor_tensor(yT[:, head, :], yT[:, head, :], z, MULT).then_inc(y_done, 1)

                    for v in range(VT):
                        low_cols(VA0 + v, wv_lo, wv_hi, va_column(v))
                        if v == 1:
                            dve.wait_ge(low_split, 1)
                            V.tensor_tensor(wv_lo[:, :, GLA_H * DV:WV], raw_low[:, :, :],
                                            wv_hi[:, :, GLA_H * DV:WV].bitcast(f32), SUB).then_inc(low_split, 1)
                            z_copy(0, (T_Z[0], 0), za[0])
                    dve.wait_ge(vec_in, 16)
                    z_copy(0, (T_Z[0], 1), za[0])
                    z_argument(0, (T_Z[0], 1), za[0], sq_a)
                    z_gate(0, za[0], sq_a)
                    link(V.memset(yT[:, 5, 0:4 * P], 0.0))

                    def decay_start(j):
                        z = cums[j]
                        dve.wait_ge(dk_z, 4)
                        link(V.tensor_scalar(z, bank(4 + 2 * j, 2), b_gu_c[:, j:j + 1], None, ADD))
                        V.scalar_tensor_tensor(out=k_e[j], in0=z, scalar=-1.0, in1=z, op0=MULT, op1=MAX)\
                            .then_inc(dk_abs, 1)
                        V.tensor_scalar(k_dT[j], z, 0.0, 1.0 / 16.0, MIN, MULT).then_inc(dk_abs, 1)

                    def decay_cumulate(j):
                        dve.wait_ge(dk_soft, 2 * (j + 1))
                        dve.wait_ge(dk_abs, 2 * (j + 1))
                        link(V.scalar_tensor_tensor(out=k_e[j], in0=k_e[j], scalar=-1.0 / 16.0, in1=k_dT[j],
                                                    op0=MULT, op1=ADD))
                        for c in range(S // CHUNK):
                            cs = slice(c * CHUNK, (c + 1) * CHUNK)
                            last = V.tensor_tensor_scan(cums[j][:, cs], ones[:, 0:CHUNK], k_e[j][:, cs], 0.0, MULT,
                                                        ADD)
                        last.then_inc(dk_cum, 1)
                        dve.wait_ge(dk_cum, j + 1)
                        cum3 = cums[j].rearrange("p (c i) -> p c i", i=CHUNK)
                        V.tensor_tensor(k_dT[j].rearrange("p (c i) -> p c i", i=CHUNK),
                                        cum3[:, :, CHUNK - 1:CHUNK].broadcast_to([P, S // CHUNK, CHUNK]), cum3,
                                        SUB).then_inc(dk_rest, 1)

                    def q_half(j, half):
                        cols = slice(half * HALF, (half + 1) * HALF)
                        u = UNIT[(T_QA[j], half)]
                        dve.wait_ge(dk_exp, 4 * j + 1)
                        dve.wait_ge(unit_done, units_done(u))
                        V.scalar_tensor_tensor(out=q_e[j][:, cols], in0=bank(u % 2), scalar=DK ** -0.5,
                                               in1=q_e[j][:, cols], op0=MULT, op1=MULT).then_inc(unit_free[u % 2], 1)

                    def k_half(j, half):
                        cols = slice(half * HALF, (half + 1) * HALF)
                        u = UNIT[(T_KA[j], half)]
                        dve.wait_ge(dk_exp, 4 * j + 4)
                        dve.wait_ge(unit_done, units_done(u))
                        V.tensor_tensor(k_e[j][:, cols], bank(u % 2), k_e[j][:, cols], MULT).then_inc(dve_seq, 1)
                        count[0] += 1
                        V.tensor_tensor(k_dT[j][:, cols], bank(u % 2), k_dT[j][:, cols], MULT)\
                            .then_inc(unit_free[u % 2], 1)

                    for j in range(PAIRS):
                        decay_start(j)
                    for j in range(PAIRS):
                        decay_cumulate(j)
                    z_copy(1, (T_Z[1], 0), za[1])
                    z_copy(1, (T_Z[1], 1), za[1])
                    z_argument(1, (T_Z[1], 1), za[1], sq_a)
                    z_gate(1, za[1], sq_a)
                    q_half(0, 0)
                    q_half(0, 1)
                    k_half(0, 0)
                    k_half(0, 1)

                    for j in range(PAIRS):
                        if j:
                            z_copy(2, gla_fill[1][0], za[2])
                        else:
                            q_half(1, 0)

                        def mask_and_states(p):
                            s = NT * j + p
                            dve.wait_ge(at_done, s + 1)
                            if s >= 2:
                                dve.wait_ge(o_done, s - 1)
                            V.copy_predicated(at_sb[:, p % 2, :, :],
                                              causal_sb[:, :].rearrange("p (a i) -> p a i", a=1)
                                              .broadcast_to([P, 2, P]),
                                              ps[:, 2:4, 0:P]).then_inc(at_masked, 1)
                            dve.wait_ge(cs_done, s + 1)
                            if p == 0 and j:
                                dve.wait_ge(o_done, NT * j)
                            for e in range(2):
                                c = 2 * p + e
                                if c == 2 * NT - 1:
                                    continue
                                new = state[:, (c + 1) % 6, :]
                                if c == 0:
                                    V.tensor_copy(new, bank(4)[:, 0:DV]).then_inc(state_done, 1)
                                else:
                                    dve.wait_ge(state_done, states(j, c))
                                    V.scalar_tensor_tensor(out=new, in0=state[:, c % 6, :], scalar=decay[j][:, c:c + 1],
                                                           in1=bank(4 + e)[:, 0:DV], op0=MULT, op1=ADD)\
                                        .then_inc(state_done, 1)

                        mask_and_states(0)
                        for p in range(NT):
                            if p + 1 < NT:
                                mask_and_states(p + 1)
                            if j and p == Z_ARG:
                                z_argument(2, gla_fill[1][1], za[2], sq_a)
                            if j and p == Z_ARG + 1:
                                z_gate(2, za[2], sq_a)
                            for n in completed(FILL, p):
                                head = 2 + (n + 1) // 2
                                if j:
                                    z_copy(head, gla_fill[1][n + 1], za[head])
                                else:
                                    (q_half, k_half)[(n + 1) // 2](1, (n + 1) % 2)
                    z_argument(3, gla_fill[1][3], za[3], sq_a)
                    z_gate(3, za[3], sq_a)
                    for head in range(GLA_H):
                        dve.wait_ge(sq_high, head + 1)
                        if head:
                            dve.wait_ge(norm_done, head)
                        V.tensor_tensor(sq_lo[:, :], sq_a, sq_hi[:, :].bitcast(f32), SUB).then_inc(sq_low, 1)
                        finish_y(head, sq_a, za[head])

                    dve.wait_ge(tab_in, 48)
                    dve.wait_ge(y_done, GLA_H)

                    def rope(h, n):
                        kind, half = divmod(n, 2)
                        cols = slice(half * HALF, (half + 1) * HALF)
                        dst = qkT[:, 2 * (h % 2) + kind, cols]
                        u = UNIT[(T_B(h, kind), half)]
                        dve.wait_ge(unit_done, units_done(u))
                        V.tensor_tensor(dst, bank(u % 2), cos_t[:, cols], MULT).then_inc(dve_seq, 1)
                        tmp = r_tmp[:, half, :]
                        if n >= 2:
                            wait_unit_evacuated(dve, u - 2)
                        elif h:
                            dve.wait_ge(z_done, GLA_H + h)
                        V.tensor_tensor(tmp[0:64, :], bank(u % 2)[64:128, :], sin_t[64:128, cols], MULT)\
                            .then_inc(dve_seq, 1)
                        V.tensor_tensor(tmp[64:128, :], bank(u % 2)[0:64, :], sin_t[0:64, cols], MULT)\
                            .then_inc(dve_seq, 1)
                        count[0] += 3
                        dve.wait_ge(dve_seq, count[0])
                        V.tensor_tensor(dst, dst, tmp, ADD).then_inc(unit_free[u % 2], 1)

                    def modulation(n):
                        if n == 0:
                            dve.wait_ge(silu_ready, 1)
                        dve.wait_ge(raw_in[slot(MOD_POS[n])], 16 * lap(MOD_POS[n]))
                        c = n - GATE_TILES
                        if c < 0:
                            mod_tile(MOD_POS[n], gate_c[:, n:n + 1], silu_b, gate_used)
                        else:
                            mod_tile(MOD_POS[n], mod[:, c:c + 1], silu_b, ada_used)
                        if c == -1:
                            dve.wait_ge(gate_used, GATE_TILES)
                            V.tensor_tensor(gate_c, gate_c, b_gate_c, ADD).then_inc(gate_col, 1)
                            dve.wait_ge(gate_col, 1)
                            V.tensor_tensor(gate_c, gate_c, g_post_c, MULT).then_inc(gate_col, 1)
                        if c == ADA_TILES - 1:
                            dve.wait_ge(ada_used, ADA_TILES)
                            dve.wait_ge(mods_in_sem, 16)
                            mods(dve, 0, KT, 0)

                    def low_y(n):
                        if n == KT - 1:
                            dve.wait_ge(y_hi, POOL_Y + 1)
                        else:
                            dve.wait_ge(y_hi_dve, n - POOL_Y + 1)
                        V.tensor_tensor(act_lo[:, n, :], yT[:, n, :], act_hi[:, n, :].bitcast(f32), SUB)\
                            .then_inc(y_lo_dve, 1)

                    def low_wo(v):
                        dve.wait_ge(s_done, NT * DIL_H)
                        if v > 3:
                            dve.wait_ge(pv_done, 4 * DIL_H)
                        low(WO0 + v, wo_lo[v // 4][:, v % 4], wo_hi[v // 4][:, v % 4])

                    def meanwhile(h, i):
                        z = (zb_0 if h % 2 else zb_1)[:, :]
                        if (h, i) in Z_ARG_STEPS:
                            z_argument(GLA_H + h - 1, dil_units(h - 1)[5], z, r_tmp2)
                        if (h, i) in Z_STEPS:
                            z_gate(GLA_H + h - 1, z, r_tmp2)
                        if h >= 2 and i in (3, 4):
                            head = GLA_H + h - 2
                            finish_y(head, sq_b[:, :], (zb_1 if head % 2 else zb_0)[:, :], [i - 3])
                        for n in range(len(MOD_STEPS)):
                            if MOD_STEPS[n] == (h, i):
                                modulation(n)
                        for n in (Y_STEPS_DVE.get(i, ()) if h == DIL_H else ()):
                            dve.wait_ge(unit_done, units_done(N_UNITS - 1))
                            dve.wait_ge(y_done, n + 1)
                            V.tensor_copy(act_hi[:, n, :], yT[:, n, :]).then_inc(y_hi_dve, 1)
                            low_y(n)

                    for h in range(DIL_H + 1):
                        for i in range(NT + 2):
                            if h and i < NT:
                                n = NT * (h - 1) + i
                                w = (i + 1) * P
                                dve.wait_ge(s_done, n + 1)
                                if n >= 2:
                                    last = pt_chunk(h - 1, i - 2, 1 if i >= 6 else 0) if i >= 2 else \
                                        pt_chunk(h - 2, NT + i - 2, 1)
                                    dve.wait_ge(pt_done, last + 1)
                                V.tensor_tensor_reduce(out=pr[:, i % 2, 0:w], in0=bank(2 + 2 * (i % 2), 2)[:, 0:w],
                                                       in1=cnt_t[:, S - w:S], scale=-SCORE_SCALE, scalar=-NEG,
                                                       op0=ADD, op1=MIN, accum_out=nmax[:, i % 2:i % 2 + 1])\
                                    .then_inc(s_masked, 1)
                            meanwhile(h, i)
                            if h and i < NT:
                                dve.wait_ge(exp_done, n + 1)
                                link(V.reciprocal(rden[:, i % 2:i % 2 + 1], den[:, i % 2:i % 2 + 1]))
                                V.tensor_scalar(pr[:, i % 2, 0:w], pr[:, i % 2, 0:w], rden[:, i % 2:i % 2 + 1], None,
                                                MULT).then_inc(p_ready, 1)
                            for h_, n in [slot_units(h)[c] for c in completed(STEP_MM[h], i)]:
                                z = zb_1 if h_ % 2 else zb_0
                                if n < 4:
                                    rope(h_, n)
                                else:
                                    z_copy(GLA_H + h_, dil_units(h_)[n], z)
                    low_wo(2)
                    low_wo(3)
                    low_wo(5)
                    low_wo(7)
                    finish_y(GLA_H + DIL_H - 1, sq_last[:, :], zb_1[:, :])
                    low_y(7)
                    dve.wait_ge(gate_ready, 1)
                    for t in range(NT):
                        dve.wait_ge(rstd_y, t + 1)
                        V.scalar_tensor_tensor(out=yT[:, t, :], in0=bank(o_bank(t), 2),
                                               scalar=rstd[:, t % 2:t % 2 + 1],
                                               in1=gate_t[:, :], op0=MULT, op1=MULT).then_inc(yp_free, 1)
                        dve.wait_ge(yp_free, t + 1)
                        dve.wait_ge(x_load[t % 2], 16 * (t // 2 + 1))
                        V.tensor_tensor(x_t[:, t % 2, :], x_t[:, t % 2, :], yT[:, t, :], ADD).then_inc(x_new, 1)
                        with dve.If(layer < DEPTH - 1):
                            dve.wait_ge(rstd_x, t + 1)
                            V.tensor_scalar(yT[:, t, :], x_t[:, t % 2, :], rs8[:, t:t + 1], None, MULT)\
                                .then_inc(xn_done, 1)
                            for m in h_after(t):
                                if m == 3:
                                    dve.wait_ge(xnT_done, m + 1)
                                    for k in range(KT // 2):
                                        V.tensor_scalar(act_hi[:, k, 2 * P * m:2 * P * (m + 1)], h_bank(4, k),
                                                        h_scale[:, k:k + 1], mod[:, 2 * k:2 * k + 1], MULT, ADD)\
                                            .then_inc(h_hi_dve, 1)
                                    for k in range(KT // 2):
                                        dve.wait_ge(h_hi_dve, k + 1)
                                        h_low(dve, m, 4, k, KT * m + k, h_tmp(m, k))
                                    continue
                                for k in range(0, KT, 2):
                                    dve.wait_ge(h_hi, KT * m + k + 2)
                                    for kk in (k, k + 1):
                                        h_low(dve, m, 4, kk, KT * m + kk, h_tmp(m, kk))

                @block.tensor
                def _(pe):
                    mm = nc.tensor.matmul
                    parts = PARTS

                    def unit_mm(key, m):
                        u = UNIT[key]
                        k, part = divmod(m, 3)
                        s, v = parts[part]
                        if m == 0:
                            if u >= 2:
                                wait_unit_evacuated(pe, u - 2)
                        dst = bank(u % 2)
                        if key[0] == "va":
                            if m == 0 and key[1] == 0:
                                for n in range(VA0, VA0 + 2) if key[2] else range(VA0 + 2, 0):
                                    wait_used(pe, n)
                                pe.wait_ge(low_split, 2)
                            tok = slice(key[1] * P, (key[1] + 1) * P)
                            cols = slice(key[2] * V_COLS, (key[2] + 1) * V_COLS)
                            dst = dst[:, 0:V_COLS]
                            w, a = (wv_hi, wv_lo)[v][:, k, cols], (act_hi, act_lo)[s][:, k, tok]
                            last = mm(dst, a, w, start=(m == 0), stop=(m == MM - 1))
                        elif key[0] == "vb":
                            if m == 0 and key[1] == 0:
                                for n in range(VB0, VB0 + VT):
                                    wait_used(pe, n)
                            tok = slice(key[1] * P, (key[1] + 1) * P)
                            w, a = (wv_hi, wv_lo)[v][:, k, 0:VT * P], (act_hi, act_lo)[s][:, k, tok]
                            last = mm(dst, a, w, start=(m == 0), stop=(m == MM - 1))
                        else:
                            t, half = key
                            if m == 0 and half == 0 and t >= FIRST_T:
                                wait_used(pe, position(t))
                            w = (wt_hi, wt_lo)[s][:, t % 2, k, :]
                            a = (act_hi, act_lo)[v][:, k, half * HALF:(half + 1) * HALF]
                            last = mm(dst, w, a, start=(m == 0), stop=(m == MM - 1))
                        if m == MM - 1:
                            last.then_inc(unit_done, 1)

                    def unit(key):
                        for m in range(MM):
                            unit_mm(key, m)

                    def fill(keys, budget, i):
                        for m in range(sum(budget[:i]), sum(budget[:i + 1])):
                            unit_mm(keys[m // MM], m % MM)

                    def norm(head, buf, b, step=1):
                        pe.wait_ge(sq_done, head + 1)
                        if head:
                            pe.wait_ge(ln_done, head)
                        for half in range(2):
                            last = mm(bank(b + step * half), ones[:, :], buf[:, half * HALF:(half + 1) * HALF], start=True,
                                      stop=True)
                        last.then_inc(norm_done, 1)

                    unit((T_Z[0], 1))
                    for t in range(NT):
                        unit(("va", t, 1))
                    unit(("va", 0, 0))
                    pe.wait_ge(act_seq, NT)
                    for t in range(NT):
                        last = nc.tensor.transpose(bank(2 + t // 4)[0:LOWRANK, (t % 4) * P:(t % 4 + 1) * P],
                                                   low_n[:, t, :], idn[:, :])
                    last.then_inc(lowT_done, 1)
                    unit(("va", 1, 0))
                    pe.wait_ge(lowT_evac, 1)
                    pe.wait_ge(gu_in, 16)
                    for j in range(PAIRS):
                        for half in range(2):
                            mm(bank(4 + 2 * j + half), w_gu[:, j * P:(j + 1) * P],
                               lrT[:, half * HALF:(half + 1) * HALF], start=True, stop=True).then_inc(dk_z, 1)
                    for t in range(2, NT):
                        unit(("va", t, 0))
                    for key in [(t, half) for t in (T_Z[1], T_QA[0], T_KA[0]) for half in range(2)]:
                        unit(key)

                    for j in range(PAIRS):
                        for m in range(MM // 2):
                            unit_mm(gla_fill[j][0], m)
                        if j:
                            pe.wait_ge(o_evac, NT * j)
                        else:
                            pe.wait_ge(dk_abs, 4)
                        wait_unit_evacuated(pe, UNIT[(T_KA[j], 0)])
                        wait_unit_evacuated(pe, UNIT[(T_KA[j], 1)])
                        for q in range(2):
                            for t in range(4):
                                last = nc.tensor.transpose(bank(6 + q)[:, t * P:(t + 1) * P],
                                                           k_dT[j][:, (4 * q + t) * P:(4 * q + t + 1) * P],
                                                           idn[:, :])
                            last.then_inc(kd_done, 1)
                        for m in range(MM // 2, MM):
                            unit_mm(gla_fill[j][0], m)
                        pe.wait_ge(kend_ready, 2 * (j + 1))

                        def scores_and_chunk_states(p):
                            s = NT * j + p
                            tok = slice(p * P, (p + 1) * P)
                            if s:
                                pe.wait_ge(at_masked, s)
                            for e in range(2):
                                rows_ = slice(e * DK, (e + 1) * DK)
                                last = mm(bank(2 + e)[:, 0:P], k_e[j][rows_, tok], q_e[j][rows_, tok], start=True, stop=True)
                            last.then_inc(at_done, 1)
                            if s:
                                pe.wait_ge(state_done, states(j, 2 * p))
                            for c in range(2):
                                in_chunk = slice(c * CHUNK, (c + 1) * CHUNK)
                                for e in range(2):
                                    if p == NT - 1 and c == 1:
                                        continue
                                    g = 2 * j + e
                                    last = mm(bank(4 + c)[e * DK:(e + 1) * DK, 0:DV],
                                              k_end[in_chunk, p, e * DK:(e + 1) * DK],
                                              va[in_chunk, p, g * DV:(g + 1) * DV], start=True, stop=True)
                            last.then_inc(cs_done, 1)

                        def outputs(p):
                            s = NT * j + p
                            pe.wait_ge(at_masked, s + 1)
                            pe.wait_ge(state_done, states(j, 2 * p + 1))
                            if s:
                                pe.wait_ge(o_evac, s)
                            for e in range(2):
                                g = 2 * j + e
                                rows_ = slice(e * DK, (e + 1) * DK)
                                mm(bank(6 + e)[:, 0:P], va[:, p, g * DV:(g + 1) * DV], at_sb[:, p % 2, e, :],
                                   start=True, stop=False)
                                for c in (2 * p, 2 * p + 1):
                                    if c:
                                        i0 = (c % 2) * CHUNK
                                        last = mm(bank(6 + e)[:, i0:i0 + CHUNK], state[rows_, c % 6, :],
                                                  q_e[j][rows_, c * CHUNK:(c + 1) * CHUNK], start=False,
                                                  stop=(c == 2 * p + 1))
                            last.then_inc(o_done, 1)

                        scores_and_chunk_states(0)
                        for p in range(NT):
                            if p + 1 < NT:
                                scores_and_chunk_states(p + 1)
                            fill(gla_fill[j][1:], FILL, p)
                            outputs(p)

                    def split_norm(head, b):
                        pe.wait_ge(sq_low, head + 1)
                        if head:
                            pe.wait_ge(ln_done, head)
                        for half in range(2):
                            cols = slice(half * HALF, (half + 1) * HALF)
                            mm(bank(b + half), ones_r[:, 0:1].broadcast_to([P, P]), sq_hi[:, cols], start=True, stop=False)
                            last = mm(bank(b + half), ones_r[:, 0:1].broadcast_to([P, P]), sq_lo[:, cols], start=False, stop=True)
                        last.then_inc(norm_done, 1)

                    for t in range(NT):
                        unit(("vb", t))
                        if t in NORM_STEPS:
                            pe.wait_ge(at_masked, NT * PAIRS)
                            split_norm(NORM_STEPS.index(t), 2)

                    def attend(h, i, unit_work):
                        q_t, k_t = qkT[:, 2 * (h % 2), :], qkT[:, 2 * (h % 2) + 1, :]
                        if i < NT:
                            n = NT * h + i
                            b = 2 + 2 * (i % 2)
                            if n >= 2:
                                pe.wait_ge(s_masked, n - 1)
                            if i == 4:
                                pe.wait_ge(ln_done, GLA_H + h)
                            if n == 0:
                                pe.wait_ge(silu_ready, 1)
                                pe.wait_ge(state_done, states(PAIRS, 0))
                            for half in range(-(-(i + 1) // 4)):
                                w = min((i + 1) * P - half * HALF, HALF)
                                last = mm(bank(b + half)[:, 0:w], q_t[:, i * P:(i + 1) * P],
                                          k_t[:, half * HALF:half * HALF + w], start=True, stop=True)
                            last.then_inc(s_done, 1)
                        if i == NT + 1:
                            unit_work()
                        if i >= 3 and i % 2:
                            g = (i - 3) // 2
                            pe.wait_ge(pt_evac, pt_chunk(h, 2 * g + 1, 1 if g >= 2 else 0) + 1)
                            if 4 * h + g:
                                pe.wait_ge(pv_evac, 4 * h + g)
                            for j in range(2 * g + 2):
                                c0 = P if j == 2 * g + 1 else 0
                                last = mm(bank(7)[:, c0:2 * P], vb[:, j, h * HD:(h + 1) * HD], pT[:, j, c0:2 * P],
                                          start=(j == 0), stop=(j == 2 * g + 1))
                            last.then_inc(pv_done, 1)

                        def transpose_p(part, j0, j1):
                            q = i - 1
                            c = pt_chunk(h, q, part)
                            pe.wait_ge(p_ready, NT * h + q + 1)
                            if c:
                                pe.wait_ge(pt_evac, c)
                            else:
                                pe.wait_ge(o_evac, NT * PAIRS)
                            for j in range(j0, j1):
                                last = nc.tensor.transpose(bank(6)[:, (j - j0) * P:(j - j0 + 1) * P],
                                                           pr[:, q % 2, j * P:(j + 1) * P], idn[:, :])
                            last.then_inc(pt_done, 1)
                        if 1 <= i <= NT:
                            transpose_p(0, *pt_parts(i - 1)[0])
                        if i <= NT:
                            unit_work()
                        if 5 <= i <= NT:
                            transpose_p(1, *pt_parts(i - 1)[1])

                    for h in range(DIL_H + 1):
                        if h:
                            for kind in range(2):
                                for half in range(2):
                                    wait_unit_evacuated(pe, UNIT[(T_B(h - 1, kind), half)])
                        for i in range(NT + 2):
                            def unit_work(i=i, h=h):
                                fill([dil_units(h_)[n] for h_, n in slot_units(h)], STEP_MM[h], i)
                                if h == DIL_H and i == 8:
                                    wait_unit_evacuated(pe, N_UNITS - 2)
                                    wait_unit_evacuated(pe, N_UNITS - 1)
                                    pe.wait_ge(gate_col, 2)
                                    rows_of(gate_c, 0, gate_mm)
                                if i == 0 and h == 0:
                                    pe.wait_ge(ln_done, GLA_H)
                                    pe.wait_ge(dk_exp, 4 * PAIRS)
                                    rows_of(silu_c, 2, silu_mm)
                                if i == 1 and h >= 2:
                                    pe.wait_ge(s_masked, NT * (h - 1))
                                    norm(GLA_H + h - 2, sq_b, 3, 2)
                            if h:
                                attend(h - 1, i, unit_work)
                            else:
                                unit_work()
                    pe.wait_ge(s_masked, NT * DIL_H)

                    def out_mm(t, half, k):
                        tok = slice(t * P, (t + 1) * P)
                        for part in range(3):
                            s, v = parts[part]
                            last = mm(bank(o_bank(t) + half), (act_hi, act_lo)[s][:, k, tok],
                                      (wo_hi, wo_lo)[v][half][:, :, k, :], start=(k == 0 and part == 0),
                                      stop=(k == KT - 1 and part == 2))
                        return last

                    pe.wait_ge(y_lo_pool, POOL_Y)
                    pe.wait_ge(y_lo_dve, KT - 1 - POOL_Y)
                    for half in range(2):
                        for v in range(4 * half, 4 * half + 4):
                            wait_used(pe, WO0 + v)
                        for t in range(2):
                            if t:
                                pe.wait_ge(gate_ready, 1)
                            for k in range(KT - 1):
                                out_mm(t, half, k)
                            if t == 0 and half == 0:
                                norm(GLA_H + DIL_H - 1, sq_last, 4)
                    for t in range(NT):
                        if t == 0:
                            pe.wait_ge(y_lo_dve, KT - POOL_Y)
                        if t >= 3:
                            pe.wait_ge(yp_free, t - 2 if t < 5 else t - 1)
                        for half in range(2):
                            for k in range(KT - 1 if t < 2 else 0, KT):
                                last = out_mm(t, half, k)
                        last.then_inc(yp_done, 1)
                        with pe.If(layer < DEPTH - 1):
                            if t == NT - 1:
                                pe.wait_ge(yp_free, NT - 1)
                                pe.wait_ge(h_lo, 2 * KT * 2)
                                wait_used(pe, len(STREAM))
                                first_unit()
                            for m in h_after(t):
                                pe.wait_ge(xn_done, 2 * m + 2)
                                pe.wait_ge(ln_done, GLA_H + DIL_H)
                                pe.wait_ge(pv_evac, 4 * DIL_H)
                                if m:
                                    pe.wait_ge(h_lo, 2 * KT * m)
                                else:
                                    pe.wait_ge(yp_free, 3)
                                for k in range(KT):
                                    last = h_transpose(m, 4, k)
                                last.then_inc(xnT_done, 1)
            nc.all_engine_barrier(sems_to_clear=range(sems[0].num, sems[-1].num + 1))


def kernel(**inputs):
    import concourse.bacc as bacc
    from concourse.bass_utils import run_bass_kernel_spmd as run

    def arr(name):
        return np.asarray(inputs[name])

    def cols(v):
        return v.reshape(-1, P).T

    w_ada, w_in, w_out = arr("w_ada"), arr("w_in"), arr("w_out")
    q0, k0, v0 = 0, GLA_H * DK, 2 * GLA_H * DK
    z0 = v0 + GLA_H * DV
    lr0 = z0 + GLA_H * DV
    b0 = lr0 + LOWRANK
    wb = DIL_H * HD

    def tile(w, layer, c):
        return w[layer, :, c:c + P].reshape(KT, P, P).transpose(1, 0, 2).reshape(P, KT * P)

    def ada_tiles(layer):
        return [w_ada[layer, :, c + k * P:c + (k + 1) * P].T for k in range(KT) for c in (0, D)]

    def t_columns():
        gla = [z0, z0 + P, q0, k0, q0 + P, k0 + P, z0 + 2 * P, z0 + 3 * P]
        return gla + [b0 + n * wb + h * P for h in range(DIL_H) for n in (0, 1, 3)]

    def first_tiles(layer):
        return [tile(w_in, layer, c) for c in t_columns()[:FIRST_T] + [v0 + va_column(n) * P for n in range(VT)]]

    def stream(layer):
        after = min(layer + 1, DEPTH - 1)
        kinds = {"t": [tile(w_in, layer, c) for c in t_columns()][FIRST_T:],
                 "vb": [tile(w_in, layer, b0 + 2 * wb + v * P) for v in range(VT)],
                 "ada": ada_tiles(after),
                 "gate": [w_ada[layer, :, 2 * D + n * P:2 * D + (n + 1) * P].T for n in range(GATE_TILES)],
                 "wo": [tile(w_out, layer, n * P) for n in range(KT)]}
        return [kinds[kind].pop(0) for kind in STREAM] + first_tiles(after)

    def turns(a):
        return a.reshape(2, KT, P).transpose(1, 0, 2).reshape(2 * KT, P).T

    b_ada, g_pre, b_gu, g_gla, g_dil, g_post = (arr(n) for n in ("b_ada", "g_pre", "b_gate_up", "g_gla", "g_dil",
                                                                 "g_post"))
    inv = (10000.0 ** (-np.arange(0, HD, 2, dtype=np.float32) / HD)).astype(np.float32)
    ang = inv[:, None] * np.arange(S, dtype=np.float32)[None, :]
    cos, sin = np.cos(ang).astype(np.float32), np.sin(ang).astype(np.float32)
    dist = np.arange(P)[:, None] + (S - P) - np.arange(S)[None, :]
    times = sum(((dist >= 0) & (dist <= w) & (dist % d == 0)).astype(np.int64)
                for w, d in ((128, 1), (512, 4), (2048, 16)))
    with np.errstate(divide="ignore"):
        cnt = np.where(times > 0, np.log(np.maximum(times, 1)) / SCORE_SCALE, NEG).astype(np.float32)
    j, i = np.arange(P)[:, None], np.arange(P)[None, :]
    with_next = list(range(DEPTH)) + [DEPTH - 1]
    data = {
        "x": arr("x"),
        "tiles": np.stack(ada_tiles(0) + first_tiles(0) + [t for layer in range(DEPTH) for t in stream(layer)]),
        "w_low": np.stack([w_in[n, :, lr0:b0].reshape(KT, P, LOWRANK).transpose(1, 0, 2).reshape(P, KT * LOWRANK)
                           for n in with_next]),
        "vecs": np.stack([np.concatenate([cols(b_gu[n]), cols(g_gla[n]), cols(g_dil[n]),
                                          cols(b_ada[n, 2 * D:]), cols(g_post[n])], axis=1)
                          for n in range(DEPTH)]),
        "mods_in": np.stack([np.concatenate([turns(b_ada[n, :2 * D]), cols(g_pre[n])], axis=1)
                             for n in with_next]),
        "w_gate_up": arr("w_gate_up").reshape(DEPTH * LOWRANK, GLA_H * DK),
        "c_cols": cols(arr("c")[0]),
        "rope_cos": np.concatenate([cos, cos]),
        "rope_sin": np.concatenate([sin, -sin]),
        "log_count": cnt,
        "ident": np.eye(P, dtype=np.float32),
        "causal": ((j <= i) & (j // CHUNK == i // CHUNK)).astype(np.int32),
    }
    data = {k: np.ascontiguousarray(v) for k, v in data.items()}
    nc = bacc.Bacc("TRN2", target_bir_lowering=False, num_devices=1)
    aps = {k: nc.dram_tensor(f"{k}_dram", v.shape, mybir.dt.from_np(v.dtype), kind="ExternalInput").ap()
           for k, v in data.items()}
    out = nc.dram_tensor("out_dram", (1, S, D), mybir.dt.float32, kind="ExternalOutput").ap()
    hybrid_trunk(nc, out=out, **aps)
    r = run(nc, [{f"{k}_dram": v for k, v in data.items()}], core_ids=[0])
    return r.results[0]["out_dram"]
```
